# Optimizing a Trainium2 kernel written in Bass

```python
import jax, jax.numpy as jnp
from jax import lax
import numpy as np

D_MODEL = 1024
BATCH = 1
SEQ = 256
DEPTH = 1

RET_WIDTH = D_MODEL // 2
RET_HEADS = 4
RET_HEAD_DIM = RET_WIDTH // RET_HEADS
CONV_WIDTH = D_MODEL - RET_WIDTH
CONV_GROUPS = 8
CONV_K = 3
MIX_WIDTH = RET_WIDTH + CONV_WIDTH
IN_COLS = 4 * RET_WIDTH + 3 * CONV_WIDTH
CHUNK = 128
ROPE_BASE = 10000.0
N_GROUPS = 8
EXPERTS_PER_GROUP = 8
N_EXPERTS = N_GROUPS * EXPERTS_PER_GROUP
TOP_K = 2
EXPERT_FF = D_MODEL // 2
MOE_BLOCK = 128
EPS = 1e-6


def rmsnorm(x, w):
    xf = x.astype(jnp.float32)
    y = xf * lax.rsqrt(jnp.mean(xf * xf, axis=-1, keepdims=True) + EPS)
    return (y * w.astype(jnp.float32)).astype(x.dtype)

def rotary(x, pos):
    half = x.shape[-1] // 2
    inv = ROPE_BASE ** (-jnp.arange(half, dtype=jnp.float32) / half)
    ang = pos.astype(jnp.float32)[:, None] * inv[None, :]
    cos = jnp.cos(ang)[None, :, None, :]
    sin = jnp.sin(ang)[None, :, None, :]
    xf = x.astype(jnp.float32)
    x1, x2 = xf[..., :half], xf[..., half:]
    return jnp.concatenate([x1 * cos - x2 * sin, x2 * cos + x1 * sin], axis=-1)

def retention_chunkwise(q, k, v):
    b, s, h, d = q.shape
    nc = s // CHUNK
    log_g = jnp.log1p(-(2.0 ** (-5.0 - jnp.arange(h, dtype=jnp.float32))))
    idx = jnp.arange(CHUNK, dtype=jnp.float32)
    rel = idx[:, None] - idx[None, :]
    causal = rel >= 0
    intra_decay = jnp.where(causal[None], jnp.exp(log_g[:, None, None] * jnp.where(causal, rel, 0.0)[None]), 0.0)
    k_decay = jnp.exp(log_g[:, None] * (CHUNK - 1 - idx)[None, :])
    q_decay = jnp.exp(log_g[:, None] * (idx + 1)[None, :])
    chunk_decay = jnp.exp(log_g * CHUNK)

    qc = q.reshape(b, nc, CHUNK, h, d)
    kc = k.reshape(b, nc, CHUNK, h, d)
    vc = v.reshape(b, nc, CHUNK, h, d)

    scores = jnp.einsum('bnihd,bnjhd->bnhij', qc, kc) * intra_decay[None, None]
    o_intra = jnp.einsum('bnhij,bnjhd->bnihd', scores, vc)

    kv = jnp.einsum('bnjhd,hj,bnjhe->bnhde', kc, k_decay, vc)

    def step(state, kv_n):
        return chunk_decay[None, :, None, None] * state + kv_n, state

    _, prev = lax.scan(step, jnp.zeros((b, h, d, d), jnp.float32), jnp.moveaxis(kv, 1, 0))
    prev = jnp.moveaxis(prev, 0, 1)
    o_inter = jnp.einsum('bnihd,bnhde->bnihe', qc, prev) * q_decay.T[None, None, :, :, None]
    return (o_intra + o_inter).reshape(b, s, h, d)

def head_groupnorm(o, w):
    b, s, h, d = o.shape
    mu = jnp.mean(o, axis=-1, keepdims=True)
    var = jnp.mean(jnp.square(o - mu), axis=-1, keepdims=True)
    y = (o - mu) * lax.rsqrt(var + EPS)
    return y.reshape(b, s, h * d) * w.astype(jnp.float32)

def causal_depthwise_conv(u, w):
    return lax.conv_general_dilated(
        u, w[:, None, :], window_strides=(1,), padding=[(CONV_K - 1, 0)],
        dimension_numbers=('NWC', 'WIO', 'NWC'), feature_group_count=u.shape[-1])

def mixer(h, w_in, ret_gn_w, conv_w, w_o):
    b, s, _ = h.shape
    proj = h @ w_in
    R, C = RET_WIDTH, CONV_WIDTH
    q, k, v, g, gb, gc, u = jnp.split(proj, [R, 2 * R, 3 * R, 4 * R, 4 * R + C, 4 * R + 2 * C], axis=-1)
    pos = jnp.arange(s)
    q = rotary(q.reshape(b, s, RET_HEADS, RET_HEAD_DIM), pos) * (RET_HEAD_DIM ** -0.5)
    k = rotary(k.reshape(b, s, RET_HEADS, RET_HEAD_DIM), pos)
    v = v.reshape(b, s, RET_HEADS, RET_HEAD_DIM).astype(jnp.float32)
    ret = retention_chunkwise(q, k, v)
    ret = (jax.nn.silu(g.astype(jnp.float32)) * head_groupnorm(ret, ret_gn_w)).astype(h.dtype)
    conv = gb * causal_depthwise_conv(gc * u, conv_w)
    return jnp.concatenate([ret, conv], axis=-1) @ w_o

def expert_dispatch(t, expert, gate, w_gate, w_up, w_down):
    n, d = t.shape
    e_total = w_gate.shape[0]
    n_slots = n * TOP_K
    flat_e = expert.reshape(-1)
    flat_tok = jnp.repeat(jnp.arange(n, dtype=jnp.int32), TOP_K)
    flat_w = gate.reshape(-1)
    order = jnp.argsort(flat_e)
    se, stok, sw = flat_e[order], flat_tok[order], flat_w[order]
    counts = jnp.bincount(flat_e, length=e_total)
    starts = jnp.cumsum(counts) - counts
    padded = ((counts + MOE_BLOCK - 1) // MOE_BLOCK) * MOE_BLOCK
    pad_ends = jnp.cumsum(padded)
    pad_starts = pad_ends - padded
    dest = pad_starts[se] + (jnp.arange(n_slots) - starts[se])
    n_blocks = -(-n_slots // MOE_BLOCK) + e_total
    cap = n_blocks * MOE_BLOCK
    buf_tok = jnp.full((cap,), n, jnp.int32).at[dest].set(stok)
    buf_w = jnp.zeros((cap,), t.dtype).at[dest].set(sw.astype(t.dtype))
    block_e = jnp.minimum(jnp.searchsorted(pad_ends, jnp.arange(n_blocks) * MOE_BLOCK, side='right'), e_total - 1)
    t_pad = jnp.concatenate([t, jnp.zeros((1, d), t.dtype)], axis=0)

    def run_block(args):
        tok, e = args
        xb = t_pad[tok]
        hb = jax.nn.silu(xb @ w_gate[e]) * (xb @ w_up[e])
        return hb @ w_down[e]

    yb = lax.map(run_block, (buf_tok.reshape(n_blocks, MOE_BLOCK), block_e))
    y = jax.ops.segment_sum(yb.reshape(cap, d) * buf_w[:, None], buf_tok, num_segments=n + 1)
    return y[:n]

def hier_moe(h, rg_w, rg_b, re_w, re_b, w_gate, w_up, w_down):
    b, s, d = h.shape
    t = h.reshape(b * s, d)
    g_prob = jax.nn.softmax((t @ rg_w).astype(jnp.float32) + rg_b.astype(jnp.float32), axis=-1)
    p_group, g_sel = lax.top_k(g_prob, 1)
    p_group, g_sel = p_group[:, 0], g_sel[:, 0]
    e_logits_all = jnp.einsum('nd,gde->nge', t, re_w).astype(jnp.float32) + re_b.astype(jnp.float32)[None]
    e_logits = jnp.take_along_axis(e_logits_all, g_sel[:, None, None], axis=1)[:, 0]
    e_prob = jax.nn.softmax(e_logits, axis=-1)
    top_p, top_i = lax.top_k(e_prob, TOP_K)
    top_p = top_p / jnp.sum(top_p, axis=-1, keepdims=True)
    gate = p_group[:, None] * top_p
    expert = g_sel[:, None] * EXPERTS_PER_GROUP + top_i
    return expert_dispatch(t, expert, gate, w_gate, w_up, w_down).reshape(b, s, d)

def first_inputs(seed: int = 0) -> dict:
    key = jax.random.key(seed)
    ks = jax.random.split(key, 16)
    f32 = jnp.float32
    nrm = lambda k, shape, scale: jax.random.normal(k, shape, f32) * scale
    return {
        "x": nrm(ks[0], (BATCH, SEQ, D_MODEL), 1.0),
        "norm1_w": 1.0 + nrm(ks[1], (DEPTH, D_MODEL), 0.02),
        "w_in": nrm(ks[2], (DEPTH, D_MODEL, IN_COLS), D_MODEL ** -0.5),
        "ret_gn_w": 1.0 + nrm(ks[3], (DEPTH, RET_WIDTH), 0.02),
        "conv_w": nrm(ks[4], (DEPTH, CONV_K, CONV_WIDTH), CONV_K ** -0.5),
        "w_o": nrm(ks[5], (DEPTH, MIX_WIDTH, D_MODEL), MIX_WIDTH ** -0.5),
        "norm2_w": 1.0 + nrm(ks[6], (DEPTH, D_MODEL), 0.02),
        "router_g_w": nrm(ks[7], (DEPTH, D_MODEL, N_GROUPS), D_MODEL ** -0.5),
        "router_g_b": nrm(ks[8], (DEPTH, N_GROUPS), 0.01),
        "router_e_w": nrm(ks[9], (DEPTH, N_GROUPS, D_MODEL, EXPERTS_PER_GROUP), D_MODEL ** -0.5),
        "router_e_b": nrm(ks[10], (DEPTH, N_GROUPS, EXPERTS_PER_GROUP), 0.01),
        "w_gate": nrm(ks[11], (DEPTH, N_EXPERTS, D_MODEL, EXPERT_FF), D_MODEL ** -0.5),
        "w_up": nrm(ks[12], (DEPTH, N_EXPERTS, D_MODEL, EXPERT_FF), D_MODEL ** -0.5),
        "w_down": nrm(ks[13], (DEPTH, N_EXPERTS, EXPERT_FF, D_MODEL), EXPERT_FF ** -0.5),
        "final_norm_w": 1.0 + nrm(ks[14], (D_MODEL,), 0.02),
    }

def first_block(x, norm1_w, w_in, ret_gn_w, conv_w, w_o, norm2_w, router_g_w, router_g_b,
              router_e_w, router_e_b, w_gate, w_up, w_down, final_norm_w):
    for l in range(DEPTH):
        h = rmsnorm(x, norm1_w[l])
        x = x + mixer(h, w_in[l], ret_gn_w[l], conv_w[l], w_o[l])
        h = rmsnorm(x, norm2_w[l])
        x = x + hier_moe(h, router_g_w[l], router_g_b[l], router_e_w[l], router_e_b[l],
                         w_gate[l], w_up[l], w_down[l])
    return rmsnorm(x, final_norm_w)


GRID_W = 64
CTX_LEN = 256
N_MIXERS = 2
N_A_LAYERS = (DEPTH + N_MIXERS - 1) // N_MIXERS
N_B_LAYERS = DEPTH // N_MIXERS
HG_EXPAND = 128
HG_HEADS = D_MODEL // HG_EXPAND
HG_DK = HG_EXPAND
HG_DV = D_MODEL // HG_HEADS
HG_F = HG_HEADS * HG_DK
CHUNK_2 = 64
D_RNN = D_MODEL
LRU_BLOCKS = 4
LRU_BW = D_RNN // LRU_BLOCKS
LRU_CONV_W = 4
LRU_C = 8.0
D_FF = 2816
FFN_CONV_W = 3


def rmsnorm_2(x, g):
    xf = x.astype(jnp.float32)
    y = xf * lax.rsqrt(jnp.mean(xf * xf, axis=-1, keepdims=True) + EPS)
    return (y * g).astype(x.dtype)

def modulate(h, shift, scale):
    return h * (1.0 + scale) + shift

def dwconv(x, w, b):
    K = w.shape[0]
    right = (K - 1) // 2
    left = K - 1 - right
    T = x.shape[1]
    xp = jnp.pad(x, ((0, 0), (left, right), (0, 0)))
    return sum(w[k] * xp[:, k:k + T] for k in range(K)) + b

def _flip(t, d, axis):
    return t if d == 0 else jnp.flip(t, axis=axis)

def hgrn2_chunk_scan(q, k, v, logf, s0):
    Bn, H, T, _ = q.shape
    n = T // CHUNK_2
    rs = lambda t: t.reshape(Bn, H, n, CHUNK_2, t.shape[-1])
    q, k, v, logf = rs(q), rs(k), rs(v), rs(logf)
    b = jnp.cumsum(logf, axis=3)
    b_ref = b[:, :, :, CHUNK_2 // 2:CHUNK_2 // 2 + 1]
    b_last = b[:, :, :, -1:]
    qe = q * jnp.exp(b - b_ref)
    ke = k * jnp.exp(b_ref - b)
    scores = jnp.einsum('bhnik,bhnjk->bhnij', qe, ke)
    mask = jnp.tril(jnp.ones((CHUNK_2, CHUNK_2), dtype=bool))
    scores = jnp.where(mask, scores, 0.0)
    o_intra = jnp.einsum('bhnij,bhnjv->bhniv', scores, v)
    kv = jnp.einsum('bhnjk,bhnjv->bhnkv', k * jnp.exp(b_last - b), v)
    decay = jnp.exp(b_last[:, :, :, 0])

    def step(s, inp):
        dcy, u = inp
        return dcy[..., None] * s + u, s

    s_final, s_start = lax.scan(step, s0, (jnp.moveaxis(decay, 2, 0), jnp.moveaxis(kv, 2, 0)))
    s_start = jnp.moveaxis(s_start, 0, 2)
    o_inter = jnp.einsum('bhnik,bhnkv->bhniv', q * jnp.exp(b), s_start)
    o = (o_intra + o_inter).reshape(Bn, H, T, v.shape[-1])
    return o, s_final

def hgrn2_mixer(h_ctx, h_lat, w_in, lb, g_gain, w_out, need_ctx):
    def prep(h):
        Bn, T, _ = h.shape
        heads = lambda t: t.reshape(Bn, T, HG_HEADS, -1).transpose(0, 2, 1, 3)
        q, zf_fwd, zf_bwd, v, g = jnp.split(h @ w_in, 5, axis=-1)
        q = heads(jax.nn.silu(q))
        v = heads(v)
        logf, k = [], []
        for d, zf in enumerate((zf_fwd, zf_bwd)):
            f = lb[d] + (1.0 - lb[d]) * jax.nn.sigmoid(zf.astype(jnp.float32))
            logf.append(heads(jnp.log(f)))
            k.append(heads(1.0 - f))
        return q, k, v, logf, g

    qc, kc, vc, lfc, gc = prep(h_ctx)
    ql, kl, vl, lfl, gl = prep(h_lat)
    s0 = jnp.zeros((h_lat.shape[0], HG_HEADS, HG_DK, HG_DV), jnp.float32)
    o_c, o_l = 0.0, 0.0
    for d in range(2):
        oc_d, s_ctx = hgrn2_chunk_scan(_flip(qc, d, 2), _flip(kc[d], d, 2), _flip(vc, d, 2),
                                       _flip(lfc[d], d, 2), s0)
        ol_d, _ = hgrn2_chunk_scan(_flip(ql, d, 2), _flip(kl[d], d, 2), _flip(vl, d, 2),
                                   _flip(lfl[d], d, 2), s_ctx)
        o_c = o_c + _flip(oc_d, d, 2)
        o_l = o_l + _flip(ol_d, d, 2)

    def readout(o, g):
        Bn, H, T, DV = o.shape
        o = rmsnorm_2(o, g_gain).transpose(0, 2, 1, 3).reshape(Bn, T, H * DV)
        return (o * jax.nn.silu(g)) @ w_out

    y_c = readout(o_c, gc) if need_ctx else None
    return y_c, readout(o_l, gl)

def lru_scan(log_a, u, h0):
    a = jnp.exp(log_a)
    u = u.at[:, 0].add(a[:, 0] * h0)

    def combine(l, r):
        al, ul = l
        ar, ur = r
        return al * ar, ar * ul + ur

    _, h = lax.associative_scan(combine, (a, u), axis=1)
    return h

def rglru_mixer(h_ctx, h_lat, w_in, conv_w, conv_b, wa, ba, wx, bx, lam, w_out, need_ctx):
    Bn, T, _ = h_lat.shape
    rows = T // GRID_W
    to_cm = lambda t: t.reshape(Bn, rows, GRID_W, -1).transpose(0, 2, 1, 3).reshape(Bn, T, -1)
    from_cm = lambda t: t.reshape(Bn, GRID_W, rows, -1).transpose(0, 2, 1, 3).reshape(Bn, T, -1)

    def branch(h):
        gate, xr = jnp.split(h @ w_in, 2, axis=-1)
        return gate, dwconv(xr, conv_w, conv_b)

    def gates(xr, d):
        xb = xr.reshape(*xr.shape[:-1], LRU_BLOCKS, LRU_BW)
        r = jax.nn.sigmoid(jnp.einsum('btnk,nkj->btnj', xb, wa[d]).reshape(xr.shape) + ba[d])
        i = jax.nn.sigmoid(jnp.einsum('btnk,nkj->btnj', xb, wx[d]).reshape(xr.shape) + bx[d])
        log_a = -LRU_C * r.astype(jnp.float32) * jax.nn.softplus(-lam[d].astype(jnp.float32))
        mult = jnp.sqrt(-jnp.expm1(2.0 * log_a))
        return log_a, mult * (i * xr)

    gate_c, xc = branch(h_ctx)
    gate_l, xl = branch(to_cm(h_lat))
    h0 = jnp.zeros((Bn, D_RNN), jnp.float32)
    y_c, y_l = 0.0, 0.0
    for d in range(2):
        la_c, u_c = gates(_flip(xc, d, 1), d)
        hc = lru_scan(la_c, u_c, h0)
        la_l, u_l = gates(_flip(xl, d, 1), d)
        hl = lru_scan(la_l, u_l, hc[:, -1])
        y_c = y_c + _flip(hc, d, 1)
        y_l = y_l + _flip(hl, d, 1)
    out_l = from_cm(y_l * jax.nn.gelu(gate_l)) @ w_out
    out_c = (y_c * jax.nn.gelu(gate_c)) @ w_out if need_ctx else None
    return out_c, out_l

def conv_ffn(h, w_up, conv_w, conv_b, w_down):
    u = dwconv(h @ w_up, conv_w, conv_b)
    gate, val = jnp.split(u, 2, axis=-1)
    return (jax.nn.silu(gate) * val) @ w_down

def second_inputs(seed: int = 0) -> dict:
    key = jax.random.key(seed)
    ks = iter(jax.random.split(key, 32))
    nrm = lambda shape, s: jax.random.normal(next(ks), shape, jnp.float32) * s
    D = D_MODEL
    a0 = jax.random.uniform(next(ks), (N_B_LAYERS, 2, D_RNN), jnp.float32, 0.9, 0.999)
    sig = a0 ** (1.0 / LRU_C)
    lam = jnp.log(sig) - jnp.log1p(-sig)
    return {
        "x": nrm((BATCH, SEQ, D), 1.0),
        "c": nrm((BATCH, D), 1.0),
        "ctx": nrm((BATCH, CTX_LEN, D), 1.0),
        "c_ctx": nrm((D,), 1.0),
        "w_ada": nrm((DEPTH, D, 6 * D), D ** -0.5),
        "b_ada": nrm((DEPTH, 6 * D), 0.02),
        "norm_g": 1.0 + nrm((DEPTH, 2, D), 0.02),
        "hg_w_in": nrm((N_A_LAYERS, D, 5 * D), D ** -0.5),
        "hg_lb_logits": nrm((N_A_LAYERS + 1, 2, HG_F), 0.1),
        "hg_gnorm": 1.0 + nrm((N_A_LAYERS, HG_DV), 0.02),
        "hg_w_out": nrm((N_A_LAYERS, D, D), D ** -0.5),
        "lru_w_in": nrm((N_B_LAYERS, D, 2 * D_RNN), D ** -0.5),
        "lru_conv_w": nrm((N_B_LAYERS, LRU_CONV_W, D_RNN), LRU_CONV_W ** -0.5),
        "lru_conv_b": nrm((N_B_LAYERS, D_RNN), 0.02),
        "lru_wa": nrm((N_B_LAYERS, 2, LRU_BLOCKS, LRU_BW, LRU_BW), LRU_BW ** -0.5),
        "lru_ba": nrm((N_B_LAYERS, 2, D_RNN), 0.02),
        "lru_wx": nrm((N_B_LAYERS, 2, LRU_BLOCKS, LRU_BW, LRU_BW), LRU_BW ** -0.5),
        "lru_bx": nrm((N_B_LAYERS, 2, D_RNN), 0.02),
        "lru_lambda": lam,
        "lru_w_out": nrm((N_B_LAYERS, D_RNN, D), D_RNN ** -0.5),
        "ffn_w_up": nrm((DEPTH, D, 2 * D_FF), D ** -0.5),
        "ffn_conv_w": nrm((DEPTH, FFN_CONV_W, 2 * D_FF), FFN_CONV_W ** -0.5),
        "ffn_conv_b": nrm((DEPTH, 2 * D_FF), 0.02),
        "ffn_w_down": nrm((DEPTH, D_FF, D), D_FF ** -0.5),
        "final_g": 1.0 + nrm((D,), 0.02),
    }

def second_block(x, c, ctx, c_ctx, w_ada, b_ada, norm_g, hg_w_in, hg_lb_logits, hg_gnorm, hg_w_out,
              lru_w_in, lru_conv_w, lru_conv_b, lru_wa, lru_ba, lru_wx, lru_bx, lru_lambda, lru_w_out,
              ffn_w_up, ffn_conv_w, ffn_conv_b, ffn_w_down, final_g):
    lower_bounds = jnp.cumsum(jax.nn.softmax(hg_lb_logits.astype(jnp.float32), axis=0), axis=0)
    lat, cx = x, ctx
    sc_lat, sc_ctx = jax.nn.silu(c), jax.nn.silu(c_ctx)
    for l in range(DEPTH):
        last = l == DEPTH - 1
        m_l = (sc_lat @ w_ada[l] + b_ada[l])[:, None, :]
        m_c = sc_ctx @ w_ada[l] + b_ada[l]
        sh1, sc1, g1, sh2, sc2, g2 = jnp.split(m_l, 6, axis=-1)
        csh1, csc1, cg1, csh2, csc2, cg2 = jnp.split(m_c, 6, axis=-1)
        hl = modulate(rmsnorm_2(lat, norm_g[l, 0]), sh1, sc1)
        hc = modulate(rmsnorm_2(cx, norm_g[l, 0]), csh1, csc1)
        j = l // N_MIXERS
        if l % N_MIXERS == 0:
            yc, yl = hgrn2_mixer(hc, hl, hg_w_in[j], lower_bounds[j], hg_gnorm[j], hg_w_out[j],
                                 not last)
        else:
            yc, yl = rglru_mixer(hc, hl, lru_w_in[j], lru_conv_w[j], lru_conv_b[j], lru_wa[j],
                                 lru_ba[j], lru_wx[j], lru_bx[j], lru_lambda[j], lru_w_out[j],
                                 not last)
        lat = lat + g1 * yl
        hl = modulate(rmsnorm_2(lat, norm_g[l, 1]), sh2, sc2)
        lat = lat + g2 * conv_ffn(hl, ffn_w_up[l], ffn_conv_w[l], ffn_conv_b[l], ffn_w_down[l])
        if not last:
            cx = cx + cg1 * yc
            hc = modulate(rmsnorm_2(cx, norm_g[l, 1]), csh2, csc2)
            cx = cx + cg2 * conv_ffn(hc, ffn_w_up[l], ffn_conv_w[l], ffn_conv_b[l], ffn_w_down[l])
    return rmsnorm_2(lat, final_g)


def setup_inputs(seed=0):
    out = dict(first_inputs(seed))
    for name, value in second_inputs(seed + 1).items():
        if name != "x":
            out[name + "_2"] = value
    return out


def reference(
    x, norm1_w, w_in, ret_gn_w, conv_w, w_o, norm2_w, router_g_w, router_g_b, router_e_w,
    router_e_b, w_gate, w_up, w_down, final_norm_w, c_2, ctx_2, c_ctx_2, w_ada_2, b_ada_2,
    norm_g_2, hg_w_in_2, hg_lb_logits_2, hg_gnorm_2, hg_w_out_2, lru_w_in_2, lru_conv_w_2,
    lru_conv_b_2, lru_wa_2, lru_ba_2, lru_wx_2, lru_bx_2, lru_lambda_2, lru_w_out_2, ffn_w_up_2,
    ffn_conv_w_2, ffn_conv_b_2, ffn_w_down_2, final_g_2,
):
    x = first_block(
        x, norm1_w, w_in, ret_gn_w, conv_w, w_o, norm2_w, router_g_w, router_g_b, router_e_w,
        router_e_b, w_gate, w_up, w_down, final_norm_w,
    )
    return second_block(
        x, c_2, ctx_2, c_ctx_2, w_ada_2, b_ada_2, norm_g_2, hg_w_in_2, hg_lb_logits_2,
        hg_gnorm_2, hg_w_out_2, lru_w_in_2, lru_conv_w_2, lru_conv_b_2, lru_wa_2, lru_ba_2,
        lru_wx_2, lru_bx_2, lru_lambda_2, lru_w_out_2, ffn_w_up_2, ffn_conv_w_2, ffn_conv_b_2,
        ffn_w_down_2, final_g_2,
    )


_drawn_inputs = setup_inputs


def setup_inputs(seed=0):
    import zlib

    import numpy as np

    out = dict(_drawn_inputs(seed))
    spreads = {}
    factors = {'ret_gn_w': 5.882,
     'norm2_w': 3.748,
     'router_g_b': 4.569,
     'router_e_b': 8.0,
     'final_norm_w': 2.677,
     'ctx_2': 3.511,
     'norm_g_2': 3.685,
     'hg_lb_logits_2': 8.0,
     'hg_gnorm_2': 6.543,
     'ffn_conv_b_2': 17.142,
     'final_g_2': 8.265}
    for name, (base, spread) in spreads.items():
        noise = np.random.default_rng([zlib.crc32(name.encode()), seed]).standard_normal(out[name].shape)
        drawn = base * np.exp(spread * noise) if base else spread * noise
        out[name] = __import__('jax').numpy.asarray(drawn.astype(out[name].dtype))
    for name, factor in factors.items():
        out[name] = (out[name] * factor).astype(out[name].dtype)
    return out
```

```python
import numpy as np
import concourse.bass as bass
from concourse import mybir
from contextlib import ExitStack

P = 128
TOKENS = 256
TT = TOKENS // P
D = 1024
KD = D // P
EPS = 1e-6
HEADS1 = 4
EXPERTS = 64
FF = 512
KF = FF // P
SLOTS = TOKENS * 2
WIN = 64
COLS = SLOTS + WIN
ROUNDS = TOKENS // WIN
HEADS2 = 8
CHUNK2 = 64
NCH = TOKENS // CHUNK2
GH = 4
NG = HEADS2 // GH
DFF = 2816
NB = DFF // P
RING = 6
SLOT = 4096

VEC = {}
_at = 0
for _name, _n in (("norm1", 8), ("ret_gn", 4), ("conv", 12), ("norm2", 8), ("final1", 8), ("norm_g", 16),
                  ("final2", 8), ("lb", 32), ("gnorm", 1), ("b_ada", 48), ("ffn_w", 3 * 2 * NB),
                  ("ffn_b", 2 * NB), ("c", 8), ("c_ctx", 8)):
    VEC[_name] = _at
    _at += _n
NVEC = _at

MOE_RANGES = [(0, 32), (32, 64)]


def tile_order():
    order = [("w_in", c) for c in range(7)] + [("w_o", c) for c in range(2)]
    for r, (e0, e1) in enumerate(MOE_RANGES):
        for e in range(e0, e1):
            order += [("gate", e), ("up", e), ("down", e)]
        if r == 0:
            order += [("ada", c) for c in range(12)]
            order += [("ctx", c) for c in range(6)]
    order += [("lat", c) for c in range(10)] + [("hg_out", c) for c in range(2)]
    order += [("ffn_up", c) for c in range(12)] + [("ffn_down", c) for c in range(6)]
    return order


def program(nc, a, out):
    f32, i32, u32 = mybir.dt.float32, mybir.dt.int32, mybir.dt.uint32
    ALU, ACT, AX = mybir.AluOpType, mybir.ActivationFunctionType, mybir.AxisListType
    X = AX.X
    ctx = ExitStack()
    with ctx:
        def sb(name, shape, dt=f32):
            return ctx.enter_context(nc.sbuf_tensor(name, shape, dt))

        sems = {}

        def sem(name):
            if name not in sems:
                sems[name] = ctx.enter_context(nc.semaphore(name))
            return sems[name]

        ring = sb("ring", [P, RING, SLOT])
        consts = sb("consts", [P, 3, P])
        ident, ones, before = consts[:, 0, :], consts[:, 1, :], consts[:, 2, :]
        vecs = sb("vecs", [P, NVEC])
        hmask = sb("hmask", [P, 2, CHUNK2], i32)
        mod = sb("mod", [P, 48, 2])
        scales = sb("scales", [P, 3, KD])
        lbs = sb("lbs", [P, 2, 2, HEADS2])
        csil = sb("csil", [P, KD, 2])
        small = sb("small", [P, 96])
        starts = sb("starts", [1, ROUNDS, EXPERTS], i32)
        many = sb("many", [1, 1], i32)
        x1 = sb("x1", [P, TT, D])
        sgT = sb("sgT", [P, SLOTS // P, TOKENS])
        state = sb("state", [P, HEADS2, 2, P])
        arena = sb("arena", [P, 20480])

        used = {}

        def at(offset, *shape, dt=None):
            n = int(np.prod(shape))
            assert offset + n <= 20480, (offset, shape)
            v = arena[:, offset:offset + n]
            if len(shape) == 2:
                v = v.rearrange("p (a b) -> p a b", b=shape[1])
            if len(shape) == 3:
                v = v.rearrange("p (a b c) -> p a b c", b=shape[1], c=shape[2])
            return v

        xn = at(0, TT, D)
        hT = at(2048, KD, TOKENS)
        qk_rot = at(4096, 2, TT, 512)
        qkT = at(6144, 2, HEADS1, TOKENS)
        mixT = at(8192, KD, TOKENS)
        v_tok = at(10240, TT, 512)
        g_tok = at(11264, TT, 512)
        probs = at(12288, HEADS1, 384)
        gb_s = at(13824, 4, TOKENS)
        gc_s = at(14848, 4, TOKENS)
        gcu = at(15872, 4, TOKENS + 2)
        decay = at(16904, HEADS1, TOKENS)
        rope = at(17928, 2, TT, P)
        rot_a = at(18440, TT * 0 + 1, 512)[:, 0, :]
        rot_b = at(18952, 1, 512)[:, 0, :]
        ret = at(4096, TT, 512)
        conv_a = at(0, 4, TOKENS)
        stats = at(1024, 8, 6)
        mv = at(1100, 8, 2)
        h2T = at(2048, KD, TOKENS)
        router_w = at(4096, KD, 72)
        router_b = at(4672, 1, 72)[:, 0, :]
        iota = at(4744, 1, SLOTS)[:, 0, :]
        logits = at(5256, TT, 72)
        rt = at(5400, TT, 160)
        onehot = at(5720, 2, TT, EXPERTS)
        assigned = at(5976, TT, EXPERTS)
        place = at(6104, TT, EXPERTS)
        count = at(6232, 3, EXPERTS)
        sel = at(6424, TT, SLOTS)
        gated = at(7448, TT, SLOTS)
        YT = at(8600, KD, COLS)
        XgT = at(13208, KD, COLS)
        win = at(17816, 2, KD, WIN)
        hidden = at(18840, 2, KF, WIN)
        silu_g = at(19352, 2, KF, WIN)
        c_raw = at(0, TT, D)
        hcT = at(2048, KD, TOKENS)
        c_f = at(4096, GH, TOKENS)
        c_p = at(5120, 2, GH, TOKENS)
        c_v = at(0, TT, 512)
        c_kT = at(1024, 2, TT, P)
        zeros = at(7168, 1, TOKENS)[:, 0, :]
        y_tok = at(13208, SLOTS // P, D)
        lat = at(0, KD, TOKENS)
        hl = at(2048, KD, TOKENS)
        sq = at(4096, KD, TOKENS)
        attn = at(4096, HEADS2, TOKENS)
        q_s = at(6144, GH, TOKENS)
        v_s = at(7168, TT, 512)
        g_s = at(8192, GH, TOKENS)
        prod = at(9216, 2, 4, GH * TOKENS)
        lf = at(17408, 1, GH * TOKENS)[:, 0, :]
        kk = at(18432, 1, GH * TOKENS)[:, 0, :]
        dd = at(19456, 1, GH * TOKENS)[:, 0, :]
        b_s = x1[:, 0, :]
        smask = x1[:, 1, :]
        stt = sgT[:, :, :].rearrange("p a b -> p (a b)")
        chunk_state = stt.rearrange("p (d c v) -> p d c v", d=2, c=4)
        kdT = sb("kdT", [P, 2, TT, P])
        masked = sb("masked", [P, 2, TT, P])
        o_sq = sb("o_sq", [P, TOKENS])
        o_n = sb("o_n", [P, TOKENS])
        dec = sb("dec", [P, 2, GH * NCH])
        up_s = at(4096, 2, 2, TOKENS)
        sg_s = at(5120, 2, TOKENS)
        act = at(8192, NB, TOKENS)
        o_tok = at(14000, TT, D)
        ps = ctx.enter_context(nc.psum_tensor("ps", [P, 8, 512], f32))

        def vec(name, i=0, n=1):
            return vecs[:, VEC[name] + i:VEC[name] + i + n]

        def col(i, n=1):
            return small[:, i:i + n]

        def kv_bank(d, c):
            i = {(0, 0): 0, (0, 2): 1, (1, 2): 2, (0, 1): 0, (1, 3): 1, (1, 1): 2}[d, c]
            return ps[:, 6 + c % 2, i * P:(i + 1) * P]

        order = tile_order()
        number = {t: n for n, t in enumerate(order)}

        def source(kind, i):
            def cols(w, c, rows=KD, width=512):
                return w[:, c:c + width].rearrange("(k p) n -> p k n", p=P), (rows, width)
            if kind == "w_in":
                return cols(a["w_in"], 512 * i)
            if kind == "w_o":
                return a["w_o"][512 * i:512 * i + 512, :].rearrange("(k p) n -> p k n", p=P), (4, 1024)
            if kind in ("gate", "up"):
                return a["w_" + kind][i].rearrange("(p k) n -> p k n", k=KD), (KD, 512)
            if kind == "down":
                return a["w_down"][i].rearrange("(k p) n -> p k n", p=P), (KF, 1024)
            if kind == "ada":
                return cols(a["w_ada"], 512 * i)
            if kind == "ctx":
                return cols(a["hg_in"], (1024, 2048, 3072)[i % 3] + 512 * (i // 3))
            if kind == "lat":
                return cols(a["hg_in"], (1024, 2048, 3072, 0, 4096)[i % 5] + 512 * (i // 5))
            if kind == "hg_out":
                return cols(a["hg_out"], 512 * i)
            if kind == "ffn_up":
                b, part = i // 2, i % 2
                return cols(a["ffn_up"], DFF * part + 512 * b, KD, min(512, DFF - 512 * b))
            half, part = i // 3, i % 3
            k0, kn = (0, 8, 16)[part], (8, 8, 6)[part]
            return (a["ffn_down"][P * k0:P * (k0 + kn), 512 * half:512 * half + 512]
                    .rearrange("(k p) n -> p k n", p=P)), (kn, 512)

        def slot(kind, i):
            k, w = source(kind, i if isinstance(i, int) else 0)[1]
            return ring[:, number[kind, i] % RING, 0:k * w].rearrange("p (k n) -> p k n", n=w)

        def full(kind, i):
            n = number[kind, i]
            return sem(f"tile_loaded_{n % RING}"), 16 * (n // RING + 1)

        dense_index = {}
        for t in order:
            if t[0] not in ("gate", "up", "down"):
                dense_index[t] = len(dense_index) + 1

        def freed(n):
            kind, i = order[n]
            if kind in ("gate", "up", "down"):
                return sem(kind + "_used"), i + 1
            return sem("dense_used"), dense_index[order[n]]

        def dense_wait(eng, kind, i):
            eng.wait_ge(sem("dense_used"), dense_index[kind, i])

        block = ctx.enter_context(nc.Block())

        @block.sync
        def _(sp):
            def load(n):
                kind, i = order[n]
                src, (k, w) = source(kind, i)
                if n >= RING:
                    sp.wait_ge(*freed(n - RING))
                sp.dma_start(slot(kind, i), src).then_inc(sem(f"tile_loaded_{n % RING}"), 16)

            n = 0
            while n < len(order):
                kind, i = order[n]
                if kind != "gate":
                    load(n)
                    n += 1
                    continue
                e0, e1 = next(r for r in MOE_RANGES if r[0] == i)
                for m in range(n, n + RING):
                    load(m)
                with sp.Fori(1, (e1 - e0) // 2) as it:
                    for u in range(2):
                        for j, what in enumerate(("gate", "up", "down")):
                            src = a["w_" + what].rearrange(
                                "e (k p) n -> e p k n" if what == "down" else "e (p k) n -> e p k n", p=P)
                            m = n + 3 * u + j
                            sp.wait_ge(sem(what + "_used"), it * 2 + (e0 + u - 1))
                            sp.dma_start(slot(what, e0 + u), src[it * 2 + (e0 + u)]).then_inc(
                                sem(f"tile_loaded_{m % RING}"), 16)
                n += 3 * (e1 - e0)
            for t in range(TT):
                sp.wait_ge(sem("out_ready"), t + 1)
                sp.dma_start(out[0, t * P:(t + 1) * P, :], o_tok[:, t, :]).then_inc(sem("out_stored"), 16)
            sp.wait_ge(sem("out_stored"), 16 * TT)

        @block.tensor
        def _(pe):
            mm, tr = nc.tensor.matmul, nc.tensor.transpose

            def tile(kind, i):
                pe.wait_ge(*full(kind, i))
                return slot(kind, i)

            def release(ins, kind, i):
                ins.then_inc(sem("dense_used"), 1)

            def feature_major(w, acts, bank, blocks=4):
                for f in range(blocks):
                    for k in range(KD):
                        last = mm(ps[:, bank + f // 2, (f % 2) * 256:(f % 2) * 256 + 256],
                                  w[:, k, f * P:(f + 1) * P], acts[:, k, :], start=k == 0, stop=k == KD - 1)
                return last

            def token_major(w, acts, bank):
                for t in range(TT):
                    for k in range(KD):
                        last = mm(ps[:, bank + t, :], acts[:, k, t * P:(t + 1) * P], w[:, k, :],
                                  start=k == 0, stop=k == KD - 1)
                return last

            def transposed(src, bank, strided=False):
                for k in range(KD):
                    for t in range(TT):
                        piece = src[:, t, k::KD] if strided else src[:, t, k * P:(k + 1) * P]
                        o = (k % 2) * 256 + t * P
                        last = tr(ps[:, bank + k // 2, o:o + P], piece, ident)
                return last

            pe.wait_ge(sem("consts_loaded"), 16)
            pe.wait_ge(sem("norm1_scaled"), TT)
            transposed(xn, 0).then_inc(sem("h1_transposed"), 1)
            pe.wait_ge(sem("h1_ready"), KD)
            release(token_major(tile("w_in", 0), hT, 4), "w_in", 0)
            release(token_major(tile("w_in", 1), hT, 6), "w_in", 1)
            pe.wait_ge(sem("qk_rotated"), 1)
            release(token_major(tile("w_in", 2), hT, 4), "w_in", 2)
            for h in range(HEADS1):
                for t in range(TT):
                    last = tr(ps[:, h // 2, (h % 2) * 256 + t * P:(h % 2) * 256 + t * P + P],
                              qk_rot[:, 0, t, h * P:(h + 1) * P], ident)
            last.then_inc(sem("qk_transposed"), 1)
            pe.wait_ge(sem("qk_rotated"), 2)
            for h in range(HEADS1):
                for t in range(TT):
                    last = tr(ps[:, 2 + h // 2, (h % 2) * 256 + t * P:(h % 2) * 256 + t * P + P],
                              qk_rot[:, 1, t, h * P:(h + 1) * P], ident)
            last.then_inc(sem("qk_transposed"), 1)
            release(token_major(tile("w_in", 3), hT, 6), "w_in", 3)
            pe.wait_ge(sem("qkT_ready"), 2)
            for h in range(HEADS1):
                mm(ps[:, h, 0:256], qkT[:, 1, h, 0:P], qkT[:, 0, h, :], start=True, stop=True)
                mm(ps[:, h, 256:384], qkT[:, 1, h, P:256], qkT[:, 0, h, P:256], start=True,
                   stop=True).then_inc(sem("scores_done"), 1)
            pe.wait_ge(sem("v_ready"), 1)
            release(feature_major(tile("w_in", 4), hT, 4), "w_in", 4)
            pe.wait_ge(sem("decayed"), HEADS1)
            for t in range(TT):
                for h in range(HEADS1):
                    o = ps[:, t, h * P:(h + 1) * P]
                    mm(o, probs[:, h, t * P:(t + 1) * P], v_tok[:, 0, h * P:(h + 1) * P], start=True, stop=t == 0)
                    if t == 1:
                        mm(o, probs[:, h, 256:384], v_tok[:, 1, h * P:(h + 1) * P], start=False, stop=True)
            pe.wait_ge(sem("g_ready"), 1)
            release(feature_major(tile("w_in", 5), hT, 6), "w_in", 5)
            pe.wait_ge(sem("gb_ready"), 1)
            release(feature_major(tile("w_in", 6), hT, 4), "w_in", 6)
            pe.wait_ge(sem("ret_ready"), TT)
            for f in range(4):
                for t in range(TT):
                    last = tr(ps[:, 2 + f // 2, (f % 2) * 256 + t * P:(f % 2) * 256 + t * P + P],
                              ret[:, t, f * P:(f + 1) * P], ident)
            last.then_inc(sem("ret_transposed"), 1)
            pe.wait_ge(sem("mix_ret_ready"), 4)
            pe.wait_ge(sem("mix_conv_ready"), 4)
            for i in range(2):
                w = tile("w_o", i)
                for t in range(TT):
                    for half in range(2):
                        for k in range(4):
                            last = mm(ps[:, 4 + 2 * t + half, :], mixT[:, 4 * i + k, t * P:(t + 1) * P],
                                      w[:, k, half * 512:half * 512 + 512], start=i + k == 0, stop=i == 1 and k == 3)
                release(last, "w_o", i)

            pe.wait_ge(sem("norm2_scaled"), TT)
            transposed(xn, 0, strided=True).then_inc(sem("h2_transposed"), 1)
            pe.wait_ge(sem("h2_ready"), KD)
            pe.wait_ge(sem("router_loaded"), 48)
            for t in range(TT):
                for k in range(KD):
                    last = mm(ps[:, 4, t * 72:t * 72 + 72], h2T[:, k, t * P:(t + 1) * P], router_w[:, k, :],
                              start=k == 0, stop=k == KD - 1)
            last.then_inc(sem("router_done"), 1)
            pe.wait_ge(sem("assigned_ready"), 1)
            mm(ps[:, 5, 0:64], before, assigned[:, 0, :], start=True, stop=True)
            mm(ps[:, 5, 64:128], ones, assigned[:, 0, :], start=True, stop=False)
            mm(ps[:, 5, 64:128], before, assigned[:, 1, :], start=False, stop=True)
            mm(ps[:, 5, 128:192], ones, assigned[:, 0, :], start=True, stop=False)
            mm(ps[:, 5, 128:192], ones, assigned[:, 1, :], start=False, stop=True).then_inc(sem("counted"), 1)
            pe.wait_ge(sem("sel_ready"), 1)
            for k in range(KD):
                if k >= 4:
                    pe.wait_ge(sem("gathered"), k - 3)
                for t in range(TT):
                    last = mm(ps[:, k % 4, :], xn[:, t, k::KD], sel[:, t, :], start=t == 0, stop=t == TT - 1)
                last.then_inc(sem("gather_done"), 1)
            pe.wait_ge(sem("gated_ready"), 1)
            for s in range(SLOTS // P):
                for t in range(TT):
                    last = tr(ps[:, 6 + s // 2, (s % 2) * 256 + t * P:(s % 2) * 256 + t * P + P],
                              gated[:, t, s * P:(s + 1) * P], ident)
            last.then_inc(sem("gated_transposed"), 1)
            pe.wait_ge(sem("gathered"), KD)

            def up_part(e, u, n, wait, rounds, r, done):
                for j, what in enumerate(("gate", "up")):
                    if r == 0:
                        pe.wait_ge(*wait(what))
                    w = ring[:, (n + j) % RING, :].rearrange("p (k n) -> p k n", n=FF)
                    for f in range(KF):
                        for k in range(KD):
                            last = mm(ps[:, 2 * j + u, f * WIN:(f + 1) * WIN],
                                      w[:, k, f * P:(f + 1) * P], win[:, u, k, :], start=k == 0, stop=k == KD - 1)
                    if r == rounds - 1:
                        last.then_inc(sem(what + "_used"), 1)
                    elif j == 1:
                        last.then_inc(sem("round_up"), 1)

            def down_part(u, n, rounds, r):
                w = ring[:, (n + 2) % RING, :].rearrange("p (k n) -> p k n", n=D)
                for f in range(KD):
                    for k in range(KF):
                        last = mm(ps[:, 4 + u, f * WIN:(f + 1) * WIN], w[:, k, f * P:(f + 1) * P],
                                  hidden[:, u, k, :], start=k == 0, stop=k == KF - 1)
                last.then_inc(sem("down_used" if r == rounds - 1 else "round_down"), 1)

            def pe_fast(e0, e1):
                n0 = number["gate", e0]

                def loaded(j, u, it):
                    n = n0 + 3 * u + j
                    return sem(f"tile_loaded_{n % RING}"), (it + n // RING + 1) * 16

                def up(u, it, first=False):
                    e = it * 2 + (e0 + u)
                    pe.wait_ge(sem("win_ready"), e + 1)
                    if not first:
                        pe.wait_ge(sem("hidden_ready"), e - 1)
                    up_part(e, u, n0 + 3 * u, lambda what: loaded(0 if what == "gate" else 1, u, it), 1, 0, None)

                def down(u, it, first=False):
                    e = it * 2 + (e0 + u)
                    pe.wait_ge(*loaded(2, u, it))
                    pe.wait_ge(sem("hidden_ready"), e + 1)
                    if not first:
                        pe.wait_ge(sem("y_written"), e - 1)
                    down_part(u, n0 + 3 * u, 1, 0)

                start = e0 == 0
                up(0, 0, start)
                up(1, 0, start)
                down(0, 0, start)
                up(0, 1)
                down(1, 0, start)
                with pe.Fori(1, (e1 - e0) // 2 - 1) as it:
                    up(1, it)
                    down(0, it)
                    up(0, it + 1)
                    down(1, it)
                last = (e1 - e0) // 2 - 1
                up(1, last)
                down(0, last)
                down(1, last)

            def pe_slow(e0, e1):
                n0 = number["gate", e0]

                def expert(u, it, first=False):
                    e = it * 2 + (e0 + u)
                    for r in range(ROUNDS):
                        pe.wait_ge(sem("win_ready"), e * ROUNDS + r + 1)
                        if not (first and u == 0 and r == 0):
                            pe.wait_ge(sem("hidden_ready"), e * ROUNDS + r)
                        up_part(e, u, n0 + 3 * u, lambda what: (
                            sem(f"tile_loaded_{(n0 + 3 * u + (what == 'up')) % RING}"),
                            (it + (n0 + 3 * u + (what == 'up')) // RING + 1) * 16), ROUNDS, r, None)
                        if r == 0:
                            pe.wait_ge(sem(f"tile_loaded_{(n0 + 3 * u + 2) % RING}"),
                                       (it + (n0 + 3 * u + 2) // RING + 1) * 16)
                        pe.wait_ge(sem("hidden_ready"), e * ROUNDS + r + 1)
                        if not (first and u == 0 and r == 0):
                            pe.wait_ge(sem("y_written"), e * ROUNDS + r)
                        down_part(u, n0 + 3 * u, ROUNDS, r)

                for u in range(2):
                    expert(u, 0, e0 == 0)
                with pe.Fori(1, (e1 - e0) // 2) as it:
                    for u in range(2):
                        expert(u, it)

            def moe(e0, e1):
                flag = pe.value_load(many[0:1, 0:1], min_val=0, max_val=1)
                with pe.If(flag < 1):
                    pe_fast(e0, e1)
                with pe.Else():
                    pe_slow(e0, e1)

            pe.wait_ge(sem("starts_ready"), 1)
            moe(*MOE_RANGES[0])

            pe.wait_ge(sem("csil_ready"), 1)
            for i in range(12):
                w = tile("ada", i)
                for f in range(4):
                    for k in range(KD):
                        last = mm(ps[:, 6, (4 * i + f) * 2:(4 * i + f) * 2 + 2], w[:, k, f * P:(f + 1) * P],
                                  csil[:, k, :], start=k == 0, stop=k == KD - 1)
                release(last, "ada", i)
            pe.wait_ge(sem("normc_scaled"), TT)
            pe.wait_ge(sem("mod_ready"), 1)
            transposed(c_raw, 4).then_inc(sem("hc_transposed"), 1)
            pe.wait_ge(sem("hc_ready"), KD)
            for g in range(NG):
                if g:
                    pe.wait_ge(sem("ctx_state_ready"), GH * g)
                release(feature_major(tile("ctx", 3 * g), hcT, 4), "ctx", 3 * g)
                release(feature_major(tile("ctx", 3 * g + 1), hcT, 6), "ctx", 3 * g + 1)
                pe.wait_ge(sem("ctx_f_read"), 2 * g + 1)
                release(token_major(tile("ctx", 3 * g + 2), hcT, 4), "ctx", 3 * g + 2)
                pe.wait_ge(sem("ctx_kd_ready"), 2 * (g + 1))
                pe.wait_ge(sem("ctx_v_ready"), g + 1)
                for h in range(GH):
                    if h or g:
                        pe.wait_ge(sem("ctx_state_ready"), GH * g + h)
                    for d in range(2):
                        for t in range(TT):
                            last = tr(ps[:, 4, (2 * d + t) * P:(2 * d + t + 1) * P],
                                      c_p[:, d, h, t * P:(t + 1) * P], ident)
                    last.then_inc(sem("ctx_kd_transposed"), 1)
                    pe.wait_ge(sem("ctx_kdT_ready"), GH * g + h + 1)
                    for d in range(2):
                        for t in range(TT):
                            last = mm(ps[:, 5, d * P:(d + 1) * P], c_kT[:, d, t, :], c_v[:, t, h * P:(h + 1) * P],
                                      start=t == 0, stop=t == 1)
                    last.then_inc(sem("ctx_state_done"), 1)
            moe(*MOE_RANGES[1])

            pe.wait_ge(sem("y_complete"), 1)
            for s in range(SLOTS // P):
                if s >= 2:
                    pe.wait_ge(sem("y_tok_ready"), s - 1)
                for k in range(KD):
                    last = tr(ps[:, 2 * (s % 2) + k // 4, (k % 4) * P:(k % 4 + 1) * P],
                              YT[:, k, s * P:(s + 1) * P], ident)
                last.then_inc(sem("y_transposed"), 1)
            pe.wait_ge(sem("y_tok_ready"), SLOTS // P)
            pe.wait_ge(sem("ctx_state_ready"), HEADS2)
            for k in range(KD):
                o = ps[:, 4 + k // 2, (k % 2) * 256:(k % 2) * 256 + 256]
                for s in range(SLOTS // P):
                    mm(o, y_tok[:, s, k * P:(k + 1) * P], sgT[:, s, :], start=s == 0, stop=False)
                for t in range(TT):
                    last = mm(o[:, t * P:(t + 1) * P], x1[:, t, k * P:(k + 1) * P], ident, start=False, stop=t == 1)
            last.then_inc(sem("combined"), 1)

            def norm_sums(name, src, bank):
                pe.wait_ge(sem(name + "_squared"), 1)
                for k in range(KD):
                    last = mm(ps[:, bank, 0:TOKENS], ones, src[:, k, :], start=k == 0, stop=k == KD - 1)
                last.then_inc(sem(name + "_summed"), 1)

            norm_sums("normf", sq, 0)
            norm_sums("norml", sq, 1)
            pe.wait_ge(sem("hl_ready"), 1)

            def attend(g):
                for h in range(GH):
                    n = GH * g + h
                    if n:
                        pe.wait_ge(sem("readout_done"), n)
                    for d in range(2):
                        for c in range(NCH):
                            lo = (c % 2) * CHUNK2
                            k0, HC = h * TOKENS + c * CHUNK2, CHUNK2 // 2
                            for half in range(2):
                                o = ((c // 2) * 2 + d) * CHUNK2 + half * HC
                                m0, mn = (half * HC, HC) if half == d else (0, CHUNK2)
                                last = mm(ps[lo + m0:lo + m0 + mn, 4, o:o + HC],
                                          prod[:, d, 1, k0 + m0:k0 + m0 + mn],
                                          prod[:, d, 0, k0 + half * HC:k0 + (half + 1) * HC], start=True, stop=True)
                    last.then_inc(sem("s_done"), 1)
                    for d in range(2):
                        for t in range(TT):
                            last = tr(ps[:, 5, (2 * d + t) * P:(2 * d + t + 1) * P],
                                      prod[:, d, 3, h * TOKENS + t * P:h * TOKENS + (t + 1) * P], ident)
                    last.then_inc(sem("kd_transposed"), 1)
                    pe.wait_ge(sem("kdT_ready"), n + 1)
                    for d in range(2):
                        for j in range(NCH - 1):
                            c = j if d == 0 else NCH - 1 - j
                            lo = (c % 2) * CHUNK2
                            last = mm(kv_bank(d, c),
                                      kdT[lo:lo + CHUNK2, d, c // 2, :],
                                      v_s[lo:lo + CHUNK2, c // 2, h * P:(h + 1) * P], start=True, stop=True)
                    last.then_inc(sem("kv_done"), 1)
                    pe.wait_ge(sem("masked_ready"), n + 1)
                    o = ps[:, 5, 0:TOKENS]
                    for t in range(TT):
                        for d in range(2):
                            mm(o[:, t * P:(t + 1) * P], v_s[:, t, h * P:(h + 1) * P], masked[:, d, t, :],
                               start=d == 0 and t == 0, stop=False, skip_group_check=True)
                    pe.wait_ge(sem("states_ready"), 2 * (n + 1))
                    for d in range(2):
                        for j in range(NCH):
                            c = j if d == 0 else NCH - 1 - j
                            s = state[:, n, d, :] if j == 0 else chunk_state[:, d, j, :]
                            last = mm(o[:, c * CHUNK2:(c + 1) * CHUNK2], s,
                                      prod[:, d, 2, h * TOKENS + c * CHUNK2:h * TOKENS + (c + 1) * CHUNK2],
                                      start=False, stop=d == 1 and j == NCH - 1, skip_group_check=True)
                    last.then_inc(sem("o_done"), 1)
                    pe.wait_ge(sem("o_squared"), n + 1)
                    mm(ps[:, 4, 256:512], ones, o_sq[:, :], start=True, stop=True).then_inc(sem("o_summed"), 1)

            for g in range(NG):
                if g:
                    pe.wait_ge(sem("lat_read"), 5 * g - 1)
                release(feature_major(tile("lat", 5 * g), hl, 0), "lat", 5 * g)
                if g:
                    pe.wait_ge(sem("lat_read"), 5 * g)
                release(feature_major(tile("lat", 5 * g + 1), hl, 2), "lat", 5 * g + 1)
                pe.wait_ge(sem("lat_read"), 5 * g + 1)
                release(token_major(tile("lat", 5 * g + 2), hl, 0), "lat", 5 * g + 2)
                pe.wait_ge(sem("lat_read"), 5 * g + 2)
                release(feature_major(tile("lat", 5 * g + 3), hl, 2), "lat", 5 * g + 3)
                pe.wait_ge(sem("lat_read"), 5 * g + 3)
                release(feature_major(tile("lat", 5 * g + 4), hl, 0), "lat", 5 * g + 4)
                pe.wait_ge(sem("lat_read"), 5 * g + 5)
                pe.wait_ge(sem("prod_ready"), 2 * (g + 1))
                attend(g)
            pe.wait_ge(sem("readout_done"), HEADS2)
            for i in range(2):
                release(feature_major(tile("hg_out", i), attn, 2 * i), "hg_out", i)
            norm_sums("norm3", sq, 4)
            pe.wait_ge(sem("hl_ready"), 2)

            for b in range(NB):
                i, f = b // 4, b % 4
                for part in range(2):
                    w = tile("ffn_up", 2 * i + part) if f == 0 else slot("ffn_up", 2 * i + part)
                    m = 2 * b + part
                    if m >= 4:
                        pe.wait_ge(sem("conv_read"), m - 3)
                    for k in range(KD):
                        last = mm(ps[:, m % 4, 0:256], w[:, k, f * P:(f + 1) * P], hl[:, k, :],
                                  start=k == 0, stop=k == KD - 1)
                    last.then_inc(sem("up_done"), 1) if not (f == 3 or b == NB - 1) else release(last, "ffn_up", 0)
            for half in range(2):
                for part in range(3):
                    w = tile("ffn_down", 3 * half + part)
                    k0, kn = (0, 8, 16)[part], (8, 8, 6)[part]
                    pe.wait_ge(sem("act_ready"), k0 + kn)
                    if half == 0 and part == 0:
                        pe.wait_ge(sem("hl_ready"), 2)
                    if half == 1 and part == 0:
                        pe.wait_ge(sem("act_ready"), NB)
                    for f in range(4):
                        for k in range(kn):
                            last = mm(ps[:, 4 - 4 * half + f, 0:TOKENS], w[:, k, f * P:(f + 1) * P], act[:, k0 + k, :],
                                      start=k0 + k == 0, stop=k0 + k == NB - 1)
                    release(last, "ffn_down", 3 * half + part)
            pe.wait_ge(sem("last_residual"), 2)
            norm_sums("norm4", sq, 0)
            pe.wait_ge(sem("final_scaled"), KD)
            for t in range(TT):
                for k in range(KD):
                    last = tr(ps[:, 4 + 2 * t + k // 4, (k % 4) * P:(k % 4 + 1) * P], hl[:, k, t * P:(t + 1) * P], ident)
                last.then_inc(sem("out_transposed"), 1)

        @block.scalar
        def _(act_e):
            af = nc.scalar.activation
            steps = [0]

            def link(ins):
                steps[0] += 1
                ins.then_inc(sem("scalar_step"), 1)
                act_e.wait_ge(sem("scalar_step"), steps[0])

            act_e.dma_start(x1[:, :, :], a["x"]).then_inc(sem("x_loaded"), 16)
            act_e.dma_start(consts[:, :, :], a["consts"]).then_inc(sem("consts_loaded"), 16)
            act_e.dma_start(vecs[:, :], a["vecs"]).then_inc(sem("vecs_loaded"), 16)
            act_e.dma_start(rope, a["rope"]).then_inc(sem("rope_loaded"), 16)
            act_e.dma_start(decay, a["decay"]).then_inc(sem("decay_loaded"), 16)
            act_e.dma_start(hmask[:, :, :], a["hmask"]).then_inc(sem("hmask_loaded"), 16)

            def sums(name, src, junk, where):
                for t in range(TT):
                    link(af(junk[:, t, :], src[:, t, :], ACT.Square, accum_out=col(where + t)))
                act_e.nop().then_inc(sem(name + "_sums"), 1)

            def rsqrt(dst, src):
                link(af(dst, src, ACT.Ln))
                return af(dst, dst, ACT.Exp, scale=-0.5)

            act_e.wait_ge(sem("x_loaded"), 16)
            for t in range(TT):
                last = af(xn[:, t, :], x1[:, t, :], ACT.Square, accum_out=col(t))
            last.then_inc(sem("norm1_sums"), 1)
            act_e.wait_ge(sem("norm1_mean"), 1)
            rsqrt(col(2, 2), col(2, 2)).then_inc(sem("norm1_rstd"), 1)
            act_e.wait_ge(sem("h1_transposed"), 1)
            act_e.wait_ge(sem("vecs_loaded"), 16)
            for k in range(KD):
                af(hT[:, k, :], ps[:, k // 2, (k % 2) * 256:(k % 2) * 256 + 256], ACT.Copy,
                   scale=vec("norm1", k)).then_inc(sem("h1_ready"), 1)
            for j, name in enumerate(("c", "c_ctx")):
                last = af(csil[:, :, j], vec(name, 0, KD), ACT.Silu)
                last.then_inc(sem("csil_part"), 1)
            act_e.wait_ge(sem("csil_part"), 2)
            act_e.nop().then_inc(sem("csil_ready"), 1)
            dense_wait(act_e, "w_in", 2)
            af(v_tok, ps[:, 4:6, :], ACT.Copy).then_inc(sem("v_ready"), 1)
            for j in range(2):
                act_e.wait_ge(sem("qk_transposed"), j + 1)
                af(qkT[:, j].rearrange("p (b h) n -> p b (h n)", b=2), ps[:, 2 * j:2 * j + 2, :],
                   ACT.Copy).then_inc(sem("qkT_ready"), 1)
            dense_wait(act_e, "w_in", 3)
            af(g_tok, ps[:, 6:8, :], ACT.Silu).then_inc(sem("g_ready"), 1)
            dense_wait(act_e, "w_in", 4)
            af(gb_s.rearrange("p (b f) n -> p b (f n)", b=2), ps[:, 4:6, :], ACT.Copy).then_inc(sem("gb_ready"), 1)
            dense_wait(act_e, "w_in", 5)
            af(gc_s.rearrange("p (b f) n -> p b (f n)", b=2), ps[:, 6:8, :], ACT.Copy).then_inc(sem("gc_ready"), 1)
            act_e.wait_ge(sem("gn_var"), 1)
            rsqrt(col(8, 8), col(8, 8)).then_inc(sem("gn_rstd"), 1)
            act_e.wait_ge(sem("ret_transposed"), 1)
            for f in range(4):
                af(mixT[:, f, :], ps[:, 2 + f // 2, (f % 2) * 256:(f % 2) * 256 + 256], ACT.Copy,
                   scale=vec("ret_gn", f)).then_inc(sem("mix_ret_ready"), 1)

            act_e.wait_ge(sem("x1_ready"), TT)
            for t in range(TT):
                last = af(xn[:, t, :], x1[:, t, :], ACT.Square, accum_out=col(t))
            last.then_inc(sem("norm2_sums"), 1)
            act_e.dma_start(router_w, a["router_w"]).then_inc(sem("router_loaded"), 16)
            act_e.dma_start(router_b, a["router_b"]).then_inc(sem("router_loaded"), 16)
            act_e.dma_start(iota, a["iota"]).then_inc(sem("router_loaded"), 16)
            act_e.wait_ge(sem("norm2_mean"), 1)
            rsqrt(col(2, 2), col(2, 2)).then_inc(sem("norm2_rstd"), 1)
            act_e.wait_ge(sem("h2_transposed"), 1)
            for k in range(KD):
                af(h2T[:, k, :], ps[:, k // 2, (k % 2) * 256:(k % 2) * 256 + 256], ACT.Copy,
                   scale=vec("norm2", k)).then_inc(sem("h2_ready"), 1)
            for j in range(2):
                act_e.wait_ge(sem("softmax_in"), j + 1)
                for t in range(TT):
                    last = af(rt[:, t, 8 + 40 * j:16 + 40 * j], rt[:, t, 8 + 40 * j:16 + 40 * j], ACT.Exp,
                              accum_out=rt[:, t, 36 + 40 * j:37 + 40 * j])
                last.then_inc(sem("softmax_exp"), 1)
            for k in range(KD):
                act_e.wait_ge(sem("gather_done"), k + 1)
                af(XgT[:, k, 0:SLOTS], ps[:, k % 4, :], ACT.Copy, scale=vec("norm2", k)).then_inc(sem("gathered"), 1)
            act_e.wait_ge(sem("gated_transposed"), 1)
            af(sgT[:, :, :].rearrange("p (b s) n -> p b (s n)", b=2), ps[:, 6:8, :], ACT.Copy).then_inc(
                sem("sgT_ready"), 1)

            def act_fast(e0, e1):
                def silu(u, it, first=False):
                    e = it * 2 + (e0 + u)
                    act_e.wait_ge(sem("gate_used"), e + 1)
                    if not first:
                        act_e.wait_ge(sem("hidden_ready"), e - 1)
                    af(silu_g[:, u].rearrange("p a b -> p (a b)"), ps[:, u, 0:256], ACT.Silu).then_inc(
                        sem("silu_ready"), 1)

                def store(u, it, first=False):
                    e = it * 2 + (e0 + u)
                    if not first:
                        act_e.wait_ge(sem("y_written"), e)
                    begin = act_e.value_load(starts[0:1, 0, bass.ds(e, 1)], min_val=0, max_val=SLOTS)
                    act_e.wait_ge(sem("down_used"), e + 1)
                    af(YT[:, :, bass.ds(begin, WIN)], ps[:, 4 + u, :].rearrange("p (a b) -> p a b", b=WIN),
                       ACT.Copy).then_inc(sem("y_written"), 1)

                start = e0 == 0
                silu(0, 0, start)
                silu(1, 0, start)
                store(0, 0, start)
                silu(0, 1)
                store(1, 0)
                with act_e.Fori(1, (e1 - e0) // 2 - 1) as it:
                    silu(1, it)
                    store(0, it)
                    silu(0, it + 1)
                    store(1, it)
                last = (e1 - e0) // 2 - 1
                silu(1, last)
                store(0, last)
                store(1, last)

            def act_slow(e0, e1):
                def expert(u, it, first=False):
                    e = it * 2 + (e0 + u)
                    for r in range(ROUNDS):
                        if r == ROUNDS - 1:
                            act_e.wait_ge(sem("up_used"), e + 1)
                        else:
                            act_e.wait_ge(sem("round_up"), e * (ROUNDS - 1) + r + 1)
                        if not (first and u == 0 and r == 0):
                            act_e.wait_ge(sem("hidden_ready"), e * ROUNDS + r)
                        af(silu_g[:, u].rearrange("p a b -> p (a b)"), ps[:, u, 0:256], ACT.Silu).then_inc(
                            sem("silu_ready"), 1)
                        begin = act_e.value_load(starts[0:1, r, bass.ds(e, 1)], min_val=0, max_val=SLOTS)
                        if not (first and u == 0 and r == 0):
                            act_e.wait_ge(sem("y_written"), e * ROUNDS + r)
                        if r == ROUNDS - 1:
                            act_e.wait_ge(sem("down_used"), e + 1)
                        else:
                            act_e.wait_ge(sem("round_down"), e * (ROUNDS - 1) + r + 1)
                        af(YT[:, :, bass.ds(begin, WIN)], ps[:, 4 + u, :].rearrange("p (a b) -> p a b", b=WIN),
                           ACT.Copy).then_inc(sem("y_written"), 1)

                for u in range(2):
                    expert(u, 0, e0 == 0)
                with act_e.Fori(1, (e1 - e0) // 2) as it:
                    for u in range(2):
                        expert(u, it)

            def moe(e0, e1):
                flag = act_e.value_load(many[0:1, 0:1], min_val=0, max_val=1)
                with act_e.If(flag < 1):
                    act_fast(e0, e1)
                with act_e.Else():
                    act_slow(e0, e1)

            act_e.wait_ge(sem("starts_ready"), 1)
            moe(*MOE_RANGES[0])

            act_e.wait_ge(sem("lb_in"), 1)
            af(vec("lb", 0, 32), vec("lb", 0, 32), ACT.Exp).then_inc(sem("lb_exp"), 1)
            act_e.wait_ge(sem("ctx_loaded"), 16)
            for t in range(TT):
                last = af(hcT.rearrange("p a b -> p (a b)")[:, t * D:(t + 1) * D], c_raw[:, t, :], ACT.Square,
                          accum_out=col(t))
            last.then_inc(sem("normc_sums"), 1)
            act_e.wait_ge(sem("normc_mean"), 1)
            rsqrt(col(2, 2), col(2, 2)).then_inc(sem("normc_rstd"), 1)
            act_e.wait_ge(sem("hc_transposed"), 1)
            act_e.wait_ge(sem("mod_ready"), 1)
            for k in range(KD):
                af(hcT[:, k, :], ps[:, 4 + k // 2, (k % 2) * 256:(k % 2) * 256 + 256], ACT.Identity,
                   scale=scales[:, 0, k:k + 1], bias=mod[:, k, 1:2]).then_inc(sem("hc_ready"), 1)
            for g in range(NG):
                for d in range(2):
                    dense_wait(act_e, "ctx", 3 * g + d)
                    if d or g:
                        act_e.wait_ge(sem("ctx_kd_ready"), 2 * g + d)
                    af(c_f.rearrange("p (b f) n -> p b (f n)", b=2), ps[:, 4 + 2 * d:6 + 2 * d, :],
                       ACT.Sigmoid).then_inc(sem("ctx_f_read"), 1)
                dense_wait(act_e, "ctx", 3 * g + 2)
                if g == 0:
                    act_e.wait_ge(sem("hc_transposed"), 1)
                else:
                    act_e.wait_ge(sem("ctx_state_done"), GH * g)
                af(c_v, ps[:, 4:6, :], ACT.Copy).then_inc(sem("ctx_v_ready"), 1)
                for h in range(GH):
                    n = GH * g + h
                    act_e.wait_ge(sem("ctx_kd_transposed"), n + 1)
                    if n:
                        act_e.wait_ge(sem("ctx_state_done"), n)
                    af(c_kT.rearrange("p a b c -> p (a b c)"), ps[:, 4, :], ACT.Copy).then_inc(sem("ctx_kdT_ready"), 1)
                    act_e.wait_ge(sem("ctx_state_done"), n + 1)
                    af(state[:, n].rearrange("p a b -> p (a b)"), ps[:, 5, 0:256], ACT.Copy).then_inc(
                        sem("ctx_state_ready"), 1)
            moe(*MOE_RANGES[1])
            flag = act_e.value_load(many[0:1, 0:1], min_val=0, max_val=1)
            with act_e.If(flag < 1):
                act_e.wait_ge(sem("y_written"), EXPERTS)
            with act_e.Else():
                act_e.wait_ge(sem("y_written"), EXPERTS * ROUNDS)
            act_e.nop().then_inc(sem("y_complete"), 1)

            for s in range(SLOTS // P):
                act_e.wait_ge(sem("y_transposed"), s + 1)
                if s == 0:
                    act_e.wait_ge(sem("up_used"), EXPERTS)
                af(y_tok[:, s, :].rearrange("p (a b) -> p a b", b=512), ps[:, 2 * (s % 2):2 * (s % 2) + 2, :],
                   ACT.Copy).then_inc(sem("y_tok_ready"), 1)

            def norm(name, src, psum_in=False):
                act_e.wait_ge(sem(name + "_in"), 1)
                af(sq.rearrange("p a b -> p (a b)"), src.rearrange("p a b -> p (a b)"), ACT.Square).then_inc(
                    sem(name + "_squared"), 1)

            def root(name, bank, width, n=1):
                act_e.wait_ge(sem(name + "_summed"), n)
                act_e.wait_ge(sem(name + "_mean"), n)
                link(af(o_n[:, :], o_n[:, :], ACT.Ln))
                af(ps[:, bank, 256:512], o_n[:, :], ACT.Exp, scale=-0.5).then_inc(sem(name + "_rstd"), 1)

            norm("normf", hl)
            root("normf", 0, D)
            norm("norml", lat)
            root("norml", 1, D)
            act_e.wait_ge(sem("hl_scaled"), 1)
            for k in range(KD):
                last = af(hl[:, k, :], hl[:, k, :], ACT.Identity, bias=mod[:, k, 0:1])
            last.then_inc(sem("hl_ready"), 1)

            for g in range(NG):
                for d in range(2):
                    dense_wait(act_e, "lat", 5 * g + d)
                    dst = (lf, dd)[d]
                    if g:
                        act_e.wait_ge(sem("prod_ready"), 2 * g)
                    af(dst.rearrange("p (b n) -> p b n", b=2), ps[:, 2 * d:2 * d + 2, :], ACT.Sigmoid).then_inc(
                        sem("lat_read"), 1)
                dense_wait(act_e, "lat", 5 * g + 2)
                if g:
                    act_e.wait_ge(sem("o_done"), GH * g)
                af(v_s, ps[:, 0:2, :], ACT.Copy).then_inc(sem("lat_read"), 1)
                dense_wait(act_e, "lat", 5 * g + 3)
                af(q_s.rearrange("p (b f) n -> p b (f n)", b=2), ps[:, 2:4, :], ACT.Silu).then_inc(sem("lat_read"), 1)
                dense_wait(act_e, "lat", 5 * g + 4)
                if g:
                    act_e.wait_ge(sem("readout_done"), GH * g)
                af(g_s.rearrange("p (b f) n -> p b (f n)", b=2), ps[:, 0:2, :], ACT.Silu).then_inc(sem("lat_read"), 1)
                for d in range(2):
                    m = 2 * g + d
                    act_e.wait_ge(sem("f_ready"), m + 1)
                    af(lf if d == 0 else dd, lf if d == 0 else dd, ACT.Ln).then_inc(sem("logf_ready"), 1)
                    if g:
                        act_e.wait_ge(sem("o_done"), GH * g)
                    act_e.wait_ge(sem("b_ready"), m + 1)
                    af(prod[:, d, 2, :], b_s, ACT.Exp).then_inc(sem("eb_ready"), 1)
                    act_e.wait_ge(sem("bref_ready"), m + 1)
                    af(prod[:, d, 0, :], prod[:, d, 1, :], ACT.Exp).then_inc(sem("eq_ready"), 1)
                    act_e.wait_ge(sem("eq_ready"), m + 1)
                    af(prod[:, d, 1, :], prod[:, d, 1, :], ACT.Exp, scale=-1.0).then_inc(sem("ek_ready"), 1)
                    act_e.wait_ge(sem("blast_ready"), m + 1)
                    af(prod[:, d, 3, :], prod[:, d, 3, :], ACT.Exp).then_inc(sem("el_ready"), 1)
                    last_of = (CHUNK2 - 1, 0)[d]
                    af(dec[:, d, :], b_s.rearrange("p (c n) -> p c n", n=CHUNK2)[:, :, last_of], ACT.Exp).then_inc(
                        sem("dec_ready"), 1)
                for h in range(GH):
                    n = GH * g + h
                    act_e.wait_ge(sem("kd_transposed"), n + 1)
                    if n:
                        act_e.wait_ge(sem("kv_done"), n)
                    af(kdT[:, :, :, :].rearrange("p a b c -> p (a b c)"), ps[:, 5, :], ACT.Copy).then_inc(
                        sem("kdT_ready"), 1)
                    act_e.wait_ge(sem("o_done"), n + 1)
                    if n:
                        act_e.wait_ge(sem("o_summed"), n)
                    af(o_sq[:, :], ps[:, 5, 0:256], ACT.Square).then_inc(sem("o_squared"), 1)
                    root("o", 6, P, n + 1)

            norm("norm3", lat)
            root("norm3", 5, D)
            act_e.wait_ge(sem("hl_scaled"), 2)
            for k in range(KD):
                last = af(hl[:, k, :], hl[:, k, :], ACT.Identity, bias=mod[:, 24 + k, 0:1])
            last.then_inc(sem("hl_ready"), 1)
            for b in range(NB):
                for part in range(2):
                    m = 2 * b + part
                    i = part * NB + b
                    if b % 4 == 3 or b == NB - 1:
                        dense_wait(act_e, "ffn_up", 2 * (b // 4) + part)
                    else:
                        act_e.wait_ge(sem("up_done"), 2 * (3 * (b // 4) + b % 4) + part + 1)
                    if b >= 2:
                        act_e.wait_ge(sem("act_ready"), b - 1)
                    af(up_s[:, b % 2, part, :], ps[:, m % 4, 0:256], ACT.Identity,
                       scale=vec("ffn_w", 2 * NB + i), bias=vec("ffn_b", i)).then_inc(sem("conv_begun"), 1)
                act_e.wait_ge(sem("conv_read"), 2 * b + 2)
                af(sg_s[:, b % 2, :], up_s[:, b % 2, 0, :], ACT.Silu).then_inc(sem("ffn_silu"), 1)
            norm("norm4", lat)
            root("norm4", 1, D)
            for t in range(TT):
                act_e.wait_ge(sem("out_transposed"), t + 1)
                af(o_tok[:, t, :].rearrange("p (a b) -> p a b", b=512), ps[:, 4 + 2 * t:6 + 2 * t, :],
                   ACT.Copy).then_inc(sem("out_ready"), 1)

        @block.gpsimd
        def _(pool):
            pool.memset(gcu[:, :, 0:2], 0.0).then_inc(sem("pads_ready"), 1)
            pool.wait_ge(sem("mix_conv_ready"), 4)
            pool.wait_ge(sem("x1_ready"), TT)
            pool.memset(XgT[:, :, SLOTS:COLS], 0.0).then_inc(sem("tail_ready"), 1)
            pool.memset(masked[:, :, :, :], 0.0).then_inc(sem("masked_zeroed"), 1)

            def pool_fast(e0, e1):
                def window(u, it, first=False):
                    e = it * 2 + (e0 + u)
                    begin = pool.value_load(starts[0:1, 0, bass.ds(e, 1)], min_val=0, max_val=SLOTS)
                    if not first:
                        pool.wait_ge(sem("up_used"), e - 1)
                    pool.tensor_copy(win[:, u], XgT[:, :, bass.ds(begin, WIN)]).then_inc(sem("win_ready"), 1)

                for u in range(2):
                    window(u, 0, e0 == 0)
                with pool.Fori(1, (e1 - e0) // 2) as it:
                    for u in range(2):
                        window(u, it)

            def pool_slow(e0, e1):
                def expert(u, it, first=False):
                    e = it * 2 + (e0 + u)
                    for r in range(ROUNDS):
                        begin = pool.value_load(starts[0:1, r, bass.ds(e, 1)], min_val=0, max_val=SLOTS)
                        if not (first and u == 0 and r == 0):
                            pool.wait_ge(sem("hidden_ready"), e * ROUNDS + r)
                        pool.tensor_copy(win[:, u], XgT[:, :, bass.ds(begin, WIN)]).then_inc(sem("win_ready"), 1)

                for u in range(2):
                    expert(u, 0, e0 == 0)
                with pool.Fori(1, (e1 - e0) // 2) as it:
                    for u in range(2):
                        expert(u, it)

            def moe(e0, e1):
                flag = pool.value_load(many[0:1, 0:1], min_val=0, max_val=1)
                with pool.If(flag < 1):
                    pool_fast(e0, e1)
                with pool.Else():
                    pool_slow(e0, e1)

            pool.wait_ge(sem("starts_ready"), 1)
            pool.wait_ge(sem("gathered"), KD)
            pool.wait_ge(sem("gated_transposed"), 1)
            pool.dma_start(c_raw, a["ctx"]).then_inc(sem("ctx_loaded"), 16)
            pool.memset(zeros, 0.0).then_inc(sem("zeros_ready"), 1)
            moe(*MOE_RANGES[0])
            moe(*MOE_RANGES[1])
            pool.wait_ge(sem("combined"), 1)
            pool.memset(smask, 1.0).then_inc(sem("smask_step"), 1)
            pool.wait_ge(sem("smask_step"), 1)
            pool.memset(smask.rearrange("p (c n) -> p c n", n=CHUNK2)[:, :, 0:1], 0.0).then_inc(sem("smask_ready"), 1)

        @block.vector
        def _(dve):
            tt, ts, stt_ = nc.vector.tensor_tensor, nc.vector.tensor_scalar, nc.vector.scalar_tensor_tensor
            steps = [0]

            def link(ins):
                steps[0] += 1
                ins.then_inc(sem("vector_step"), 1)
                dve.wait_ge(sem("vector_step"), steps[0])

            def token_norm(name, src, dst):
                dve.wait_ge(sem(name + "_sums"), 1)
                ts(col(2, 2), col(0, 2), 1.0 / D, EPS, ALU.mult, ALU.add).then_inc(sem(name + "_mean"), 1)
                dve.wait_ge(sem(name + "_rstd"), 1)
                for t in range(TT):
                    ts(dst[:, t, :], src[:, t, :], col(2 + t), None, ALU.mult).then_inc(sem(name + "_scaled"), 1)

            token_norm("norm1", x1, xn)
            dve.wait_ge(sem("rope_loaded"), 16)
            for j in range(2):
                dense_wait(dve, "w_in", j)
                for t in range(TT):
                    src = ps[:, 4 + 2 * j + t, :].rearrange("p (h s d) -> p h s d", h=HEADS1, s=2)
                    ra = rot_a.rearrange("p (h d) -> p h d", h=HEADS1)
                    rb = rot_b.rearrange("p (h s d) -> p h s d", h=HEADS1, s=2)
                    cos = rope[:, 0, t, :].unsqueeze(1).to_broadcast([P, HEADS1, P])
                    tt(ra, ps[:, 4 + 2 * j + t, :].rearrange("p (h d) -> p h d", h=HEADS1), cos, ALU.mult)
                    for s in range(2):
                        sin = rope[:, 1, t, s * 64:(s + 1) * 64].unsqueeze(1).to_broadcast([P, HEADS1, 64])
                        last = tt(rb[:, :, s, :], src[:, :, 1 - s, :], sin, ALU.mult)
                    link(last)
                    last = tt(qk_rot[:, j, t, :], rot_a, rot_b, ALU.add)
                    if t == 0:
                        link(last)
                last.then_inc(sem("qk_rotated"), 1)
                dve.wait_ge(sem("qk_rotated"), j + 1)
            dve.wait_ge(sem("decay_loaded"), 16)
            for h in range(HEADS1):
                dve.wait_ge(sem("scores_done"), h + 1)
                tt(probs[:, h, 0:256], ps[:, h, 0:256], decay[:, h, :], ALU.mult)
                tt(probs[:, h, 256:384], ps[:, h, 256:384], decay[:, h, 0:P], ALU.mult).then_inc(sem("decayed"), 1)
            dense_wait(dve, "w_in", 5)
            for t in range(TT):
                for h in range(HEADS1):
                    last = nc.vector.bn_stats(stats[:, 4 * t + h, :], ps[:, t, h * P:(h + 1) * P])
            link(last)
            for m in range(8):
                last = nc.vector.bn_aggr(mv[:, m, :], stats[:, m, :])
            link(last)
            ts(col(8, 8), mv[:, :, 1], EPS, None, ALU.add).then_inc(sem("gn_var"), 1)
            dve.wait_ge(sem("gn_rstd"), 1)
            for t in range(TT):
                for h in range(HEADS1):
                    m = 4 * t + h
                    last = ts(ret[:, t, h * P:(h + 1) * P], ps[:, t, h * P:(h + 1) * P], mv[:, m, 0:1], col(8 + m),
                              ALU.subtract, ALU.mult)
            link(last)
            dve.wait_ge(sem("g_ready"), 1)
            for t in range(TT):
                tt(ret[:, t, :], ret[:, t, :], g_tok[:, t, :], ALU.mult).then_inc(sem("ret_ready"), 1)
            dense_wait(dve, "w_in", 6)
            dve.wait_ge(sem("gc_ready"), 1)
            dve.wait_ge(sem("pads_ready"), 1)
            for f in range(4):
                last = tt(gcu[:, f, 2:], gc_s[:, f, :], ps[:, 4 + f // 2, (f % 2) * 256:(f % 2) * 256 + 256], ALU.mult)
            link(last)
            for f in range(4):
                last = ts(conv_a[:, f, :], gcu[:, f, 0:256], vec("conv", f), None, ALU.mult)
            link(last)
            for tap in (1, 2):
                for f in range(4):
                    last = stt_(conv_a[:, f, :], gcu[:, f, tap:tap + 256], vec("conv", 4 * tap + f), conv_a[:, f, :],
                                ALU.mult, ALU.add)
                link(last)
            dve.wait_ge(sem("gb_ready"), 1)
            dve.wait_ge(sem("qkT_ready"), 2)
            for f in range(4):
                tt(mixT[:, 4 + f, :], conv_a[:, f, :], gb_s[:, f, :], ALU.mult).then_inc(sem("mix_conv_ready"), 1)
            dense_wait(dve, "w_o", 1)
            for t in range(TT):
                xv = x1[:, t, :].rearrange("p (a b) -> p a b", b=512)
                tt(xv, xv, ps[:, 4 + 2 * t:6 + 2 * t, :], ALU.add).then_inc(sem("x1_ready"), 1)

            token_norm("norm2", x1, xn)
            dve.wait_ge(sem("router_done"), 1)
            dve.wait_ge(sem("router_loaded"), 48)
            L = logits
            for t in range(TT):
                last = tt(L[:, t, :], ps[:, 4, t * 72:t * 72 + 72], router_b, ALU.add)
            link(last)

            def softmax_in(j, src):
                o = 40 * j
                for t in range(TT):
                    last = nc.vector.max(rt[:, t, o:o + 8], src(t))
                link(last)
                for t in range(TT):
                    last = ts(rt[:, t, o + 8:o + 16], src(t), rt[:, t, o:o + 1], None, ALU.subtract)
                last.then_inc(sem("softmax_in"), 1)

            def softmax_top(j):
                o = 40 * j
                dve.wait_ge(sem("softmax_exp"), j + 1)
                for t in range(TT):
                    last = nc.vector.reciprocal(rt[:, t, o + 37:o + 38], rt[:, t, o + 36:o + 37])
                link(last)
                for t in range(TT):
                    last = ts(rt[:, t, o + 8:o + 16], rt[:, t, o + 8:o + 16], rt[:, t, o + 37:o + 38], None, ALU.mult)
                link(last)
                for t in range(TT):
                    last = nc.vector.max(rt[:, t, o + 16:o + 24], rt[:, t, o + 8:o + 16])
                link(last)
                for t in range(TT):
                    last = nc.vector.max_index(rt[:, t, o + 24:o + 32].bitcast(u32), rt[:, t, o + 16:o + 24],
                                               rt[:, t, o + 8:o + 16])
                link(last)
                for t in range(TT):
                    last = nc.vector.tensor_copy(rt[:, t, o + 32:o + 34], rt[:, t, o + 24:o + 26].bitcast(u32))
                link(last)

            softmax_in(0, lambda t: L[:, t, 0:8])
            softmax_top(0)
            for t in range(TT):
                last = ts(rt[:, t, 80:88], iota[:, 0:8], rt[:, t, 32:33], None, ALU.is_equal)
            link(last)
            for t in range(TT):
                last = tt(rt[:, t, 96:160].rearrange("p (e g) -> p e g", g=8),
                          L[:, t, 8:72].rearrange("p (g e) -> p e g", g=8),
                          rt[:, t, 80:88].unsqueeze(1).to_broadcast([P, 8, 8]), ALU.mult)
            link(last)
            for t in range(TT):
                last = nc.vector.reduce_sum(rt[:, t, 88:96], rt[:, t, 96:160].rearrange("p (e g) -> p e g", g=8), axis=X)
            link(last)
            softmax_in(1, lambda t: rt[:, t, 88:96])
            softmax_top(1)
            for t in range(TT):
                last = stt_(rt[:, t, 80:82], rt[:, t, 32:33].to_broadcast([P, 2]), 8.0, rt[:, t, 72:74], ALU.mult, ALU.add)
            link(last)
            for t in range(TT):
                last = tt(rt[:, t, 84:85], rt[:, t, 56:57], rt[:, t, 57:58], ALU.add)
            link(last)
            for t in range(TT):
                last = nc.vector.reciprocal(rt[:, t, 84:85], rt[:, t, 84:85])
            link(last)
            for t in range(TT):
                last = ts(rt[:, t, 82:84], rt[:, t, 56:58], rt[:, t, 84:85], rt[:, t, 16:17], ALU.mult, ALU.mult)
            link(last)
            for j in range(2):
                for t in range(TT):
                    last = ts(onehot[:, j, t, :], iota[:, 0:EXPERTS], rt[:, t, 80 + j:81 + j], None, ALU.is_equal)
            link(last)
            tt(assigned, onehot[:, 0], onehot[:, 1], ALU.add).then_inc(sem("assigned_ready"), 1)
            dve.wait_ge(sem("counted"), 1)
            link(nc.vector.tensor_copy(count, ps[:, 5, 0:192].rearrange("p (a b) -> p a b", b=EXPERTS)))
            link(ts(place[:, 0, :], count[:, 2, :], 0.0, 1.0, ALU.mult, ALU.add))
            link(nc.vector.tensor_tensor_scan(place[:, 1, :], place[:, 0, :], count[:, 2, :], 0.0, ALU.mult, ALU.add))
            link(tt(place[:, 1, :], place[:, 1, :], count[:, 2, :], ALU.subtract))
            for r in range(ROUNDS):
                ts(starts[0:1, r, :], place[0:1, 1, :], float(WIN * r), float(SLOTS), ALU.add, ALU.min)
            link(nc.vector.reduce_max(col(20), count[:, 2, :], axis=X))
            ts(many[0:1, 0:1], col(20)[0:1, :], float(WIN), None, ALU.is_gt).then_inc(sem("starts_ready"), 1)
            for t in range(TT):
                last = tt(count[:, t, :], count[:, t, :], place[:, 1, :], ALU.add)
            link(last)
            for j in range(2):
                for t in range(TT):
                    last = tt(onehot[:, j, t, :], onehot[:, j, t, :], count[:, t, :], ALU.mult)
            link(last)
            link(nc.vector.reduce_sum(col(24, 4), onehot.rearrange("p j t e -> p (j t) e"), axis=X))
            for t in range(TT):
                last = ts(sel[:, t, :], iota, col(24 + t), None, ALU.is_equal)
            link(last)
            for t in range(TT):
                last = stt_(sel[:, t, :], iota, col(26 + t), sel[:, t, :], ALU.is_equal, ALU.add)
            last.then_inc(sem("sel_ready"), 1)
            for t in range(TT):
                last = ts(gated[:, t, :], iota, col(24 + t), rt[:, t, 82:83], ALU.is_equal, ALU.mult)
            link(last)
            for t in range(TT):
                last = ts(h2T.rearrange("p a b -> p (a b)")[:, t * 512:(t + 1) * 512], iota, col(26 + t),
                          rt[:, t, 83:84], ALU.is_equal, ALU.mult)
            link(last)
            for t in range(TT):
                last = tt(gated[:, t, :], gated[:, t, :], h2T.rearrange("p a b -> p (a b)")[:, t * 512:(t + 1) * 512],
                          ALU.add)
            last.then_inc(sem("gated_ready"), 1)

            def multiply(u):
                tt(hidden[:, u].rearrange("p a b -> p (a b)"), silu_g[:, u].rearrange("p a b -> p (a b)"),
                   ps[:, 2 + u, 0:256], ALU.mult).then_inc(sem("hidden_ready"), 1)

            def dve_fast(e0, e1):
                def one(u, it, first=False):
                    e = it * 2 + (e0 + u)
                    dve.wait_ge(sem("silu_ready"), e + 1)
                    dve.wait_ge(sem("up_used"), e + 1)
                    if not first:
                        dve.wait_ge(sem("down_used"), e - 1)
                    multiply(u)

                for u in range(2):
                    one(u, 0, e0 == 0)
                with dve.Fori(1, (e1 - e0) // 2) as it:
                    for u in range(2):
                        one(u, it)

            def dve_slow(e0, e1):
                def expert(u, it, first=False):
                    e = it * 2 + (e0 + u)
                    for r in range(ROUNDS):
                        dve.wait_ge(sem("silu_ready"), e * ROUNDS + r + 1)
                        if not (first and u == 0 and r == 0):
                            dve.wait_ge(sem("y_written"), e * ROUNDS + r)
                        multiply(u)

                for u in range(2):
                    expert(u, 0, e0 == 0)
                with dve.Fori(1, (e1 - e0) // 2) as it:
                    for u in range(2):
                        expert(u, it)

            def moe(e0, e1):
                flag = dve.value_load(many[0:1, 0:1], min_val=0, max_val=1)
                with dve.If(flag < 1):
                    dve_fast(e0, e1)
                with dve.Else():
                    dve_slow(e0, e1)

            lbv = vecs[:, VEC["lb"]:VEC["lb"] + 32].rearrange("p (l n) -> p l n", l=2)
            link(tt(small[:, 32:48], lbv[:, 0, :], lbv[:, 1, :], ALU.max))
            for l in range(2):
                last = tt(lbv[:, l, :], lbv[:, l, :], small[:, 32:48], ALU.subtract)
            last.then_inc(sem("lb_in"), 1)
            dve.wait_ge(sem("starts_ready"), 1)
            moe(*MOE_RANGES[0])

            dve.wait_ge(sem("lb_exp"), 1)
            link(tt(small[:, 32:48], lbv[:, 0, :], lbv[:, 1, :], ALU.add))
            link(nc.vector.reciprocal(small[:, 32:48], small[:, 32:48]))
            lbf = lbs[:, 0].rearrange("p a b -> p (a b)")
            link(tt(lbf, lbv[:, 0, :], small[:, 32:48], ALU.mult))
            link(ts(lbs[:, 1].rearrange("p a b -> p (a b)"), lbf, -1.0, 1.0, ALU.mult, ALU.add))
            token_norm("normc", c_raw, c_raw)
            dense_wait(dve, "ada", 11)
            for j in range(2):
                last = tt(mod[:, :, j], ps[:, 6, 0:96].rearrange("p (a b) -> p a b", b=2)[:, :, j], vec("b_ada", 0, 48),
                          ALU.add)
            link(last)
            for row, (chunk, who, gain) in enumerate(((8, 1, 0), (8, 0, 0), (32, 0, 8))):
                last = stt_(scales[:, row, :], mod[:, chunk:chunk + 8, who], 1.0, vec("norm_g", gain, 8), ALU.add,
                            ALU.mult)
            last.then_inc(sem("mod_ready"), 1)
            dve.wait_ge(sem("zeros_ready"), 1)
            for g in range(NG):
                for d in range(2):
                    m = 2 * g + d
                    dve.wait_ge(sem("ctx_f_read"), m + 1)
                    for h in range(GH):
                        last = ts(c_f[:, h, :], c_f[:, h, :], lbs[:, 1, d, GH * g + h:GH * g + h + 1],
                                  lbs[:, 0, d, GH * g + h:GH * g + h + 1], ALU.mult, ALU.add)
                    link(last)
                    if g:
                        dve.wait_ge(sem("ctx_kd_transposed"), GH * g)
                    for h in range(GH):
                        if d == 0:
                            nc.vector.memset(c_p[:, d, h, TOKENS - 1:TOKENS], 1.0)
                            last = nc.vector.tensor_tensor_scan(c_p[:, d, h, TOKENS - 2::-1], c_f[:, h, TOKENS - 1:0:-1],
                                                                zeros[:, 0:TOKENS - 1], 1.0, ALU.mult, ALU.add)
                        else:
                            nc.vector.memset(c_p[:, d, h, 0:1], 1.0)
                            last = nc.vector.tensor_tensor_scan(c_p[:, d, h, 1:TOKENS], c_f[:, h, 0:TOKENS - 1],
                                                                zeros[:, 0:TOKENS - 1], 1.0, ALU.mult, ALU.add)
                    link(last)
                    cf = c_f.rearrange("p a b -> p (a b)")
                    cp = c_p[:, d].rearrange("p a b -> p (a b)")
                    link(ts(cf, cf, -1.0, 1.0, ALU.mult, ALU.add))
                    tt(cp, cp, cf, ALU.mult).then_inc(sem("ctx_kd_ready"), 1)
            moe(*MOE_RANGES[1])

            def mean(name, bank, width, n=1):
                dve.wait_ge(sem(name + "_summed"), n)
                ts(o_n[:, :], ps[:, bank, 0:256] if name != "o" else ps[:, 4, 256:512], 1.0 / width, EPS, ALU.mult,
                   ALU.add).then_inc(sem(name + "_mean"), 1)
                dve.wait_ge(sem(name + "_rstd"), n)

            dve.wait_ge(sem("combined"), 1)
            nc.vector.tensor_copy(hl.rearrange("p (b f) n -> p b (f n)", b=4), ps[:, 4:8, :]).then_inc(
                sem("normf_in"), 1)
            mean("normf", 0, D)
            for k in range(KD):
                last = stt_(lat[:, k, :], hl[:, k, :], vec("final1", k), ps[:, 0, 256:512], ALU.mult, ALU.mult)
            last.then_inc(sem("norml_in"), 1)
            mean("norml", 1, D)
            for k in range(KD):
                last = stt_(hl[:, k, :], lat[:, k, :], scales[:, 1, k:k + 1], ps[:, 1, 256:512], ALU.mult, ALU.mult)
            last.then_inc(sem("hl_scaled"), 1)

            dve.wait_ge(sem("smask_ready"), 1)
            dve.wait_ge(sem("hmask_loaded"), 16)
            dve.wait_ge(sem("masked_zeroed"), 1)
            chunks = lambda v: v.rearrange("p (c n) -> p c n", n=CHUNK2)
            wide = lambda v: v.unsqueeze(2).to_broadcast([P, GH * NCH, CHUNK2])
            qf = q_s.rearrange("p a b -> p (a b)")
            for g in range(NG):
                for d in range(2):
                    m = 2 * g + d
                    buf = lf if d == 0 else dd
                    dve.wait_ge(sem("lat_read"), 5 * g + d + 1)
                    for h in range(GH):
                        last = ts(buf[:, h * TOKENS:(h + 1) * TOKENS], buf[:, h * TOKENS:(h + 1) * TOKENS],
                                  lbs[:, 1, d, GH * g + h:GH * g + h + 1], lbs[:, 0, d, GH * g + h:GH * g + h + 1],
                                  ALU.mult, ALU.add)
                    link(last)
                    ts(kk, buf, -1.0, 1.0, ALU.mult, ALU.add).then_inc(sem("f_ready"), 1)
                    dve.wait_ge(sem("logf_ready"), m + 1)
                    if m:
                        dve.wait_ge(sem("dec_ready"), m)
                    if d == 0:
                        nc.vector.tensor_tensor_scan(b_s, smask, buf, 0.0, ALU.mult, ALU.add).then_inc(sem("b_ready"), 1)
                    else:
                        link(nc.vector.tensor_tensor_scan(lf, smask, buf, 0.0, ALU.mult, ALU.add))
                        link(tt(buf, buf, lf, ALU.subtract))
                        tt(chunks(b_s), chunks(buf), wide(chunks(lf)[:, :, CHUNK2 - 1]), ALU.add).then_inc(
                            sem("b_ready"), 1)
                    dve.wait_ge(sem("b_ready"), m + 1)
                    if g:
                        dve.wait_ge(sem("o_done"), GH * g)
                    ref, end = (CHUNK2 // 2, CHUNK2 - 1) if d == 0 else (CHUNK2 - 1 - CHUNK2 // 2, 0)
                    tt(chunks(prod[:, d, 1, :]), chunks(b_s), wide(chunks(b_s)[:, :, ref]), ALU.subtract).then_inc(
                        sem("bref_ready"), 1)
                    tt(chunks(prod[:, d, 3, :]), wide(chunks(b_s)[:, :, end]), chunks(b_s), ALU.subtract).then_inc(
                        sem("blast_ready"), 1)
                    dve.wait_ge(sem("lat_read"), 5 * g + 4)
                    dve.wait_ge(sem("eb_ready"), m + 1)
                    tt(prod[:, d, 2, :], prod[:, d, 2, :], qf, ALU.mult)
                    dve.wait_ge(sem("eq_ready"), m + 1)
                    tt(prod[:, d, 0, :], prod[:, d, 0, :], qf, ALU.mult)
                    dve.wait_ge(sem("ek_ready"), m + 1)
                    tt(prod[:, d, 1, :], prod[:, d, 1, :], kk, ALU.mult)
                    dve.wait_ge(sem("el_ready"), m + 1)
                    tt(prod[:, d, 3, :], prod[:, d, 3, :], kk, ALU.mult).then_inc(sem("prod_ready"), 1)
                    dve.wait_ge(sem("prod_ready"), m + 1)
                    dve.wait_ge(sem("dec_ready"), m + 1)
                for h in range(GH):
                    n = GH * g + h
                    dve.wait_ge(sem("s_done"), n + 1)
                    if n:
                        dve.wait_ge(sem("o_done"), n)
                    for d in range(2):
                        for quarter in range(4):
                            HC = CHUNK2 // 2
                            lo, late = quarter * HC, quarter % 2 != d
                            q0, qn = ((quarter % 2) * HC, HC) if late else (0, CHUNK2)
                            to = (quarter // 2) * CHUNK2 + q0
                            last = nc.vector.copy_predicated(
                                masked[lo:lo + HC, d, :, to:to + qn],
                                hmask[lo:lo + HC, d, q0:q0 + qn].unsqueeze(1).to_broadcast([HC, TT, qn]),
                                ps[lo:lo + HC, 4, 0:256].rearrange("p (t d n) -> p t d n", t=TT, d=2)[:, :, d, q0:q0 + qn])
                    last.then_inc(sem("masked_ready"), 1)
                    for d in range(2):
                        dve.wait_ge(sem("kv_done"), n + 1)
                        for j in range(1, NCH):
                            c = j - 1 if d == 0 else NCH - j
                            prev = state[:, n, d, :] if j == 1 else chunk_state[:, d, j - 1, :]
                            last = stt_(chunk_state[:, d, j, :], prev, dec[:, d, h * NCH + c:h * NCH + c + 1],
                                        kv_bank(d, c), ALU.mult, ALU.add)
                            if j < NCH - 1:
                                link(last)
                        last.then_inc(sem("states_ready"), 1)
                    mean("o", 4, P, n + 1)
                    link(tt(o_sq[:, :], g_s[:, h, :], ps[:, 6, 256:512], ALU.mult))
                    stt_(attn[:, n, :], ps[:, 5, 0:256], vec("gnorm"), o_sq[:, :], ALU.mult, ALU.mult).then_inc(
                        sem("readout_done"), 1)
            for i in range(2):
                dense_wait(dve, "hg_out", i)
                for f in range(4):
                    k = 4 * i + f
                    last = stt_(lat[:, k, :], ps[:, 2 * i + f // 2, (f % 2) * 256:(f % 2) * 256 + 256], mod[:, 16 + k, 0:1],
                                lat[:, k, :], ALU.mult, ALU.add)
            last.then_inc(sem("norm3_in"), 1)
            mean("norm3", 4, D)
            for k in range(KD):
                last = stt_(hl[:, k, :], lat[:, k, :], scales[:, 2, k:k + 1], ps[:, 5, 256:512], ALU.mult, ALU.mult)
            last.then_inc(sem("hl_scaled"), 1)

            for b in range(NB):
                for part in range(2):
                    i = part * NB + b
                    dve.wait_ge(sem("conv_begun"), 2 * b + part + 1)
                    p_in, acc = ps[:, (2 * b + part) % 4, 0:256], up_s[:, b % 2, part, :]
                    link(stt_(acc[:, 1:], p_in[:, 0:255], vec("ffn_w", i), acc[:, 1:], ALU.mult, ALU.add))
                    stt_(acc[:, 0:255], p_in[:, 1:], vec("ffn_w", 4 * NB + i), acc[:, 0:255], ALU.mult,
                         ALU.add).then_inc(sem("conv_read"), 1)
                dve.wait_ge(sem("conv_read"), 2 * b + 2)
                dve.wait_ge(sem("ffn_silu"), b + 1)
                tt(act[:, b, :], sg_s[:, b % 2, :], up_s[:, b % 2, 1, :], ALU.mult).then_inc(sem("act_ready"), 1)
            for half in range(2):
                dense_wait(dve, "ffn_down", 3 * half + 2)
                for f in range(4):
                    k = 4 * half + f
                    last = stt_(lat[:, k, :], ps[:, 4 - 4 * half + f, 0:256], mod[:, 40 + k, 0:1], lat[:, k, :], ALU.mult,
                                ALU.add)
                last.then_inc(sem("last_residual"), 1)
            dve.wait_ge(sem("last_residual"), 2)
            dve.nop().then_inc(sem("norm4_in"), 1)
            mean("norm4", 0, D)
            for k in range(KD):
                stt_(hl[:, k, :], lat[:, k, :], vec("final2", k), ps[:, 1, 256:512], ALU.mult, ALU.mult).then_inc(
                    sem("final_scaled"), 1)


def constants():
    t = np.arange(TOKENS, dtype=np.float32)
    half = 64
    inv = (10000.0 ** (-np.arange(half, dtype=np.float32) / half)).astype(np.float32)
    ang = t[:, None] * inv[None, :]
    cos, sin = np.cos(ang).astype(np.float32), np.sin(ang).astype(np.float32)
    rope = np.stack([np.concatenate([cos, cos], 1), np.concatenate([-sin, sin], 1)])
    rope = rope.reshape(2, TT, P, P).transpose(2, 0, 1, 3)
    log_g = np.log1p(-(2.0 ** (-5.0 - np.arange(HEADS1))))
    rel = np.arange(TOKENS)[None, :] - np.arange(P)[:, None]
    decay = np.where(rel[:, None] >= 0, np.exp(log_g[None, :, None] * np.maximum(rel, 0)[:, None]), 0.0) * 128 ** -0.5
    p = np.arange(P)
    consts = np.stack([np.eye(P), np.ones((P, P)), p[:, None] < p[None, :]], 1)
    j, i = p[:, None] % CHUNK2, np.arange(CHUNK2)[None, :]
    hmask = np.stack([j <= i, j >= i], 1)
    iota = np.broadcast_to(np.arange(SLOTS), (P, SLOTS))
    f = lambda v, dt=np.float32: np.ascontiguousarray(v).astype(dt)
    return {"rope": f(rope), "decay": f(decay), "consts": f(consts), "hmask": f(hmask, np.int32), "iota": f(iota)}


def kernel(**inputs):
    import concourse.bacc as bacc
    from concourse.bass_utils import run_bass_kernel_spmd as run

    g = {k: np.asarray(v) for k, v in inputs.items()}
    tok = lambda v: np.ascontiguousarray(v.reshape(TT, P, D).transpose(1, 0, 2))
    blk = lambda v: v.reshape(-1, P).T
    packed = {"norm1": blk(g["norm1_w"]), "ret_gn": blk(g["ret_gn_w"]), "conv": blk(g["conv_w"]),
              "norm2": g["norm2_w"].reshape(P, KD), "final1": blk(g["final_norm_w"]), "norm_g": blk(g["norm_g_2"]),
              "final2": blk(g["final_g_2"]), "lb": blk(g["hg_lb_logits_2"]), "gnorm": blk(g["hg_gnorm_2"]),
              "b_ada": blk(g["b_ada_2"]), "ffn_w": blk(g["ffn_conv_w_2"]), "ffn_b": blk(g["ffn_conv_b_2"]),
              "c": blk(g["c_2"]), "c_ctx": blk(g["c_ctx_2"])}
    taps = g["ffn_conv_w_2"].reshape(3, 2 * DFF)
    packed["ffn_w"] = blk(np.ascontiguousarray(taps[[0, 1, 2]]))
    router = np.concatenate([g["router_g_w"][0], g["router_e_w"][0].transpose(1, 0, 2).reshape(D, 64)], 1)
    bias = np.concatenate([g["router_g_b"].reshape(1, 8), g["router_e_b"].reshape(1, 64)], 1)
    arrays = {
        "x": tok(g["x"]), "ctx": tok(g["ctx_2"]),
        "vecs": np.ascontiguousarray(np.concatenate([packed[n] for n in VEC], 1)),
        "router_w": np.ascontiguousarray(router.reshape(P, KD, 72)),
        "router_b": np.ascontiguousarray(np.repeat(bias, P, 0)),
        "w_in": g["w_in"][0], "w_o": g["w_o"][0], "w_gate": g["w_gate"][0], "w_up": g["w_up"][0],
        "w_down": g["w_down"][0], "w_ada": g["w_ada_2"][0], "hg_in": g["hg_w_in_2"][0], "hg_out": g["hg_w_out_2"][0],
        "ffn_up": g["ffn_w_up_2"][0], "ffn_down": g["ffn_w_down_2"][0],
        **constants(),
    }
    nc = bacc.Bacc("TRN2", target_bir_lowering=False, num_devices=1)
    sent, a = {}, {}
    for name, v in arrays.items():
        v = np.ascontiguousarray(v)
        sent["in_" + name] = v
        a[name] = nc.dram_tensor("in_" + name, v.shape, mybir.dt.from_np(v.dtype), kind="ExternalInput").ap()
    out = nc.dram_tensor("out_0", (1, TOKENS, D), mybir.dt.float32, kind="ExternalOutput").ap()
    program(nc, a, out)
    return run(nc, [sent], core_ids=[0]).results[0]["out_0"]
```

```python
import numpy as np
import concourse.bass as bass
from concourse import mybir
from contextlib import ExitStack

P = 128
TOKENS = 256
TT = TOKENS // P
D = 1024
KD = D // P
EPS = 1e-6
HEADS1 = 4
EXPERTS = 64
FF = 512
KF = FF // P
SLOTS = TOKENS * 2
WIN = 32
COLS = SLOTS + WIN
ROUNDS = TOKENS // WIN
HEADS2 = 8
CHUNK2 = 64
NCH = TOKENS // CHUNK2
GH = 4
NG = HEADS2 // GH
DFF = 2816
NB = DFF // P
RING = 6
SLOT = 4096

VEC = {}
_at = 0
for _name, _n in (("norm1", 8), ("ret_gn", 4), ("conv", 12), ("norm2", 8), ("final1", 8), ("norm_g", 16),
                  ("final2", 8), ("lb", 32), ("gnorm", 1), ("b_ada", 48), ("ffn_w", 3 * 2 * NB),
                  ("ffn_b", 2 * NB), ("c", 8), ("c_ctx", 8)):
    VEC[_name] = _at
    _at += _n
NVEC = _at

MOE_RANGES = [(0, 20), (20, 40), (40, 64)]
BETWEEN = [[("ctx", c) for c in range(3)], [("ctx", c) for c in range(3, 6)], []]


def tile_order():
    order = [("w_in", c) for c in range(7)] + [("w_o", c) for c in range(2)]
    order += [("ada", c) for c in range(12)]
    for r, (e0, e1) in enumerate(MOE_RANGES):
        for e in range(e0, e1):
            order += [("gate", e), ("up", e), ("down", e)]
        order += BETWEEN[r]
    order += [("lat", c) for c in range(10)] + [("hg_out", c) for c in range(2)]
    order += [("ffn_up", c) for c in range(12)] + [("ffn_down", c) for c in range(6)]
    return order


def program(nc, a, out):
    f32, i32, u32 = mybir.dt.float32, mybir.dt.int32, mybir.dt.uint32
    ALU, ACT, AX = mybir.AluOpType, mybir.ActivationFunctionType, mybir.AxisListType
    X = AX.X
    ctx = ExitStack()
    with ctx:
        def sb(name, shape, dt=f32):
            return ctx.enter_context(nc.sbuf_tensor(name, shape, dt))

        sems = {}

        def sem(name):
            if name not in sems:
                sems[name] = ctx.enter_context(nc.semaphore(name))
            return sems[name]

        ring = sb("ring", [P, RING, SLOT])
        consts = sb("consts", [P, 5, P])
        ident, ones, before = consts[:, 0, :], consts[:, 1, :], consts[:, 2, :]
        fold_pairs, fold_all = consts[:, 3, :], consts[:, 4, :]
        vecs = sb("vecs", [P, NVEC])
        hmask = sb("hmask", [P, 2, CHUNK2], i32)
        mod = sb("mod", [P, 48, 2])
        scales = sb("scales", [P, 3, KD])
        lbs = sb("lbs", [P, 2, 2, HEADS2])
        small = sb("small", [P, 96])
        many = sb("many", [1, 1], i32)
        x1 = sb("x1", [P, TT, D])
        sgT = sb("sgT", [P, SLOTS // P, TOKENS])
        state = sb("state", [P, HEADS2, 2, P])
        arena = sb("arena", [P, 20480])

        used = {}

        def at(offset, *shape, dt=None):
            n = int(np.prod(shape))
            assert offset + n <= 20480, (offset, shape)
            v = arena[:, offset:offset + n]
            if len(shape) == 2:
                v = v.rearrange("p (a b) -> p a b", b=shape[1])
            if len(shape) == 3:
                v = v.rearrange("p (a b c) -> p a b c", b=shape[1], c=shape[2])
            return v

        xn = at(0, TT, D)
        hT = at(2048, KD, TOKENS)
        qk_rot = at(4096, 2, TT, 512)
        qkT = at(6144, 2, HEADS1, TOKENS)
        mixT = at(8192, KD, TOKENS)
        v_tok = at(10240, TT, 512)
        g_tok = at(11264, TT, 512)
        probs = at(12288, HEADS1, 384)
        gb_s = at(13824, 4, TOKENS)
        gc_s = at(14848, 4, TOKENS)
        gcu = at(15872, 4, TOKENS + 2)
        decay = at(16904, HEADS1, TOKENS)
        rope = at(17928, 2, TT, P)
        rot_a = at(18440, TT * 0 + 1, 512)[:, 0, :]
        rot_b = at(18952, 1, 512)[:, 0, :]
        ret = at(4096, TT, 512)
        conv_a = at(0, 4, TOKENS)
        stats = at(1024, 8, 6)
        mv = at(1100, 8, 2)
        h2T = at(2048, KD, TOKENS)
        router_w = at(4096, KD, 72)
        router_b = at(4672, 1, 72)[:, 0, :]
        iota = at(4744, 1, SLOTS)[:, 0, :]
        logits = at(5256, TT, 72)
        rt = at(5400, TT, 160)
        onehot = at(5720, 2, TT, EXPERTS)
        assigned = at(5976, TT, EXPERTS)
        place = at(6104, TT, EXPERTS)
        count = at(6232, 3, EXPERTS)
        sel = at(6424, TT, SLOTS)
        gated = at(7448, TT, SLOTS)
        starts = arena[:, 8472:8472 + ROUNDS * EXPERTS].bitcast(i32).rearrange("p (r e) -> p r e", e=EXPERTS)
        YT = at(8984, KD, COLS)
        XgT = at(13336, KD, COLS)
        win = at(17688, 2, KD, WIN)
        hidden = at(18200, 2, KF, WIN)
        silu_g = at(18456, KF, WIN)
        gu_s = at(18584, 1, 512)[:, 0, :]
        y_s = at(19096, 1, 512)[:, 0, :]
        ada_s = at(19608, 1, 512)[:, 0, :]
        csil = at(20120, KD, 32)
        c_raw = at(0, TT, D)
        hcT = at(2048, KD, TOKENS)
        c_f = at(4096, GH, TOKENS)
        c_p = at(5120, 2, GH, TOKENS)
        c_v = at(0, TT, 512)
        c_kT = at(1024, 2, TT, P)
        zeros = at(7168, 1, TOKENS)[:, 0, :]
        y_tok = at(13336, SLOTS // P, D)
        lat = at(0, KD, TOKENS)
        hl = at(2048, KD, TOKENS)
        sq = at(4096, KD, TOKENS)
        attn = at(4096, HEADS2, TOKENS)
        q_s = at(6144, GH, TOKENS)
        v_s = at(7168, TT, 512)
        g_s = at(8192, GH, TOKENS)
        prod = at(9216, 2, 4, GH * TOKENS)
        lf = at(17408, 1, GH * TOKENS)[:, 0, :]
        kk = at(18432, 1, GH * TOKENS)[:, 0, :]
        dd = at(19456, 1, GH * TOKENS)[:, 0, :]
        b_s = x1[:, 0, :]
        smask = x1[:, 1, :]
        stt = sgT[:, :, :].rearrange("p a b -> p (a b)")
        chunk_state = stt.rearrange("p (d c v) -> p d c v", d=2, c=4)
        kdT = sb("kdT", [P, 2, TT, P])
        masked = sb("masked", [P, 2, TT, P])
        o_sq = sb("o_sq", [P, TOKENS])
        o_n = sb("o_n", [P, TOKENS])
        dec = sb("dec", [P, 2, GH * NCH])
        up_s = at(4096, 2, 2, TOKENS)
        sg_s = at(5120, 2, TOKENS)
        act = at(8192, NB, TOKENS)
        o_tok = at(14000, TT, D)
        ps = ctx.enter_context(nc.psum_tensor("ps", [P, 8, 512], f32))

        def vec(name, i=0, n=1):
            return vecs[:, VEC[name] + i:VEC[name] + i + n]

        def col(i, n=1):
            return small[:, i:i + n]

        def kv_bank(d, c):
            i = {(0, 0): 0, (0, 2): 1, (1, 2): 2, (0, 1): 0, (1, 3): 1, (1, 1): 2}[d, c]
            return ps[:, 6 + c % 2, i * P:(i + 1) * P]

        order = tile_order()
        number = {t: n for n, t in enumerate(order)}

        def source(kind, i):
            def cols(w, c, rows=KD, width=512):
                return w[:, c:c + width].rearrange("(k p) n -> p k n", p=P), (rows, width)
            if kind == "w_in":
                return cols(a["w_in"], 512 * i)
            if kind == "w_o":
                return a["w_o"][512 * i:512 * i + 512, :].rearrange("(k p) n -> p k n", p=P), (4, 1024)
            if kind in ("gate", "up"):
                return a["w_" + kind][i].rearrange("(p k) n -> p k n", k=KD), (KD, 512)
            if kind == "down":
                return a["w_down"][i].rearrange("(k p) n -> p k n", p=P), (KF, 1024)
            if kind == "ada":
                return cols(a["w_ada"], 512 * i)
            if kind == "ctx":
                return cols(a["hg_in"], (1024, 2048, 3072)[i % 3] + 512 * (i // 3))
            if kind == "lat":
                return cols(a["hg_in"], (1024, 2048, 3072, 0, 4096)[i % 5] + 512 * (i // 5))
            if kind == "hg_out":
                return cols(a["hg_out"], 512 * i)
            if kind == "ffn_up":
                b, part = i // 2, i % 2
                return cols(a["ffn_up"], DFF * part + 512 * b, KD, min(512, DFF - 512 * b))
            half, part = i // 3, i % 3
            k0, kn = (0, 8, 16)[part], (8, 8, 6)[part]
            return (a["ffn_down"][P * k0:P * (k0 + kn), 512 * half:512 * half + 512]
                    .rearrange("(k p) n -> p k n", p=P)), (kn, 512)

        def slot(kind, i):
            k, w = source(kind, i if isinstance(i, int) else 0)[1]
            return ring[:, number[kind, i] % RING, 0:k * w].rearrange("p (k n) -> p k n", n=w)

        def full(kind, i):
            n = number[kind, i]
            return sem(f"tile_loaded_{n % RING}"), 16 * (n // RING + 1)

        dense_index = {}
        for t in order:
            if t[0] not in ("gate", "up", "down"):
                dense_index[t] = len(dense_index) + 1

        def freed(n):
            kind, i = order[n]
            if kind in ("gate", "up", "down"):
                return sem(kind + "_used"), i + 1
            return sem("dense_used"), dense_index[order[n]]

        def dense_wait(eng, kind, i):
            eng.wait_ge(sem("dense_used"), dense_index[kind, i])

        def wait(eng, name, value):
            if not isinstance(value, int) or value > 0:
                eng.wait_ge(sem(name), value)

        block = ctx.enter_context(nc.Block())

        @block.sync
        def _(sp):
            def load(n):
                kind, i = order[n]
                src, (k, w) = source(kind, i)
                if n >= RING:
                    sp.wait_ge(*freed(n - RING))
                sp.dma_start(slot(kind, i), src).then_inc(sem(f"tile_loaded_{n % RING}"), 16)

            n = 0
            while n < len(order):
                kind, i = order[n]
                if kind != "gate":
                    load(n)
                    n += 1
                    continue
                e0, e1 = next(r for r in MOE_RANGES if r[0] == i)
                for m in range(n, n + RING):
                    load(m)
                with sp.Fori(1, (e1 - e0) // 2) as it:
                    for u in range(2):
                        for j, what in enumerate(("gate", "up", "down")):
                            src = a["w_" + what].rearrange(
                                "e (k p) n -> e p k n" if what == "down" else "e (p k) n -> e p k n", p=P)
                            m = n + 3 * u + j
                            sp.wait_ge(sem(what + "_used"), it * 2 + (e0 + u - 1))
                            sp.dma_start(slot(what, e0 + u), src[it * 2 + (e0 + u)]).then_inc(
                                sem(f"tile_loaded_{m % RING}"), 16)
                n += 3 * (e1 - e0)
            for t in range(TT):
                sp.wait_ge(sem("out_ready"), t + 1)
                sp.dma_start(out[0, t * P:(t + 1) * P, :], o_tok[:, t, :]).then_inc(sem("out_stored"), 16)
            sp.wait_ge(sem("out_stored"), 16 * TT)

        @block.tensor
        def _(pe):
            mm, tr = nc.tensor.matmul, nc.tensor.transpose

            def tile(kind, i):
                pe.wait_ge(*full(kind, i))
                return slot(kind, i)

            def release(ins, kind, i):
                ins.then_inc(sem("dense_used"), 1)

            def feature_major(w, acts, bank, blocks=4):
                for f in range(blocks):
                    for k in range(KD):
                        last = mm(ps[:, bank + f // 2, (f % 2) * 256:(f % 2) * 256 + 256],
                                  w[:, k, f * P:(f + 1) * P], acts[:, k, :], start=k == 0, stop=k == KD - 1)
                return last

            def token_major(w, acts, bank):
                for t in range(TT):
                    for k in range(KD):
                        last = mm(ps[:, bank + t, :], acts[:, k, t * P:(t + 1) * P], w[:, k, :],
                                  start=k == 0, stop=k == KD - 1)
                return last

            def transposed(src, bank, strided=False):
                for k in range(KD):
                    for t in range(TT):
                        piece = src[:, t, k::KD] if strided else src[:, t, k * P:(k + 1) * P]
                        o = (k % 2) * 256 + t * P
                        last = tr(ps[:, bank + k // 2, o:o + P], piece, ident)
                return last

            pe.wait_ge(sem("consts_loaded"), 16)
            pe.wait_ge(sem("norm1_scaled"), TT)
            transposed(xn, 0).then_inc(sem("h1_transposed"), 1)
            pe.wait_ge(sem("h1_ready"), KD)
            release(token_major(tile("w_in", 0), hT, 4), "w_in", 0)
            release(token_major(tile("w_in", 1), hT, 6), "w_in", 1)
            pe.wait_ge(sem("qk_rotated"), 1)
            release(token_major(tile("w_in", 2), hT, 4), "w_in", 2)
            for h in range(HEADS1):
                for t in range(TT):
                    last = tr(ps[:, h // 2, (h % 2) * 256 + t * P:(h % 2) * 256 + t * P + P],
                              qk_rot[:, 0, t, h * P:(h + 1) * P], ident)
            last.then_inc(sem("qk_transposed"), 1)
            pe.wait_ge(sem("qk_rotated"), 2)
            for h in range(HEADS1):
                for t in range(TT):
                    last = tr(ps[:, 2 + h // 2, (h % 2) * 256 + t * P:(h % 2) * 256 + t * P + P],
                              qk_rot[:, 1, t, h * P:(h + 1) * P], ident)
            last.then_inc(sem("qk_transposed"), 1)
            release(token_major(tile("w_in", 3), hT, 6), "w_in", 3)
            pe.wait_ge(sem("qkT_ready"), 2)
            for h in range(HEADS1):
                mm(ps[:, h, 0:256], qkT[:, 1, h, 0:P], qkT[:, 0, h, :], start=True, stop=True)
                mm(ps[:, h, 256:384], qkT[:, 1, h, P:256], qkT[:, 0, h, P:256], start=True,
                   stop=True).then_inc(sem("scores_done"), 1)
            pe.wait_ge(sem("v_ready"), 1)
            release(feature_major(tile("w_in", 4), hT, 4), "w_in", 4)
            pe.wait_ge(sem("decayed"), HEADS1)
            for t in range(TT):
                for h in range(HEADS1):
                    o = ps[:, t, h * P:(h + 1) * P]
                    mm(o, probs[:, h, t * P:(t + 1) * P], v_tok[:, 0, h * P:(h + 1) * P], start=True, stop=t == 0)
                    if t == 1:
                        mm(o, probs[:, h, 256:384], v_tok[:, 1, h * P:(h + 1) * P], start=False, stop=True)
            pe.wait_ge(sem("g_ready"), 1)
            release(feature_major(tile("w_in", 5), hT, 6), "w_in", 5)
            pe.wait_ge(sem("gb_ready"), 1)
            release(feature_major(tile("w_in", 6), hT, 4), "w_in", 6)
            pe.wait_ge(sem("ret_ready"), TT)
            for f in range(4):
                for t in range(TT):
                    last = tr(ps[:, 2 + f // 2, (f % 2) * 256 + t * P:(f % 2) * 256 + t * P + P],
                              ret[:, t, f * P:(f + 1) * P], ident)
            last.then_inc(sem("ret_transposed"), 1)
            pe.wait_ge(sem("mix_ret_ready"), 4)
            pe.wait_ge(sem("mix_conv_ready"), 4)
            for i in range(2):
                w = tile("w_o", i)
                for t in range(TT):
                    for half in range(2):
                        for k in range(4):
                            last = mm(ps[:, 4 + 2 * t + half, :], mixT[:, 4 * i + k, t * P:(t + 1) * P],
                                      w[:, k, half * 512:half * 512 + 512], start=i + k == 0, stop=i == 1 and k == 3)
                release(last, "w_o", i)

            def ada(i):
                if i:
                    pe.wait_ge(sem("ada_copied"), i)
                    if i > 1:
                        pe.wait_ge(sem("mod_copied"), i - 1)
                    for f in range(4):
                        last = mm(ps[:, 7, f * P:(f + 1) * P], ada_s[:, f * P:(f + 1) * P], fold_all,
                                  start=True, stop=True)
                    last.then_inc(sem("ada_folded"), 1)
                if i == 12:
                    return
                w = tile("ada", i)
                for k in range(2):
                    for q in range(4):
                        last = mm(ps[32 * q:32 * q + 32, 6, :], csil[:, 2 * q + k, :], w[:, 2 * q + k, :],
                                  start=k == 0, stop=k == 1)
                release(last, "ada", i)

            pe.wait_ge(sem("x1_ready"), TT)
            pe.wait_ge(sem("csil_ready"), 1)
            ada(0)
            ada(1)
            pe.wait_ge(sem("norm2_scaled"), TT)
            transposed(xn, 0, strided=True).then_inc(sem("h2_transposed"), 1)
            ada(2)
            pe.wait_ge(sem("h2_ready"), KD)
            pe.wait_ge(sem("router_loaded"), 48)
            for t in range(TT):
                for k in range(KD):
                    last = mm(ps[:, 4, t * 72:t * 72 + 72], h2T[:, k, t * P:(t + 1) * P], router_w[:, k, :],
                              start=k == 0, stop=k == KD - 1)
            last.then_inc(sem("router_done"), 1)
            for i in (3, 4, 5, 6):
                ada(i)
            pe.wait_ge(sem("assigned_ready"), 1)
            mm(ps[:, 5, 0:64], before, assigned[:, 0, :], start=True, stop=True)
            mm(ps[:, 5, 64:128], ones, assigned[:, 0, :], start=True, stop=False)
            mm(ps[:, 5, 64:128], before, assigned[:, 1, :], start=False, stop=True)
            mm(ps[:, 5, 128:192], ones, assigned[:, 0, :], start=True, stop=False)
            mm(ps[:, 5, 128:192], ones, assigned[:, 1, :], start=False, stop=True).then_inc(sem("counted"), 1)
            for i in (7, 8, 9):
                ada(i)
            pe.wait_ge(sem("sel_ready"), 1)
            for k in range(KD):
                if k >= 4:
                    pe.wait_ge(sem("gathered"), k - 3)
                for t in range(TT):
                    last = mm(ps[:, k % 4, :], xn[:, t, k::KD], sel[:, t, :], start=t == 0, stop=t == TT - 1)
                last.then_inc(sem("gather_done"), 1)
            for i in (10, 11, 12):
                ada(i)
            pe.wait_ge(sem("gated_ready"), 1)
            for s in range(SLOTS // P):
                for t in range(TT):
                    last = tr(ps[:, 4 + s // 2, (s % 2) * 256 + t * P:(s % 2) * 256 + t * P + P],
                              gated[:, t, s * P:(s + 1) * P], ident)
            last.then_inc(sem("gated_transposed"), 1)
            pe.wait_ge(sem("gathered"), KD)

            def ring_tile(n, width):
                return ring[:, n % RING, :].rearrange("p (k n) -> p k n", n=width)

            def gate_up(u, n):
                gate, up = ring_tile(n, FF), ring_tile(n + 1, FF)
                for k in range(KD // 2):
                    for q, (w, kk) in enumerate(((gate, k), (gate, KD // 2 + k), (up, k), (up, KD // 2 + k))):
                        last = mm(ps[32 * q:32 * q + 32, 0, :], win[:, u, kk, :], w[:, kk, :],
                                  start=k == 0, stop=k == KD // 2 - 1)
                        if k == KD // 2 - 1 and q == 1:
                            last_gate = last
                return last_gate, last

            def down(u, n):
                w = ring_tile(n + 2, D)
                for k in range(KF // 2):
                    for q in range(4):
                        kk = KF // 2 * (q % 2) + k
                        last = mm(ps[32 * q:32 * q + 32, 2, :], hidden[:, u, kk, :],
                                  w[:, kk, (q // 2) * 512:(q // 2) * 512 + 512], start=k == 0, stop=k == KF // 2 - 1)
                return last

            def fold(src, bank, matrix=None):
                for f in range(4):
                    last = mm(ps[:, bank, f * P:(f + 1) * P], src[:, f * P:(f + 1) * P],
                              fold_pairs if matrix is None else matrix, start=True, stop=True)
                return last

            def loaded(n0, u, j, it):
                n = n0 + 3 * u + j
                return sem(f"tile_loaded_{n % RING}"), (it + n // RING + 1) * 16

            def pe_fast(e0, e1):
                n0 = number["gate", e0]

                def gate_up_of(u, it):
                    e = it * 2 + (e0 + u)
                    pe.wait_ge(*loaded(n0, u, 0, it))
                    pe.wait_ge(*loaded(n0, u, 1, it))
                    wait(pe, "win_ready", e + 1)
                    wait(pe, "gu_copied", e)
                    last_gate, last_up = gate_up(u, n0 + 3 * u)
                    last_gate.then_inc(sem("gate_used"), 1)
                    last_up.then_inc(sem("up_used"), 1)

                def fold_gate_up(u, it):
                    e = it * 2 + (e0 + u)
                    wait(pe, "gu_copied", e + 1)
                    wait(pe, "hidden_ready", e)
                    fold(gu_s, 1).then_inc(sem("gu_folded"), 1)

                def down_of(u, it):
                    e = it * 2 + (e0 + u)
                    pe.wait_ge(*loaded(n0, u, 2, it))
                    wait(pe, "hidden_ready", e + 1)
                    wait(pe, "y_copied", e)
                    down(u, n0 + 3 * u).then_inc(sem("down_used"), 1)

                def fold_down(u, it):
                    e = it * 2 + (e0 + u)
                    wait(pe, "y_copied", e + 1)
                    wait(pe, "y_written", e)
                    fold(y_s, 3).then_inc(sem("y_folded"), 1)

                def step(u, it, more=True):
                    after = (1, it) if u == 0 else (0, it + 1)
                    if more:
                        gate_up_of(*after)
                    down_of(u, it)
                    if more:
                        fold_gate_up(*after)
                    fold_down(u, it)

                gate_up_of(0, 0)
                fold_gate_up(0, 0)
                step(0, 0)
                step(1, 0)
                with pe.Fori(1, (e1 - e0) // 2 - 1) as it:
                    step(0, it)
                    step(1, it)
                step(0, (e1 - e0) // 2 - 1)
                step(1, (e1 - e0) // 2 - 1, more=False)

            def pe_slow(e0, e1):
                n0 = number["gate", e0]

                def expert(u, it):
                    for j in range(3):
                        pe.wait_ge(*loaded(n0, u, j, it))
                    for r in range(ROUNDS):
                        q = (it * 2 + (e0 + u)) * ROUNDS + r
                        wait(pe, "win_ready", q + 1)
                        wait(pe, "gu_copied", q)
                        last_gate, last_up = gate_up(u, n0 + 3 * u)
                        if r == ROUNDS - 1:
                            last_gate.then_inc(sem("gate_used"), 1)
                        last_up.then_inc(sem("up_used" if r == ROUNDS - 1 else "round_up"), 1)
                        wait(pe, "gu_copied", q + 1)
                        wait(pe, "hidden_ready", q)
                        fold(gu_s, 1).then_inc(sem("gu_folded"), 1)
                        wait(pe, "hidden_ready", q + 1)
                        wait(pe, "y_copied", q)
                        down(u, n0 + 3 * u).then_inc(sem("down_used" if r == ROUNDS - 1 else "round_down"), 1)
                        wait(pe, "y_copied", q + 1)
                        wait(pe, "y_written", q)
                        fold(y_s, 3).then_inc(sem("y_folded"), 1)

                for u in range(2):
                    expert(u, 0)
                with pe.Fori(1, (e1 - e0) // 2) as it:
                    for u in range(2):
                        expert(u, it)

            def moe(e0, e1):
                flag = pe.value_load(many[0:1, 0:1], min_val=0, max_val=1)
                with pe.If(flag < 1):
                    pe_fast(e0, e1)
                with pe.Else():
                    pe_slow(e0, e1)

            pe.wait_ge(sem("starts_ready"), 1)
            moe(*MOE_RANGES[0])

            pe.wait_ge(sem("normc_scaled"), TT)
            pe.wait_ge(sem("mod_copied"), 12)
            pe.wait_ge(sem("sgT_ready"), 1)
            transposed(c_raw, 4).then_inc(sem("hc_transposed"), 1)
            pe.wait_ge(sem("hc_ready"), KD)
            for g in range(NG):
                if g:
                    pe.wait_ge(sem("ctx_state_ready"), GH * g)
                release(feature_major(tile("ctx", 3 * g), hcT, 4), "ctx", 3 * g)
                release(feature_major(tile("ctx", 3 * g + 1), hcT, 6), "ctx", 3 * g + 1)
                pe.wait_ge(sem("ctx_f_read"), 2 * g + 1)
                release(token_major(tile("ctx", 3 * g + 2), hcT, 4), "ctx", 3 * g + 2)
                pe.wait_ge(sem("ctx_kd_ready"), 2 * (g + 1))
                pe.wait_ge(sem("ctx_v_ready"), g + 1)
                for h in range(GH):
                    if h or g:
                        pe.wait_ge(sem("ctx_state_ready"), GH * g + h)
                    for d in range(2):
                        for t in range(TT):
                            last = tr(ps[:, 4, (2 * d + t) * P:(2 * d + t + 1) * P],
                                      c_p[:, d, h, t * P:(t + 1) * P], ident)
                    last.then_inc(sem("ctx_kd_transposed"), 1)
                    pe.wait_ge(sem("ctx_kdT_ready"), GH * g + h + 1)
                    for d in range(2):
                        for t in range(TT):
                            last = mm(ps[:, 5, d * P:(d + 1) * P], c_kT[:, d, t, :], c_v[:, t, h * P:(h + 1) * P],
                                      start=t == 0, stop=t == 1)
                    last.then_inc(sem("ctx_state_done"), 1)
                moe(*MOE_RANGES[1 + g])

            pe.wait_ge(sem("y_complete"), 1)
            for s in range(SLOTS // P):
                if s >= 2:
                    pe.wait_ge(sem("y_tok_ready"), s - 1)
                for k in range(KD):
                    last = tr(ps[:, 2 * (s % 2) + k // 4, (k % 4) * P:(k % 4 + 1) * P],
                              YT[:, 2 * (k % 4) + k // 4, s * P:(s + 1) * P], ident)
                last.then_inc(sem("y_transposed"), 1)
            pe.wait_ge(sem("y_tok_ready"), SLOTS // P)
            pe.wait_ge(sem("ctx_state_ready"), HEADS2)
            for k in range(KD):
                o = ps[:, 4 + k // 2, (k % 2) * 256:(k % 2) * 256 + 256]
                for s in range(SLOTS // P):
                    mm(o, y_tok[:, s, k * P:(k + 1) * P], sgT[:, s, :], start=s == 0, stop=False)
                for t in range(TT):
                    last = mm(o[:, t * P:(t + 1) * P], x1[:, t, k * P:(k + 1) * P], ident, start=False, stop=t == 1)
            last.then_inc(sem("combined"), 1)

            def norm_sums(name, src, bank):
                pe.wait_ge(sem(name + "_squared"), 1)
                for k in range(KD):
                    last = mm(ps[:, bank, 0:TOKENS], ones, src[:, k, :], start=k == 0, stop=k == KD - 1)
                last.then_inc(sem(name + "_summed"), 1)

            norm_sums("normf", sq, 0)
            norm_sums("norml", sq, 1)
            pe.wait_ge(sem("hl_ready"), 1)

            def attend(g):
                for h in range(GH):
                    n = GH * g + h
                    if n:
                        pe.wait_ge(sem("readout_done"), n)
                    for d in range(2):
                        for c in range(NCH):
                            lo = (c % 2) * CHUNK2
                            k0, HC = h * TOKENS + c * CHUNK2, CHUNK2 // 2
                            for half in range(2):
                                o = ((c // 2) * 2 + d) * CHUNK2 + half * HC
                                m0, mn = (half * HC, HC) if half == d else (0, CHUNK2)
                                last = mm(ps[lo + m0:lo + m0 + mn, 4, o:o + HC],
                                          prod[:, d, 1, k0 + m0:k0 + m0 + mn],
                                          prod[:, d, 0, k0 + half * HC:k0 + (half + 1) * HC], start=True, stop=True)
                    last.then_inc(sem("s_done"), 1)
                    for d in range(2):
                        for t in range(TT):
                            last = tr(ps[:, 5, (2 * d + t) * P:(2 * d + t + 1) * P],
                                      prod[:, d, 3, h * TOKENS + t * P:h * TOKENS + (t + 1) * P], ident)
                    last.then_inc(sem("kd_transposed"), 1)
                    pe.wait_ge(sem("kdT_ready"), n + 1)
                    for d in range(2):
                        for j in range(NCH - 1):
                            c = j if d == 0 else NCH - 1 - j
                            lo = (c % 2) * CHUNK2
                            last = mm(kv_bank(d, c),
                                      kdT[lo:lo + CHUNK2, d, c // 2, :],
                                      v_s[lo:lo + CHUNK2, c // 2, h * P:(h + 1) * P], start=True, stop=True)
                    last.then_inc(sem("kv_done"), 1)
                    pe.wait_ge(sem("masked_ready"), n + 1)
                    o = ps[:, 5, 0:TOKENS]
                    for t in range(TT):
                        for d in range(2):
                            mm(o[:, t * P:(t + 1) * P], v_s[:, t, h * P:(h + 1) * P], masked[:, d, t, :],
                               start=d == 0 and t == 0, stop=False, skip_group_check=True)
                    pe.wait_ge(sem("states_ready"), 2 * (n + 1))
                    for d in range(2):
                        for j in range(NCH):
                            c = j if d == 0 else NCH - 1 - j
                            s = state[:, n, d, :] if j == 0 else chunk_state[:, d, j, :]
                            last = mm(o[:, c * CHUNK2:(c + 1) * CHUNK2], s,
                                      prod[:, d, 2, h * TOKENS + c * CHUNK2:h * TOKENS + (c + 1) * CHUNK2],
                                      start=False, stop=d == 1 and j == NCH - 1, skip_group_check=True)
                    last.then_inc(sem("o_done"), 1)
                    pe.wait_ge(sem("o_squared"), n + 1)
                    mm(ps[:, 4, 256:512], ones, o_sq[:, :], start=True, stop=True).then_inc(sem("o_summed"), 1)

            for g in range(NG):
                if g:
                    pe.wait_ge(sem("lat_read"), 5 * g - 1)
                release(feature_major(tile("lat", 5 * g), hl, 0), "lat", 5 * g)
                if g:
                    pe.wait_ge(sem("lat_read"), 5 * g)
                release(feature_major(tile("lat", 5 * g + 1), hl, 2), "lat", 5 * g + 1)
                pe.wait_ge(sem("lat_read"), 5 * g + 1)
                release(token_major(tile("lat", 5 * g + 2), hl, 0), "lat", 5 * g + 2)
                pe.wait_ge(sem("lat_read"), 5 * g + 2)
                release(feature_major(tile("lat", 5 * g + 3), hl, 2), "lat", 5 * g + 3)
                pe.wait_ge(sem("lat_read"), 5 * g + 3)
                release(feature_major(tile("lat", 5 * g + 4), hl, 0), "lat", 5 * g + 4)
                pe.wait_ge(sem("lat_read"), 5 * g + 5)
                pe.wait_ge(sem("prod_ready"), 2 * (g + 1))
                attend(g)
            pe.wait_ge(sem("readout_done"), HEADS2)
            for i in range(2):
                release(feature_major(tile("hg_out", i), attn, 2 * i), "hg_out", i)
            norm_sums("norm3", sq, 4)
            pe.wait_ge(sem("hl_ready"), 2)

            for b in range(NB):
                i, f = b // 4, b % 4
                for part in range(2):
                    w = tile("ffn_up", 2 * i + part) if f == 0 else slot("ffn_up", 2 * i + part)
                    m = 2 * b + part
                    if m >= 4:
                        pe.wait_ge(sem("conv_read"), m - 3)
                    for k in range(KD):
                        last = mm(ps[:, m % 4, 0:256], w[:, k, f * P:(f + 1) * P], hl[:, k, :],
                                  start=k == 0, stop=k == KD - 1)
                    last.then_inc(sem("up_done"), 1) if not (f == 3 or b == NB - 1) else release(last, "ffn_up", 0)
            for half in range(2):
                for part in range(3):
                    w = tile("ffn_down", 3 * half + part)
                    k0, kn = (0, 8, 16)[part], (8, 8, 6)[part]
                    pe.wait_ge(sem("act_ready"), k0 + kn)
                    if half == 0 and part == 0:
                        pe.wait_ge(sem("hl_ready"), 2)
                    if half == 1 and part == 0:
                        pe.wait_ge(sem("act_ready"), NB)
                    for f in range(4):
                        for k in range(kn):
                            last = mm(ps[:, 4 - 4 * half + f, 0:TOKENS], w[:, k, f * P:(f + 1) * P], act[:, k0 + k, :],
                                      start=k0 + k == 0, stop=k0 + k == NB - 1)
                    release(last, "ffn_down", 3 * half + part)
            pe.wait_ge(sem("last_residual"), 2)
            norm_sums("norm4", sq, 0)
            pe.wait_ge(sem("final_scaled"), KD)
            for t in range(TT):
                for k in range(KD):
                    last = tr(ps[:, 4 + 2 * t + k // 4, (k % 4) * P:(k % 4 + 1) * P], hl[:, k, t * P:(t + 1) * P], ident)
                last.then_inc(sem("out_transposed"), 1)

        @block.scalar
        def _(act_e):
            af = nc.scalar.activation
            steps = [0]

            def link(ins):
                steps[0] += 1
                ins.then_inc(sem("scalar_step"), 1)
                act_e.wait_ge(sem("scalar_step"), steps[0])

            act_e.dma_start(x1[:, :, :], a["x"]).then_inc(sem("x_loaded"), 16)
            act_e.dma_start(consts[:, :, :], a["consts"]).then_inc(sem("consts_loaded"), 16)
            act_e.dma_start(vecs[:, :], a["vecs"]).then_inc(sem("vecs_loaded"), 16)
            act_e.dma_start(rope, a["rope"]).then_inc(sem("rope_loaded"), 16)
            act_e.dma_start(decay, a["decay"]).then_inc(sem("decay_loaded"), 16)
            act_e.dma_start(hmask[:, :, :], a["hmask"]).then_inc(sem("hmask_loaded"), 16)

            def sums(name, src, junk, where):
                for t in range(TT):
                    link(af(junk[:, t, :], src[:, t, :], ACT.Square, accum_out=col(where + t)))
                act_e.nop().then_inc(sem(name + "_sums"), 1)

            def rsqrt(dst, src):
                link(af(dst, src, ACT.Ln))
                return af(dst, dst, ACT.Exp, scale=-0.5)

            act_e.wait_ge(sem("x_loaded"), 16)
            for t in range(TT):
                last = af(xn[:, t, :], x1[:, t, :], ACT.Square, accum_out=col(t))
            last.then_inc(sem("norm1_sums"), 1)
            act_e.wait_ge(sem("norm1_mean"), 1)
            rsqrt(col(2, 2), col(2, 2)).then_inc(sem("norm1_rstd"), 1)
            act_e.wait_ge(sem("h1_transposed"), 1)
            act_e.wait_ge(sem("vecs_loaded"), 16)
            for k in range(KD):
                af(hT[:, k, :], ps[:, k // 2, (k % 2) * 256:(k % 2) * 256 + 256], ACT.Copy,
                   scale=vec("norm1", k)).then_inc(sem("h1_ready"), 1)
            act_e.wait_ge(sem("csil_zeroed"), 1)
            for j, name in enumerate(("c", "c_ctx")):
                last = af(csil[:, :, j], vec(name, 0, KD), ACT.Silu)
            last.then_inc(sem("csil_ready"), 1)
            dense_wait(act_e, "w_in", 2)
            af(v_tok, ps[:, 4:6, :], ACT.Copy).then_inc(sem("v_ready"), 1)
            for j in range(2):
                act_e.wait_ge(sem("qk_transposed"), j + 1)
                af(qkT[:, j].rearrange("p (b h) n -> p b (h n)", b=2), ps[:, 2 * j:2 * j + 2, :],
                   ACT.Copy).then_inc(sem("qkT_ready"), 1)
            dense_wait(act_e, "w_in", 3)
            af(g_tok, ps[:, 6:8, :], ACT.Silu).then_inc(sem("g_ready"), 1)
            dense_wait(act_e, "w_in", 4)
            af(gb_s.rearrange("p (b f) n -> p b (f n)", b=2), ps[:, 4:6, :], ACT.Copy).then_inc(sem("gb_ready"), 1)
            dense_wait(act_e, "w_in", 5)
            af(gc_s.rearrange("p (b f) n -> p b (f n)", b=2), ps[:, 6:8, :], ACT.Copy).then_inc(sem("gc_ready"), 1)
            act_e.wait_ge(sem("gn_var"), 1)
            rsqrt(col(8, 8), col(8, 8)).then_inc(sem("gn_rstd"), 1)
            act_e.wait_ge(sem("ret_transposed"), 1)
            for f in range(4):
                af(mixT[:, f, :], ps[:, 2 + f // 2, (f % 2) * 256:(f % 2) * 256 + 256], ACT.Copy,
                   scale=vec("ret_gn", f)).then_inc(sem("mix_ret_ready"), 1)

            def ada(i):
                if i < 12:
                    dense_wait(act_e, "ada", i)
                    if i:
                        act_e.wait_ge(sem("ada_folded"), i)
                    af(ada_s, ps[:, 6, :], ACT.Copy).then_inc(sem("ada_copied"), 1)
                if i:
                    act_e.wait_ge(sem("ada_folded"), i)
                    af(mod[:, 4 * i - 4:4 * i, :], ps[:, 7, :].rearrange("p (f n) -> p f n", f=4)[:, :, 0:2],
                       ACT.Copy).then_inc(sem("mod_copied"), 1)

            act_e.wait_ge(sem("x1_ready"), TT)
            for t in range(TT):
                last = af(xn[:, t, :], x1[:, t, :], ACT.Square, accum_out=col(t))
            last.then_inc(sem("norm2_sums"), 1)
            act_e.dma_start(router_w, a["router_w"]).then_inc(sem("router_loaded"), 16)
            act_e.dma_start(router_b, a["router_b"]).then_inc(sem("router_loaded"), 16)
            act_e.dma_start(iota, a["iota"]).then_inc(sem("router_loaded"), 16)
            ada(0)
            act_e.wait_ge(sem("norm2_mean"), 1)
            rsqrt(col(2, 2), col(2, 2)).then_inc(sem("norm2_rstd"), 1)
            ada(1)
            act_e.wait_ge(sem("h2_transposed"), 1)
            for k in range(KD):
                af(h2T[:, k, :], ps[:, k // 2, (k % 2) * 256:(k % 2) * 256 + 256], ACT.Copy,
                   scale=vec("norm2", k)).then_inc(sem("h2_ready"), 1)
            ada(2)
            for j in range(2):
                act_e.wait_ge(sem("softmax_in"), j + 1)
                for t in range(TT):
                    last = af(rt[:, t, 8 + 40 * j:16 + 40 * j], rt[:, t, 8 + 40 * j:16 + 40 * j], ACT.Exp,
                              accum_out=rt[:, t, 36 + 40 * j:37 + 40 * j])
                last.then_inc(sem("softmax_exp"), 1)
                for i in ((3, 4), (5, 6, 7, 8, 9))[j]:
                    ada(i)
            for k in range(KD):
                act_e.wait_ge(sem("gather_done"), k + 1)
                af(XgT[:, k, 0:SLOTS], ps[:, k % 4, :], ACT.Copy, scale=vec("norm2", k)).then_inc(sem("gathered"), 1)
            for i in (10, 11, 12):
                ada(i)
            act_e.wait_ge(sem("gated_transposed"), 1)
            af(sgT[:, :, :].rearrange("p (b s) n -> p b (s n)", b=2), ps[:, 4:6, :], ACT.Copy).then_inc(
                sem("sgT_ready"), 1)

            def copy_gu(q):
                wait(act_e, "gu_folded", q)
                af(gu_s, ps[:, 0, :], ACT.Copy).then_inc(sem("gu_copied"), 1)

            def silu(q):
                wait(act_e, "gu_folded", q + 1)
                wait(act_e, "hidden_ready", q)
                af(silu_g, ps[:, 1, :].rearrange("p (f n) -> p f n", f=KF)[:, :, 0:WIN], ACT.Silu).then_inc(
                    sem("silu_ready"), 1)

            def store(e, r, q):
                begin = act_e.value_load(starts[0:1, r, bass.ds(e, 1)], min_val=0, max_val=SLOTS)
                wait(act_e, "y_folded", q + 1)
                wait(act_e, "y_written", q)
                for f in range(4):
                    last = af(YT[:, 2 * f:2 * f + 2, bass.ds(begin, WIN)],
                              ps[:, 3, f * P:f * P + 2 * WIN].rearrange("p (a b) -> p a b", b=WIN), ACT.Copy)
                last.then_inc(sem("y_written"), 1)

            def act_fast(e0, e1):
                def step(u, it, more=True):
                    e = it * 2 + (e0 + u)
                    if more:
                        wait(act_e, "up_used", e + 2)
                        copy_gu(e + 1)
                        silu(e + 1)
                    store(e, 0, e)

                wait(act_e, "up_used", e0 + 1)
                copy_gu(e0)
                silu(e0)
                step(0, 0)
                step(1, 0)
                with act_e.Fori(1, (e1 - e0) // 2 - 1) as it:
                    step(0, it)
                    step(1, it)
                step(0, (e1 - e0) // 2 - 1)
                step(1, (e1 - e0) // 2 - 1, more=False)

            def act_slow(e0, e1):
                def expert(u, it):
                    e = it * 2 + (e0 + u)
                    for r in range(ROUNDS):
                        q = e * ROUNDS + r
                        if r == ROUNDS - 1:
                            wait(act_e, "up_used", e + 1)
                        else:
                            wait(act_e, "round_up", e * (ROUNDS - 1) + (r + 1))
                        copy_gu(q)
                        silu(q)
                        store(e, r, q)

                for u in range(2):
                    expert(u, 0)
                with act_e.Fori(1, (e1 - e0) // 2) as it:
                    for u in range(2):
                        expert(u, it)

            def moe(e0, e1):
                flag = act_e.value_load(many[0:1, 0:1], min_val=0, max_val=1)
                with act_e.If(flag < 1):
                    act_fast(e0, e1)
                with act_e.Else():
                    act_slow(e0, e1)

            act_e.wait_ge(sem("starts_ready"), 1)
            moe(*MOE_RANGES[0])

            act_e.wait_ge(sem("lb_in"), 1)
            af(vec("lb", 0, 32), vec("lb", 0, 32), ACT.Exp).then_inc(sem("lb_exp"), 1)
            act_e.wait_ge(sem("ctx_loaded"), 16)
            for t in range(TT):
                last = af(hcT.rearrange("p a b -> p (a b)")[:, t * D:(t + 1) * D], c_raw[:, t, :], ACT.Square,
                          accum_out=col(t))
            last.then_inc(sem("normc_sums"), 1)
            act_e.wait_ge(sem("normc_mean"), 1)
            rsqrt(col(2, 2), col(2, 2)).then_inc(sem("normc_rstd"), 1)
            act_e.wait_ge(sem("hc_transposed"), 1)
            act_e.wait_ge(sem("mod_ready"), 1)
            for k in range(KD):
                af(hcT[:, k, :], ps[:, 4 + k // 2, (k % 2) * 256:(k % 2) * 256 + 256], ACT.Identity,
                   scale=scales[:, 0, k:k + 1], bias=mod[:, k, 1:2]).then_inc(sem("hc_ready"), 1)
            for g in range(NG):
                for d in range(2):
                    dense_wait(act_e, "ctx", 3 * g + d)
                    if d or g:
                        act_e.wait_ge(sem("ctx_kd_ready"), 2 * g + d)
                    af(c_f.rearrange("p (b f) n -> p b (f n)", b=2), ps[:, 4 + 2 * d:6 + 2 * d, :],
                       ACT.Sigmoid).then_inc(sem("ctx_f_read"), 1)
                dense_wait(act_e, "ctx", 3 * g + 2)
                if g == 0:
                    act_e.wait_ge(sem("hc_transposed"), 1)
                else:
                    act_e.wait_ge(sem("ctx_state_done"), GH * g)
                af(c_v, ps[:, 4:6, :], ACT.Copy).then_inc(sem("ctx_v_ready"), 1)
                for h in range(GH):
                    n = GH * g + h
                    act_e.wait_ge(sem("ctx_kd_transposed"), n + 1)
                    if n:
                        act_e.wait_ge(sem("ctx_state_done"), n)
                    af(c_kT.rearrange("p a b c -> p (a b c)"), ps[:, 4, :], ACT.Copy).then_inc(sem("ctx_kdT_ready"), 1)
                    act_e.wait_ge(sem("ctx_state_done"), n + 1)
                    af(state[:, n].rearrange("p a b -> p (a b)"), ps[:, 5, 0:256], ACT.Copy).then_inc(
                        sem("ctx_state_ready"), 1)
                moe(*MOE_RANGES[1 + g])
            flag = act_e.value_load(many[0:1, 0:1], min_val=0, max_val=1)
            with act_e.If(flag < 1):
                act_e.wait_ge(sem("y_written"), EXPERTS)
            with act_e.Else():
                act_e.wait_ge(sem("y_written"), EXPERTS * ROUNDS)
            act_e.nop().then_inc(sem("y_complete"), 1)

            for s in range(SLOTS // P):
                act_e.wait_ge(sem("y_transposed"), s + 1)
                if s == 0:
                    act_e.wait_ge(sem("up_used"), EXPERTS)
                af(y_tok[:, s, :].rearrange("p (a b) -> p a b", b=512), ps[:, 2 * (s % 2):2 * (s % 2) + 2, :],
                   ACT.Copy).then_inc(sem("y_tok_ready"), 1)

            def norm(name, src, psum_in=False):
                act_e.wait_ge(sem(name + "_in"), 1)
                af(sq.rearrange("p a b -> p (a b)"), src.rearrange("p a b -> p (a b)"), ACT.Square).then_inc(
                    sem(name + "_squared"), 1)

            def root(name, bank, width, n=1):
                act_e.wait_ge(sem(name + "_summed"), n)
                act_e.wait_ge(sem(name + "_mean"), n)
                link(af(o_n[:, :], o_n[:, :], ACT.Ln))
                af(ps[:, bank, 256:512], o_n[:, :], ACT.Exp, scale=-0.5).then_inc(sem(name + "_rstd"), 1)

            norm("normf", hl)
            root("normf", 0, D)
            norm("norml", lat)
            root("norml", 1, D)
            act_e.wait_ge(sem("hl_scaled"), 1)
            for k in range(KD):
                last = af(hl[:, k, :], hl[:, k, :], ACT.Identity, bias=mod[:, k, 0:1])
            last.then_inc(sem("hl_ready"), 1)

            for g in range(NG):
                for d in range(2):
                    dense_wait(act_e, "lat", 5 * g + d)
                    dst = (lf, dd)[d]
                    if g:
                        act_e.wait_ge(sem("prod_ready"), 2 * g)
                    af(dst.rearrange("p (b n) -> p b n", b=2), ps[:, 2 * d:2 * d + 2, :], ACT.Sigmoid).then_inc(
                        sem("lat_read"), 1)
                dense_wait(act_e, "lat", 5 * g + 2)
                if g:
                    act_e.wait_ge(sem("o_done"), GH * g)
                af(v_s, ps[:, 0:2, :], ACT.Copy).then_inc(sem("lat_read"), 1)
                dense_wait(act_e, "lat", 5 * g + 3)
                af(q_s.rearrange("p (b f) n -> p b (f n)", b=2), ps[:, 2:4, :], ACT.Silu).then_inc(sem("lat_read"), 1)
                dense_wait(act_e, "lat", 5 * g + 4)
                if g:
                    act_e.wait_ge(sem("readout_done"), GH * g)
                af(g_s.rearrange("p (b f) n -> p b (f n)", b=2), ps[:, 0:2, :], ACT.Silu).then_inc(sem("lat_read"), 1)
                for d in range(2):
                    m = 2 * g + d
                    act_e.wait_ge(sem("f_ready"), m + 1)
                    af(lf if d == 0 else dd, lf if d == 0 else dd, ACT.Ln).then_inc(sem("logf_ready"), 1)
                    if g:
                        act_e.wait_ge(sem("o_done"), GH * g)
                    act_e.wait_ge(sem("b_ready"), m + 1)
                    af(prod[:, d, 2, :], b_s, ACT.Exp).then_inc(sem("eb_ready"), 1)
                    act_e.wait_ge(sem("bref_ready"), m + 1)
                    af(prod[:, d, 0, :], prod[:, d, 1, :], ACT.Exp).then_inc(sem("eq_ready"), 1)
                    act_e.wait_ge(sem("eq_ready"), m + 1)
                    af(prod[:, d, 1, :], prod[:, d, 1, :], ACT.Exp, scale=-1.0).then_inc(sem("ek_ready"), 1)
                    act_e.wait_ge(sem("blast_ready"), m + 1)
                    af(prod[:, d, 3, :], prod[:, d, 3, :], ACT.Exp).then_inc(sem("el_ready"), 1)
                    last_of = (CHUNK2 - 1, 0)[d]
                    af(dec[:, d, :], b_s.rearrange("p (c n) -> p c n", n=CHUNK2)[:, :, last_of], ACT.Exp).then_inc(
                        sem("dec_ready"), 1)
                for h in range(GH):
                    n = GH * g + h
                    act_e.wait_ge(sem("kd_transposed"), n + 1)
                    if n:
                        act_e.wait_ge(sem("kv_done"), n)
                    af(kdT[:, :, :, :].rearrange("p a b c -> p (a b c)"), ps[:, 5, :], ACT.Copy).then_inc(
                        sem("kdT_ready"), 1)
                    act_e.wait_ge(sem("o_done"), n + 1)
                    if n:
                        act_e.wait_ge(sem("o_summed"), n)
                    af(o_sq[:, :], ps[:, 5, 0:256], ACT.Square).then_inc(sem("o_squared"), 1)
                    root("o", 6, P, n + 1)

            norm("norm3", lat)
            root("norm3", 5, D)
            act_e.wait_ge(sem("hl_scaled"), 2)
            for k in range(KD):
                last = af(hl[:, k, :], hl[:, k, :], ACT.Identity, bias=mod[:, 24 + k, 0:1])
            last.then_inc(sem("hl_ready"), 1)
            for b in range(NB):
                for part in range(2):
                    m = 2 * b + part
                    i = part * NB + b
                    if b % 4 == 3 or b == NB - 1:
                        dense_wait(act_e, "ffn_up", 2 * (b // 4) + part)
                    else:
                        act_e.wait_ge(sem("up_done"), 2 * (3 * (b // 4) + b % 4) + part + 1)
                    if b >= 2:
                        act_e.wait_ge(sem("act_ready"), b - 1)
                    af(up_s[:, b % 2, part, :], ps[:, m % 4, 0:256], ACT.Identity,
                       scale=vec("ffn_w", 2 * NB + i), bias=vec("ffn_b", i)).then_inc(sem("conv_begun"), 1)
                act_e.wait_ge(sem("conv_read"), 2 * b + 2)
                af(sg_s[:, b % 2, :], up_s[:, b % 2, 0, :], ACT.Silu).then_inc(sem("ffn_silu"), 1)
            norm("norm4", lat)
            root("norm4", 1, D)
            for t in range(TT):
                act_e.wait_ge(sem("out_transposed"), t + 1)
                af(o_tok[:, t, :].rearrange("p (a b) -> p a b", b=512), ps[:, 4 + 2 * t:6 + 2 * t, :],
                   ACT.Copy).then_inc(sem("out_ready"), 1)

        @block.gpsimd
        def _(pool):
            pool.memset(csil, 0.0).then_inc(sem("csil_zeroed"), 1)
            pool.memset(gcu[:, :, 0:2], 0.0).then_inc(sem("pads_ready"), 1)
            pool.wait_ge(sem("mix_conv_ready"), 4)
            pool.wait_ge(sem("x1_ready"), TT)
            pool.memset(XgT[:, :, SLOTS:COLS], 0.0).then_inc(sem("tail_ready"), 1)
            pool.memset(masked[:, :, :, :], 0.0).then_inc(sem("masked_zeroed"), 1)

            def pool_fast(e0, e1):
                def one(u, it):
                    e = it * 2 + (e0 + u)
                    begin = pool.value_load(starts[0:1, 0, bass.ds(e, 1)], min_val=0, max_val=SLOTS)
                    wait(pool, "up_used", e - 1)
                    pool.tensor_copy(win[:, u], XgT[:, :, bass.ds(begin, WIN)]).then_inc(sem("win_ready"), 1)

                for u in range(2):
                    one(u, 0)
                with pool.Fori(1, (e1 - e0) // 2) as it:
                    for u in range(2):
                        one(u, it)

            def pool_slow(e0, e1):
                def expert(u, it):
                    e = it * 2 + (e0 + u)
                    for r in range(ROUNDS):
                        begin = pool.value_load(starts[0:1, r, bass.ds(e, 1)], min_val=0, max_val=SLOTS)
                        wait(pool, "gu_copied", e * ROUNDS + r)
                        pool.tensor_copy(win[:, u], XgT[:, :, bass.ds(begin, WIN)]).then_inc(sem("win_ready"), 1)

                for u in range(2):
                    expert(u, 0)
                with pool.Fori(1, (e1 - e0) // 2) as it:
                    for u in range(2):
                        expert(u, it)

            def moe(e0, e1):
                flag = pool.value_load(many[0:1, 0:1], min_val=0, max_val=1)
                with pool.If(flag < 1):
                    pool_fast(e0, e1)
                with pool.Else():
                    pool_slow(e0, e1)

            pool.wait_ge(sem("starts_ready"), 1)
            pool.wait_ge(sem("gathered"), KD)
            pool.wait_ge(sem("gated_transposed"), 1)
            pool.dma_start(c_raw, a["ctx"]).then_inc(sem("ctx_loaded"), 16)
            pool.memset(zeros, 0.0).then_inc(sem("zeros_ready"), 1)
            for e0, e1 in MOE_RANGES:
                moe(e0, e1)
            pool.wait_ge(sem("combined"), 1)
            pool.memset(smask, 1.0).then_inc(sem("smask_step"), 1)
            pool.wait_ge(sem("smask_step"), 1)
            pool.memset(smask.rearrange("p (c n) -> p c n", n=CHUNK2)[:, :, 0:1], 0.0).then_inc(sem("smask_ready"), 1)

        @block.vector
        def _(dve):
            tt, ts, stt_ = nc.vector.tensor_tensor, nc.vector.tensor_scalar, nc.vector.scalar_tensor_tensor
            steps = [0]

            def link(ins):
                steps[0] += 1
                ins.then_inc(sem("vector_step"), 1)
                dve.wait_ge(sem("vector_step"), steps[0])

            def token_norm(name, src, dst):
                dve.wait_ge(sem(name + "_sums"), 1)
                ts(col(2, 2), col(0, 2), 1.0 / D, EPS, ALU.mult, ALU.add).then_inc(sem(name + "_mean"), 1)
                dve.wait_ge(sem(name + "_rstd"), 1)
                for t in range(TT):
                    ts(dst[:, t, :], src[:, t, :], col(2 + t), None, ALU.mult).then_inc(sem(name + "_scaled"), 1)

            token_norm("norm1", x1, xn)
            dve.wait_ge(sem("rope_loaded"), 16)
            for j in range(2):
                dense_wait(dve, "w_in", j)
                for t in range(TT):
                    src = ps[:, 4 + 2 * j + t, :].rearrange("p (h s d) -> p h s d", h=HEADS1, s=2)
                    ra = rot_a.rearrange("p (h d) -> p h d", h=HEADS1)
                    rb = rot_b.rearrange("p (h s d) -> p h s d", h=HEADS1, s=2)
                    cos = rope[:, 0, t, :].unsqueeze(1).to_broadcast([P, HEADS1, P])
                    tt(ra, ps[:, 4 + 2 * j + t, :].rearrange("p (h d) -> p h d", h=HEADS1), cos, ALU.mult)
                    for s in range(2):
                        sin = rope[:, 1, t, s * 64:(s + 1) * 64].unsqueeze(1).to_broadcast([P, HEADS1, 64])
                        last = tt(rb[:, :, s, :], src[:, :, 1 - s, :], sin, ALU.mult)
                    link(last)
                    last = tt(qk_rot[:, j, t, :], rot_a, rot_b, ALU.add)
                    if t == 0:
                        link(last)
                last.then_inc(sem("qk_rotated"), 1)
                dve.wait_ge(sem("qk_rotated"), j + 1)
            dve.wait_ge(sem("decay_loaded"), 16)
            for h in range(HEADS1):
                dve.wait_ge(sem("scores_done"), h + 1)
                tt(probs[:, h, 0:256], ps[:, h, 0:256], decay[:, h, :], ALU.mult)
                tt(probs[:, h, 256:384], ps[:, h, 256:384], decay[:, h, 0:P], ALU.mult).then_inc(sem("decayed"), 1)
            dense_wait(dve, "w_in", 5)
            for t in range(TT):
                for h in range(HEADS1):
                    last = nc.vector.bn_stats(stats[:, 4 * t + h, :], ps[:, t, h * P:(h + 1) * P])
            link(last)
            for m in range(8):
                last = nc.vector.bn_aggr(mv[:, m, :], stats[:, m, :])
            link(last)
            ts(col(8, 8), mv[:, :, 1], EPS, None, ALU.add).then_inc(sem("gn_var"), 1)
            dve.wait_ge(sem("gn_rstd"), 1)
            for t in range(TT):
                for h in range(HEADS1):
                    m = 4 * t + h
                    last = ts(ret[:, t, h * P:(h + 1) * P], ps[:, t, h * P:(h + 1) * P], mv[:, m, 0:1], col(8 + m),
                              ALU.subtract, ALU.mult)
            link(last)
            dve.wait_ge(sem("g_ready"), 1)
            for t in range(TT):
                tt(ret[:, t, :], ret[:, t, :], g_tok[:, t, :], ALU.mult).then_inc(sem("ret_ready"), 1)
            dense_wait(dve, "w_in", 6)
            dve.wait_ge(sem("gc_ready"), 1)
            dve.wait_ge(sem("pads_ready"), 1)
            for f in range(4):
                last = tt(gcu[:, f, 2:], gc_s[:, f, :], ps[:, 4 + f // 2, (f % 2) * 256:(f % 2) * 256 + 256], ALU.mult)
            link(last)
            for f in range(4):
                last = ts(conv_a[:, f, :], gcu[:, f, 0:256], vec("conv", f), None, ALU.mult)
            link(last)
            for tap in (1, 2):
                for f in range(4):
                    last = stt_(conv_a[:, f, :], gcu[:, f, tap:tap + 256], vec("conv", 4 * tap + f), conv_a[:, f, :],
                                ALU.mult, ALU.add)
                link(last)
            dve.wait_ge(sem("gb_ready"), 1)
            dve.wait_ge(sem("qkT_ready"), 2)
            for f in range(4):
                tt(mixT[:, 4 + f, :], conv_a[:, f, :], gb_s[:, f, :], ALU.mult).then_inc(sem("mix_conv_ready"), 1)
            dense_wait(dve, "w_o", 1)
            for t in range(TT):
                xv = x1[:, t, :].rearrange("p (a b) -> p a b", b=512)
                tt(xv, xv, ps[:, 4 + 2 * t:6 + 2 * t, :], ALU.add).then_inc(sem("x1_ready"), 1)

            token_norm("norm2", x1, xn)
            dve.wait_ge(sem("router_done"), 1)
            dve.wait_ge(sem("router_loaded"), 48)
            L = logits
            for t in range(TT):
                last = tt(L[:, t, :], ps[:, 4, t * 72:t * 72 + 72], router_b, ALU.add)
            link(last)

            def softmax_in(j, src, both):
                o = 40 * j
                for t in range(TT):
                    last = nc.vector.max(rt[:, t, o:o + 8], src(t))
                link(last)
                tt(rt[:, :, o + 8:o + 16], both, rt[:, :, o:o + 1].to_broadcast([P, TT, 8]), ALU.subtract).then_inc(
                    sem("softmax_in"), 1)

            def softmax_top(j):
                o = 40 * j
                dve.wait_ge(sem("softmax_exp"), j + 1)
                link(nc.vector.reciprocal(rt[:, :, o + 37:o + 38], rt[:, :, o + 36:o + 37]))
                link(tt(rt[:, :, o + 8:o + 16], rt[:, :, o + 8:o + 16], rt[:, :, o + 37:o + 38].to_broadcast([P, TT, 8]),
                        ALU.mult))
                for t in range(TT):
                    last = nc.vector.max(rt[:, t, o + 16:o + 24], rt[:, t, o + 8:o + 16])
                link(last)
                for t in range(TT):
                    last = nc.vector.max_index(rt[:, t, o + 24:o + 32].bitcast(u32), rt[:, t, o + 16:o + 24],
                                               rt[:, t, o + 8:o + 16])
                link(last)
                link(nc.vector.tensor_copy(rt[:, :, o + 32:o + 34], rt[:, :, o + 24:o + 26].bitcast(u32)))

            softmax_in(0, lambda t: L[:, t, 0:8], L[:, :, 0:8])
            softmax_top(0)
            for t in range(TT):
                last = ts(rt[:, t, 80:88], iota[:, 0:8], rt[:, t, 32:33], None, ALU.is_equal)
            link(last)
            for t in range(TT):
                last = tt(rt[:, t, 96:160].rearrange("p (e g) -> p e g", g=8),
                          L[:, t, 8:72].rearrange("p (g e) -> p e g", g=8),
                          rt[:, t, 80:88].unsqueeze(1).to_broadcast([P, 8, 8]), ALU.mult)
            link(last)
            for t in range(TT):
                last = nc.vector.reduce_sum(rt[:, t, 88:96], rt[:, t, 96:160].rearrange("p (e g) -> p e g", g=8), axis=X)
            link(last)
            softmax_in(1, lambda t: rt[:, t, 88:96], rt[:, :, 88:96])
            softmax_top(1)
            for t in range(TT):
                last = stt_(rt[:, t, 80:82], rt[:, t, 32:33].to_broadcast([P, 2]), 8.0, rt[:, t, 72:74], ALU.mult, ALU.add)
            link(last)
            for t in range(TT):
                last = tt(rt[:, t, 84:85], rt[:, t, 56:57], rt[:, t, 57:58], ALU.add)
            link(last)
            for t in range(TT):
                last = nc.vector.reciprocal(rt[:, t, 84:85], rt[:, t, 84:85])
            link(last)
            for t in range(TT):
                last = ts(rt[:, t, 82:84], rt[:, t, 56:58], rt[:, t, 84:85], rt[:, t, 16:17], ALU.mult, ALU.mult)
            link(last)
            for j in range(2):
                for t in range(TT):
                    last = ts(onehot[:, j, t, :], iota[:, 0:EXPERTS], rt[:, t, 80 + j:81 + j], None, ALU.is_equal)
            link(last)
            tt(assigned, onehot[:, 0], onehot[:, 1], ALU.add).then_inc(sem("assigned_ready"), 1)
            dve.wait_ge(sem("counted"), 1)
            link(nc.vector.tensor_copy(count, ps[:, 5, 0:192].rearrange("p (a b) -> p a b", b=EXPERTS)))
            link(ts(place[:, 0, :], count[:, 2, :], 0.0, 1.0, ALU.mult, ALU.add))
            link(nc.vector.tensor_tensor_scan(place[:, 1, :], place[:, 0, :], count[:, 2, :], 0.0, ALU.mult, ALU.add))
            link(tt(place[:, 1, :], place[:, 1, :], count[:, 2, :], ALU.subtract))
            for r in range(ROUNDS):
                ts(starts[0:1, r, :], place[0:1, 1, :], float(WIN * r), float(SLOTS), ALU.add, ALU.min)
            link(nc.vector.reduce_max(col(20), count[:, 2, :], axis=X))
            ts(many[0:1, 0:1], col(20)[0:1, :], float(WIN), None, ALU.is_gt).then_inc(sem("starts_ready"), 1)
            for t in range(TT):
                last = tt(count[:, t, :], count[:, t, :], place[:, 1, :], ALU.add)
            link(last)
            for j in range(2):
                for t in range(TT):
                    last = tt(onehot[:, j, t, :], onehot[:, j, t, :], count[:, t, :], ALU.mult)
            link(last)
            link(nc.vector.reduce_sum(col(24, 4), onehot.rearrange("p j t e -> p (j t) e"), axis=X))
            for t in range(TT):
                last = ts(sel[:, t, :], iota, col(24 + t), None, ALU.is_equal)
            link(last)
            for t in range(TT):
                last = stt_(sel[:, t, :], iota, col(26 + t), sel[:, t, :], ALU.is_equal, ALU.add)
            last.then_inc(sem("sel_ready"), 1)
            for t in range(TT):
                last = ts(gated[:, t, :], iota, col(24 + t), rt[:, t, 82:83], ALU.is_equal, ALU.mult)
            link(last)
            for t in range(TT):
                last = ts(h2T.rearrange("p a b -> p (a b)")[:, t * 512:(t + 1) * 512], iota, col(26 + t),
                          rt[:, t, 83:84], ALU.is_equal, ALU.mult)
            link(last)
            for t in range(TT):
                last = tt(gated[:, t, :], gated[:, t, :], h2T.rearrange("p a b -> p (a b)")[:, t * 512:(t + 1) * 512],
                          ALU.add)
            last.then_inc(sem("gated_ready"), 1)

            def copy_y(q):
                wait(dve, "y_folded", q)
                nc.vector.tensor_copy(y_s, ps[:, 2, :]).then_inc(sem("y_copied"), 1)

            def multiply(u, q):
                wait(dve, "silu_ready", q + 1)
                tt(hidden[:, u], silu_g, ps[:, 1, :].rearrange("p (f n) -> p f n", f=KF)[:, :, WIN:2 * WIN],
                   ALU.mult).then_inc(sem("hidden_ready"), 1)

            def dve_fast(e0, e1):
                def step(u, it, more=True):
                    e = it * 2 + (e0 + u)
                    wait(dve, "down_used", e + 1)
                    copy_y(e)
                    if more:
                        multiply(1 - u, e + 1)

                multiply(0, e0)
                step(0, 0)
                step(1, 0)
                with dve.Fori(1, (e1 - e0) // 2 - 1) as it:
                    step(0, it)
                    step(1, it)
                step(0, (e1 - e0) // 2 - 1)
                step(1, (e1 - e0) // 2 - 1, more=False)

            def dve_slow(e0, e1):
                def expert(u, it):
                    e = it * 2 + (e0 + u)
                    for r in range(ROUNDS):
                        q = e * ROUNDS + r
                        multiply(u, q)
                        if r == ROUNDS - 1:
                            wait(dve, "down_used", e + 1)
                        else:
                            wait(dve, "round_down", e * (ROUNDS - 1) + (r + 1))
                        copy_y(q)

                for u in range(2):
                    expert(u, 0)
                with dve.Fori(1, (e1 - e0) // 2) as it:
                    for u in range(2):
                        expert(u, it)

            def moe(e0, e1):
                flag = dve.value_load(many[0:1, 0:1], min_val=0, max_val=1)
                with dve.If(flag < 1):
                    dve_fast(e0, e1)
                with dve.Else():
                    dve_slow(e0, e1)

            lbv = vecs[:, VEC["lb"]:VEC["lb"] + 32].rearrange("p (l n) -> p l n", l=2)
            link(tt(small[:, 32:48], lbv[:, 0, :], lbv[:, 1, :], ALU.max))
            for l in range(2):
                last = tt(lbv[:, l, :], lbv[:, l, :], small[:, 32:48], ALU.subtract)
            last.then_inc(sem("lb_in"), 1)
            dve.wait_ge(sem("starts_ready"), 1)
            moe(*MOE_RANGES[0])

            dve.wait_ge(sem("mod_copied"), 12)
            link(tt(mod[:, :, :], mod[:, :, :], vec("b_ada", 0, 48).unsqueeze(2).to_broadcast([P, 48, 2]), ALU.add))
            for row, (chunk, who, gain) in enumerate(((8, 1, 0), (8, 0, 0), (32, 0, 8))):
                last = stt_(scales[:, row, :], mod[:, chunk:chunk + 8, who], 1.0, vec("norm_g", gain, 8), ALU.add,
                            ALU.mult)
            last.then_inc(sem("mod_ready"), 1)
            dve.wait_ge(sem("lb_exp"), 1)
            link(tt(small[:, 32:48], lbv[:, 0, :], lbv[:, 1, :], ALU.add))
            link(nc.vector.reciprocal(small[:, 32:48], small[:, 32:48]))
            lbf = lbs[:, 0].rearrange("p a b -> p (a b)")
            link(tt(lbf, lbv[:, 0, :], small[:, 32:48], ALU.mult))
            link(ts(lbs[:, 1].rearrange("p a b -> p (a b)"), lbf, -1.0, 1.0, ALU.mult, ALU.add))
            token_norm("normc", c_raw, c_raw)
            dve.wait_ge(sem("zeros_ready"), 1)
            for g in range(NG):
                for d in range(2):
                    m = 2 * g + d
                    dve.wait_ge(sem("ctx_f_read"), m + 1)
                    for h in range(GH):
                        last = ts(c_f[:, h, :], c_f[:, h, :], lbs[:, 1, d, GH * g + h:GH * g + h + 1],
                                  lbs[:, 0, d, GH * g + h:GH * g + h + 1], ALU.mult, ALU.add)
                    link(last)
                    if g:
                        dve.wait_ge(sem("ctx_kd_transposed"), GH * g)
                    for h in range(GH):
                        if d == 0:
                            nc.vector.memset(c_p[:, d, h, TOKENS - 1:TOKENS], 1.0)
                            last = nc.vector.tensor_tensor_scan(c_p[:, d, h, TOKENS - 2::-1], c_f[:, h, TOKENS - 1:0:-1],
                                                                zeros[:, 0:TOKENS - 1], 1.0, ALU.mult, ALU.add)
                        else:
                            nc.vector.memset(c_p[:, d, h, 0:1], 1.0)
                            last = nc.vector.tensor_tensor_scan(c_p[:, d, h, 1:TOKENS], c_f[:, h, 0:TOKENS - 1],
                                                                zeros[:, 0:TOKENS - 1], 1.0, ALU.mult, ALU.add)
                    link(last)
                    cf = c_f.rearrange("p a b -> p (a b)")
                    cp = c_p[:, d].rearrange("p a b -> p (a b)")
                    link(ts(cf, cf, -1.0, 1.0, ALU.mult, ALU.add))
                    tt(cp, cp, cf, ALU.mult).then_inc(sem("ctx_kd_ready"), 1)
                moe(*MOE_RANGES[1 + g])

            def mean(name, bank, width, n=1):
                dve.wait_ge(sem(name + "_summed"), n)
                ts(o_n[:, :], ps[:, bank, 0:256] if name != "o" else ps[:, 4, 256:512], 1.0 / width, EPS, ALU.mult,
                   ALU.add).then_inc(sem(name + "_mean"), 1)
                dve.wait_ge(sem(name + "_rstd"), n)

            dve.wait_ge(sem("combined"), 1)
            nc.vector.tensor_copy(hl.rearrange("p (b f) n -> p b (f n)", b=4), ps[:, 4:8, :]).then_inc(
                sem("normf_in"), 1)
            mean("normf", 0, D)
            for k in range(KD):
                last = stt_(lat[:, k, :], hl[:, k, :], vec("final1", k), ps[:, 0, 256:512], ALU.mult, ALU.mult)
            last.then_inc(sem("norml_in"), 1)
            mean("norml", 1, D)
            for k in range(KD):
                last = stt_(hl[:, k, :], lat[:, k, :], scales[:, 1, k:k + 1], ps[:, 1, 256:512], ALU.mult, ALU.mult)
            last.then_inc(sem("hl_scaled"), 1)

            dve.wait_ge(sem("smask_ready"), 1)
            dve.wait_ge(sem("hmask_loaded"), 16)
            dve.wait_ge(sem("masked_zeroed"), 1)
            chunks = lambda v: v.rearrange("p (c n) -> p c n", n=CHUNK2)
            wide = lambda v: v.unsqueeze(2).to_broadcast([P, GH * NCH, CHUNK2])
            qf = q_s.rearrange("p a b -> p (a b)")
            for g in range(NG):
                for d in range(2):
                    m = 2 * g + d
                    buf = lf if d == 0 else dd
                    dve.wait_ge(sem("lat_read"), 5 * g + d + 1)
                    for h in range(GH):
                        last = ts(buf[:, h * TOKENS:(h + 1) * TOKENS], buf[:, h * TOKENS:(h + 1) * TOKENS],
                                  lbs[:, 1, d, GH * g + h:GH * g + h + 1], lbs[:, 0, d, GH * g + h:GH * g + h + 1],
                                  ALU.mult, ALU.add)
                    link(last)
                    ts(kk, buf, -1.0, 1.0, ALU.mult, ALU.add).then_inc(sem("f_ready"), 1)
                    dve.wait_ge(sem("logf_ready"), m + 1)
                    if m:
                        dve.wait_ge(sem("dec_ready"), m)
                    if d == 0:
                        nc.vector.tensor_tensor_scan(b_s, smask, buf, 0.0, ALU.mult, ALU.add).then_inc(sem("b_ready"), 1)
                    else:
                        link(nc.vector.tensor_tensor_scan(lf, smask, buf, 0.0, ALU.mult, ALU.add))
                        link(tt(buf, buf, lf, ALU.subtract))
                        tt(chunks(b_s), chunks(buf), wide(chunks(lf)[:, :, CHUNK2 - 1]), ALU.add).then_inc(
                            sem("b_ready"), 1)
                    dve.wait_ge(sem("b_ready"), m + 1)
                    if g:
                        dve.wait_ge(sem("o_done"), GH * g)
                    ref, end = (CHUNK2 // 2, CHUNK2 - 1) if d == 0 else (CHUNK2 - 1 - CHUNK2 // 2, 0)
                    tt(chunks(prod[:, d, 1, :]), chunks(b_s), wide(chunks(b_s)[:, :, ref]), ALU.subtract).then_inc(
                        sem("bref_ready"), 1)
                    tt(chunks(prod[:, d, 3, :]), wide(chunks(b_s)[:, :, end]), chunks(b_s), ALU.subtract).then_inc(
                        sem("blast_ready"), 1)
                    dve.wait_ge(sem("lat_read"), 5 * g + 4)
                    dve.wait_ge(sem("eb_ready"), m + 1)
                    tt(prod[:, d, 2, :], prod[:, d, 2, :], qf, ALU.mult)
                    dve.wait_ge(sem("eq_ready"), m + 1)
                    tt(prod[:, d, 0, :], prod[:, d, 0, :], qf, ALU.mult)
                    dve.wait_ge(sem("ek_ready"), m + 1)
                    tt(prod[:, d, 1, :], prod[:, d, 1, :], kk, ALU.mult)
                    dve.wait_ge(sem("el_ready"), m + 1)
                    tt(prod[:, d, 3, :], prod[:, d, 3, :], kk, ALU.mult).then_inc(sem("prod_ready"), 1)
                    dve.wait_ge(sem("prod_ready"), m + 1)
                    dve.wait_ge(sem("dec_ready"), m + 1)
                for h in range(GH):
                    n = GH * g + h
                    dve.wait_ge(sem("s_done"), n + 1)
                    if n:
                        dve.wait_ge(sem("o_done"), n)
                    for d in range(2):
                        for quarter in range(4):
                            HC = CHUNK2 // 2
                            lo, late = quarter * HC, quarter % 2 != d
                            q0, qn = ((quarter % 2) * HC, HC) if late else (0, CHUNK2)
                            to = (quarter // 2) * CHUNK2 + q0
                            last = nc.vector.copy_predicated(
                                masked[lo:lo + HC, d, :, to:to + qn],
                                hmask[lo:lo + HC, d, q0:q0 + qn].unsqueeze(1).to_broadcast([HC, TT, qn]),
                                ps[lo:lo + HC, 4, 0:256].rearrange("p (t d n) -> p t d n", t=TT, d=2)[:, :, d, q0:q0 + qn])
                    last.then_inc(sem("masked_ready"), 1)
                    for d in range(2):
                        dve.wait_ge(sem("kv_done"), n + 1)
                        for j in range(1, NCH):
                            c = j - 1 if d == 0 else NCH - j
                            prev = state[:, n, d, :] if j == 1 else chunk_state[:, d, j - 1, :]
                            last = stt_(chunk_state[:, d, j, :], prev, dec[:, d, h * NCH + c:h * NCH + c + 1],
                                        kv_bank(d, c), ALU.mult, ALU.add)
                            if j < NCH - 1:
                                link(last)
                        last.then_inc(sem("states_ready"), 1)
                    mean("o", 4, P, n + 1)
                    link(tt(o_sq[:, :], g_s[:, h, :], ps[:, 6, 256:512], ALU.mult))
                    stt_(attn[:, n, :], ps[:, 5, 0:256], vec("gnorm"), o_sq[:, :], ALU.mult, ALU.mult).then_inc(
                        sem("readout_done"), 1)
            for i in range(2):
                dense_wait(dve, "hg_out", i)
                for f in range(4):
                    k = 4 * i + f
                    last = stt_(lat[:, k, :], ps[:, 2 * i + f // 2, (f % 2) * 256:(f % 2) * 256 + 256], mod[:, 16 + k, 0:1],
                                lat[:, k, :], ALU.mult, ALU.add)
            last.then_inc(sem("norm3_in"), 1)
            mean("norm3", 4, D)
            for k in range(KD):
                last = stt_(hl[:, k, :], lat[:, k, :], scales[:, 2, k:k + 1], ps[:, 5, 256:512], ALU.mult, ALU.mult)
            last.then_inc(sem("hl_scaled"), 1)

            for b in range(NB):
                for part in range(2):
                    i = part * NB + b
                    dve.wait_ge(sem("conv_begun"), 2 * b + part + 1)
                    p_in, acc = ps[:, (2 * b + part) % 4, 0:256], up_s[:, b % 2, part, :]
                    link(stt_(acc[:, 1:], p_in[:, 0:255], vec("ffn_w", i), acc[:, 1:], ALU.mult, ALU.add))
                    stt_(acc[:, 0:255], p_in[:, 1:], vec("ffn_w", 4 * NB + i), acc[:, 0:255], ALU.mult,
                         ALU.add).then_inc(sem("conv_read"), 1)
                dve.wait_ge(sem("conv_read"), 2 * b + 2)
                dve.wait_ge(sem("ffn_silu"), b + 1)
                tt(act[:, b, :], sg_s[:, b % 2, :], up_s[:, b % 2, 1, :], ALU.mult).then_inc(sem("act_ready"), 1)
            for half in range(2):
                dense_wait(dve, "ffn_down", 3 * half + 2)
                for f in range(4):
                    k = 4 * half + f
                    last = stt_(lat[:, k, :], ps[:, 4 - 4 * half + f, 0:256], mod[:, 40 + k, 0:1], lat[:, k, :], ALU.mult,
                                ALU.add)
                last.then_inc(sem("last_residual"), 1)
            dve.wait_ge(sem("last_residual"), 2)
            dve.nop().then_inc(sem("norm4_in"), 1)
            mean("norm4", 0, D)
            for k in range(KD):
                stt_(hl[:, k, :], lat[:, k, :], vec("final2", k), ps[:, 1, 256:512], ALU.mult, ALU.mult).then_inc(
                    sem("final_scaled"), 1)


def constants():
    t = np.arange(TOKENS, dtype=np.float32)
    half = 64
    inv = (10000.0 ** (-np.arange(half, dtype=np.float32) / half)).astype(np.float32)
    ang = t[:, None] * inv[None, :]
    cos, sin = np.cos(ang).astype(np.float32), np.sin(ang).astype(np.float32)
    rope = np.stack([np.concatenate([cos, cos], 1), np.concatenate([-sin, sin], 1)])
    rope = rope.reshape(2, TT, P, P).transpose(2, 0, 1, 3)
    log_g = np.log1p(-(2.0 ** (-5.0 - np.arange(HEADS1))))
    rel = np.arange(TOKENS)[None, :] - np.arange(P)[:, None]
    decay = np.where(rel[:, None] >= 0, np.exp(log_g[None, :, None] * np.maximum(rel, 0)[:, None]), 0.0) * 128 ** -0.5
    p = np.arange(P)
    quarter, row, n = p[:, None] // 32, p[:, None] % 32, p[None, :]
    pairs, every = (quarter // 2 == n // 32) & (row == n % 32), (row == n)
    consts = np.stack([np.eye(P), np.ones((P, P)), p[:, None] < p[None, :], pairs, every], 1)
    j, i = p[:, None] % CHUNK2, np.arange(CHUNK2)[None, :]
    hmask = np.stack([j <= i, j >= i], 1)
    iota = np.broadcast_to(np.arange(SLOTS), (P, SLOTS))
    f = lambda v, dt=np.float32: np.ascontiguousarray(v).astype(dt)
    return {"rope": f(rope), "decay": f(decay), "consts": f(consts), "hmask": f(hmask, np.int32), "iota": f(iota)}


def kernel(**inputs):
    import concourse.bacc as bacc
    from concourse.bass_utils import run_bass_kernel_spmd as run

    g = {k: np.asarray(v) for k, v in inputs.items()}
    tok = lambda v: np.ascontiguousarray(v.reshape(TT, P, D).transpose(1, 0, 2))
    blk = lambda v: v.reshape(-1, P).T
    packed = {"norm1": blk(g["norm1_w"]), "ret_gn": blk(g["ret_gn_w"]), "conv": blk(g["conv_w"]),
              "norm2": g["norm2_w"].reshape(P, KD), "final1": blk(g["final_norm_w"]), "norm_g": blk(g["norm_g_2"]),
              "final2": blk(g["final_g_2"]), "lb": blk(g["hg_lb_logits_2"]), "gnorm": blk(g["hg_gnorm_2"]),
              "b_ada": blk(g["b_ada_2"]), "ffn_w": blk(g["ffn_conv_w_2"]), "ffn_b": blk(g["ffn_conv_b_2"]),
              "c": blk(g["c_2"]), "c_ctx": blk(g["c_ctx_2"])}
    taps = g["ffn_conv_w_2"].reshape(3, 2 * DFF)
    packed["ffn_w"] = blk(np.ascontiguousarray(taps[[0, 1, 2]]))
    router = np.concatenate([g["router_g_w"][0], g["router_e_w"][0].transpose(1, 0, 2).reshape(D, 64)], 1)
    bias = np.concatenate([g["router_g_b"].reshape(1, 8), g["router_e_b"].reshape(1, 64)], 1)
    arrays = {
        "x": tok(g["x"]), "ctx": tok(g["ctx_2"]),
        "vecs": np.ascontiguousarray(np.concatenate([packed[n] for n in VEC], 1)),
        "router_w": np.ascontiguousarray(router.reshape(P, KD, 72)),
        "router_b": np.ascontiguousarray(np.repeat(bias, P, 0)),
        "w_in": g["w_in"][0], "w_o": g["w_o"][0], "w_gate": g["w_gate"][0], "w_up": g["w_up"][0],
        "w_down": g["w_down"][0], "w_ada": g["w_ada_2"][0], "hg_in": g["hg_w_in_2"][0], "hg_out": g["hg_w_out_2"][0],
        "ffn_up": g["ffn_w_up_2"][0], "ffn_down": g["ffn_w_down_2"][0],
        **constants(),
    }
    nc = bacc.Bacc("TRN2", target_bir_lowering=False, num_devices=1)
    sent, a = {}, {}
    for name, v in arrays.items():
        v = np.ascontiguousarray(v)
        sent["in_" + name] = v
        a[name] = nc.dram_tensor("in_" + name, v.shape, mybir.dt.from_np(v.dtype), kind="ExternalInput").ap()
    out = nc.dram_tensor("out_0", (1, TOKENS, D), mybir.dt.float32, kind="ExternalOutput").ap()
    program(nc, a, out)
    return run(nc, [sent], core_ids=[0]).results[0]["out_0"]
```

```python
import numpy as np
import concourse.bass as bass
from concourse import mybir
from contextlib import ExitStack

P = 128
TOKENS = 256
TT = TOKENS // P
D = 1024
KD = D // P
EPS = 1e-6
HEADS1 = 4
EXPERTS = 64
FF = 512
KF = FF // P
SLOTS = TOKENS * 2
WIN = 32
COLS = SLOTS + WIN
ROUNDS = TOKENS // WIN
HEADS2 = 8
CHUNK2 = 64
NCH = TOKENS // CHUNK2
GH = 4
NG = HEADS2 // GH
DFF = 2816
NB = DFF // P
PARTS = (("forward", "backward", "query", "value", "gate"), ("value", "gate", "forward", "backward", "query"))
HG_COLUMN = {"query": 0, "forward": D, "backward": 2 * D, "value": 3 * D, "gate": 4 * D}
RING = 6
RING_LATE = 3
SLOT = 4096

VEC = {}
_at = 0
for _name, _n in (("norm1", 8), ("ret_gn", 4), ("conv", 12), ("norm2", 8), ("final1", 8), ("norm_g", 16),
                  ("lb", 32), ("gnorm", 1), ("b_ada", 48), ("ffn_w", 3 * 2 * NB),
                  ("ffn_b", 2 * NB), ("c", 8), ("c_ctx", 8)):
    VEC[_name] = _at
    _at += _n
NVEC = _at

CTX_STAGES = ("f0", "f1", "v", "heads") * NG
MOE_RANGES = [(0, 16)] + [(16 + 4 * r, 20 + 4 * r) for r in range(len(CTX_STAGES) - 1)] + [(44, EXPERTS)]
CTX_TILES = {"f0": 0, "f1": 1, "v": 2}


def tile_order():
    order = [("w_in", c) for c in range(7)] + [("ada", c) for c in range(3)] + [("w_o", c) for c in range(2)]
    order += [("ada", c) for c in range(3, 12)]
    for r, (e0, e1) in enumerate(MOE_RANGES):
        for e in range(e0, e1):
            order += [("gate", e), ("up", e), ("down", e)]
        if r < len(CTX_STAGES) and CTX_STAGES[r] in CTX_TILES:
            order.append(("ctx", 3 * (r // 4) + CTX_TILES[CTX_STAGES[r]]))
    order += [("lat", c) for c in range(10)] + [("hg_out", c) for c in range(2)]
    order += [("ffn_up", c) for c in range(12)] + [("ffn_down", c) for c in range(6)]
    return order


def program(nc, a, out):
    f32, i32, u32 = mybir.dt.float32, mybir.dt.int32, mybir.dt.uint32
    ALU, ACT, AX = mybir.AluOpType, mybir.ActivationFunctionType, mybir.AxisListType
    X = AX.X
    ctx = ExitStack()
    with ctx:
        def sb(name, shape, dt=f32):
            return ctx.enter_context(nc.sbuf_tensor(name, shape, dt))

        sems = {}

        def sem(name):
            if name not in sems:
                sems[name] = ctx.enter_context(nc.semaphore(name))
            return sems[name]

        ring = sb("ring", [P, RING, SLOT])
        consts = sb("consts", [P, 5, P])
        ident, ones, before = consts[:, 0, :], consts[:, 1, :], consts[:, 2, :]
        fold_pairs, fold_all = consts[:, 3, :], consts[:, 4, :]
        vecs = sb("vecs", [P, NVEC])
        hmask = sb("hmask", [P, 2, CHUNK2], i32)
        mod = sb("mod", [P, 48, 2])
        scales = sb("scales", [P, 3, KD])
        lbs = sb("lbs", [P, 2, 2, HEADS2])
        small = sb("small", [P, 96])
        many = sb("many", [1, 1], i32)
        x1 = sb("x1", [P, TT, D])
        sgT = sb("sgT", [P, SLOTS // P, TOKENS])
        state = sb("state", [P, HEADS2, 2, P])
        arena = sb("arena", [P, 20480])

        def at(offset, *shape, dt=None):
            n = int(np.prod(shape))
            assert offset + n <= 20480, (offset, shape)
            v = arena[:, offset:offset + n]
            if len(shape) == 2:
                v = v.rearrange("p (a b) -> p a b", b=shape[1])
            if len(shape) == 3:
                v = v.rearrange("p (a b c) -> p a b c", b=shape[1], c=shape[2])
            return v

        xn = at(0, TT, D)
        hT = at(2048, KD, TOKENS)
        qk_rot = at(4096, 2, TT, 512)
        qkT = at(6144, 2, HEADS1, TOKENS)
        mixT = at(8192, KD, TOKENS)
        v_tok = at(10240, TT, 512)
        g_tok = at(11264, TT, 512)
        probs = at(12288, HEADS1, 384)
        gb_s = at(13824, 4, TOKENS)
        gc_s = at(14848, 4, TOKENS)
        gcu = at(15872, 4, TOKENS + 2)
        decay = at(16904, HEADS1, TOKENS)
        rope = at(17928, 2, TT, P)
        rot_a = at(18440, 1, 512)[:, 0, :]
        rot_b = at(18952, 1, 512)[:, 0, :]
        ret = at(4096, TT, 512)
        conv_a = at(0, 4, TOKENS)
        stats = at(1024, 8, 6)
        mv = at(1100, 8, 2)
        h2T = at(2048, KD, TOKENS)
        router_w = at(4096, KD, 72)
        router_b = at(4672, 1, 72)[:, 0, :]
        iota = at(4744, 1, SLOTS)[:, 0, :]
        logits = at(5256, TT, 72)
        rt = at(5400, TT, 160)
        onehot = at(5720, 2, TT, EXPERTS)
        assigned = at(5976, TT, EXPERTS)
        place = at(6104, TT, EXPERTS)
        count = at(6232, 3, EXPERTS)
        sel = at(6424, TT, SLOTS)
        gated = at(7448, TT, SLOTS)
        starts = arena[:, 8472:8472 + ROUNDS * EXPERTS].bitcast(i32).rearrange("p (r e) -> p r e", e=EXPERTS)
        YT = at(8984, KD, COLS)
        XgT = at(13336, KD, COLS)
        win = at(17688, 2, KD, WIN)
        hidden = at(18200, 2, KF, WIN)
        silu_g = at(18456, KF, WIN)
        gu_s = at(18584, 1, 512)[:, 0, :]
        y_s = at(19096, 1, 512)[:, 0, :]
        ada_s = at(19608, 1, 512)[:, 0, :]
        csil = at(20120, KD, 32)
        c_raw = at(0, TT, D)
        hcT = at(2048, KD, TOKENS)
        c_f = at(4096, GH, TOKENS)
        c_p = at(5120, 2, GH, TOKENS)
        c_v = at(0, TT, 512)
        c_kT = at(1024, 2, TT, P)
        zeros = at(7168, 1, TOKENS)[:, 0, :]
        y_tok = at(13336, SLOTS // P, D)
        lat = at(0, KD, TOKENS)
        hl = at(2048, KD, TOKENS)
        sq = at(4096, KD, TOKENS)
        sq_gained = at(6144, KD, TOKENS)
        attn = at(4096, HEADS2, TOKENS)
        q_s = at(6144, GH, TOKENS)
        late = ring[:, RING_LATE:, :].rearrange("p a b -> p (a b)")
        v_s = [at(7168, TT, 512), late[:, 8192:9216].rearrange("p (a b) -> p a b", b=512)]
        g_s = [at(8192, GH, TOKENS), late[:, 9216:10240].rearrange("p (a b) -> p a b", b=TOKENS)]
        prod = [at(9216, 2, 4, GH * TOKENS), late[:, 0:8192].rearrange("p (a b c) -> p a b c", a=2, b=4)]
        gated_rstd = late[:, 10240:10496]
        lf = at(17408, 1, GH * TOKENS)[:, 0, :]
        kk = at(18432, 1, GH * TOKENS)[:, 0, :]
        dd = at(19456, 1, GH * TOKENS)[:, 0, :]
        b_s = x1[:, 0, :]
        smask = x1[:, 1, :]
        stt = sgT[:, :, :].rearrange("p a b -> p (a b)")
        chunk_state = stt.rearrange("p (d c v) -> p d c v", d=2, c=4)
        kdT = sb("kdT", [P, 2, TT, P])
        masked = sb("masked", [P, 2, TT, P])
        o_sq = sb("o_sq", [P, TOKENS])
        o_n = sb("o_n", [P, TOKENS])
        dec = sb("dec", [P, NG, 2, GH * NCH])
        up_s = at(4096, 2, 2, TOKENS)
        sg_s = at(5120, 2, TOKENS)
        act = at(8192, NB, TOKENS)
        o_tok = at(14000, TT, D)
        final_gain = at(16384, 1, D)[:, 0, :]
        ps = ctx.enter_context(nc.psum_tensor("ps", [P, 8, 512], f32))

        def halves_to(g, part):
            return 10 * g + 2 * PARTS[g].index(part) + 2

        def vec(name, i=0, n=1):
            return vecs[:, VEC[name] + i:VEC[name] + i + n]

        def col(i, n=1):
            return small[:, i:i + n]

        def kv_bank(d, c):
            i = {(0, 0): 0, (0, 2): 1, (1, 2): 2, (0, 1): 0, (1, 3): 1, (1, 1): 2}[d, c]
            return ps[:, 6 + c % 2, i * P:(i + 1) * P]

        order = tile_order()
        number = {t: n for n, t in enumerate(order)}

        def source(kind, i):
            def cols(w, c, rows=KD, width=512):
                return w[:, c:c + width].rearrange("(k p) n -> p k n", p=P), (rows, width)
            if kind == "w_in":
                return cols(a["w_in"], 512 * i)
            if kind in ("w_o", "hg_out"):
                return a[kind][512 * i:512 * i + 512, :].rearrange("(k p) n -> p k n", p=P), (4, 1024)
            if kind in ("gate", "up"):
                return a["w_" + kind][i].rearrange("(p k) n -> p k n", k=KD), (KD, 512)
            if kind == "down":
                return a["w_down"][i].rearrange("(k p) n -> p k n", p=P), (KF, 1024)
            if kind == "ada":
                return cols(a["w_ada"], 512 * i)
            if kind == "ctx":
                return cols(a["hg_in"], (1024, 2048, 3072)[i % 3] + 512 * (i // 3))
            if kind == "lat":
                return cols(a["hg_in"], HG_COLUMN[PARTS[i // 5][i % 5]] + 512 * (i // 5))
            if kind == "ffn_up":
                b, part = i // 2, i % 2
                return cols(a["ffn_up"], DFF * part + 512 * b, KD, min(512, DFF - 512 * b))
            half, part = i // 3, i % 3
            k0, kn = (0, 8, 16)[part], (8, 8, 6)[part]
            return (a["ffn_down"][P * k0:P * (k0 + kn), 512 * half:512 * half + 512]
                    .rearrange("(k p) n -> p k n", p=P)), (kn, 512)

        late_from = number["lat", 0]
        slot_of = [n % RING if n < late_from else (n - late_from) % RING_LATE for n in range(len(order))]
        before_it, loads, last_in = [], [], {}
        for n, place_ in enumerate(slot_of):
            before_it.append(last_in.get(place_))
            last_in[place_] = n
            loads.append(1 + (loads[before_it[n]] if before_it[n] is not None else 0))

        def slot(kind, i):
            k, w = source(kind, i if isinstance(i, int) else 0)[1]
            return ring[:, slot_of[number[kind, i]], 0:k * w].rearrange("p (k n) -> p k n", n=w)

        def full(kind, i):
            n = number[kind, i]
            return sem(f"tile_loaded_{slot_of[n]}"), 16 * loads[n]

        dense_index = {}
        for t in order:
            if t[0] not in ("gate", "up", "down", "lat", "hg_out"):
                dense_index[t] = len(dense_index) + 1

        def freed(n):
            kind, i = order[n]
            if kind in ("gate", "up", "down"):
                return sem(kind + "_used"), i + 1
            if kind == "lat":
                return sem("lat_half_done"), 2 * i + 2
            if kind == "hg_out":
                return sem("hg_done"), 4 * i + 4
            return sem("dense_used"), dense_index[order[n]]

        def dense_wait(eng, kind, i):
            eng.wait_ge(sem("dense_used"), dense_index[kind, i])

        def wait(eng, name, value):
            if not isinstance(value, int) or value > 0:
                eng.wait_ge(sem(name), value)

        block = ctx.enter_context(nc.Block())

        @block.sync
        def _(sp):
            def load(n):
                kind, i = order[n]
                src, (k, w) = source(kind, i)
                if before_it[n] is not None:
                    sp.wait_ge(*freed(before_it[n]))
                sp.dma_start(slot(kind, i), src).then_inc(sem(f"tile_loaded_{slot_of[n]}"), 16)

            sp.dma_start(x1[:, :, :], a["x"]).then_inc(sem("x_loaded"), 16)
            n = 0
            while n < len(order):
                kind, i = order[n]
                if kind != "gate":
                    load(n)
                    n += 1
                    continue
                e0, e1 = next(r for r in MOE_RANGES if r[0] == i)
                for m in range(n, n + RING):
                    load(m)
                with sp.Fori(1, (e1 - e0) // 2) as it:
                    for u in range(2):
                        for j, what in enumerate(("gate", "up", "down")):
                            src = a["w_" + what].rearrange(
                                "e (k p) n -> e p k n" if what == "down" else "e (p k) n -> e p k n", p=P)
                            m = n + 3 * u + j
                            sp.wait_ge(sem(what + "_used"), it * 2 + (e0 + u - 1))
                            sp.dma_start(slot(what, e0 + u), src[it * 2 + (e0 + u)]).then_inc(
                                sem(f"tile_loaded_{m % RING}"), 16)
                n += 3 * (e1 - e0)
            for t in range(TT):
                sp.wait_ge(sem("out_ready"), t + 1)
                sp.dma_start(out[0, t * P:(t + 1) * P, :], o_tok[:, t, :]).then_inc(sem("out_stored"), 16)
            sp.wait_ge(sem("out_stored"), 16 * TT)

        @block.tensor
        def _(pe):
            mm, tr = nc.tensor.matmul, nc.tensor.transpose

            def tile(kind, i):
                pe.wait_ge(*full(kind, i))
                return slot(kind, i)

            def release(ins, kind, i):
                ins.then_inc(sem("dense_used"), 1)

            def feature_major(w, acts, bank, blocks=4):
                for f in range(blocks):
                    for k in range(KD):
                        last = mm(ps[:, bank + f // 2, (f % 2) * 256:(f % 2) * 256 + 256],
                                  w[:, k, f * P:(f + 1) * P], acts[:, k, :], start=k == 0, stop=k == KD - 1)
                return last

            def token_major(w, acts, bank):
                for t in range(TT):
                    for k in range(KD):
                        last = mm(ps[:, bank + t, :], acts[:, k, t * P:(t + 1) * P], w[:, k, :],
                                  start=k == 0, stop=k == KD - 1)
                return last

            def transposed(src, bank, strided=False):
                for k in range(KD):
                    for t in range(TT):
                        piece = src[:, t, k::KD] if strided else src[:, t, k * P:(k + 1) * P]
                        o = (k % 2) * 256 + t * P
                        last = tr(ps[:, bank + k // 2, o:o + P], piece, ident)
                return last

            def ada(i):
                if i:
                    pe.wait_ge(sem("ada_copied"), i)
                    if i > 1:
                        pe.wait_ge(sem("mod_copied"), i - 1)
                    for f in range(4):
                        last = mm(ps[:, 7, f * P:(f + 1) * P], ada_s[:, f * P:(f + 1) * P], fold_all,
                                  start=True, stop=True)
                    last.then_inc(sem("ada_folded"), 1)
                if i == 12:
                    return
                w = tile("ada", i)
                for k in range(2):
                    for q in range(4):
                        last = mm(ps[32 * q:32 * q + 32, 6, :], csil[:, 2 * q + k, :], w[:, 2 * q + k, :],
                                  start=k == 0, stop=k == 1)
                release(last, "ada", i)

            pe.wait_ge(sem("consts_loaded"), 16)
            pe.wait_ge(sem("token_scaled"), TT)
            transposed(xn, 0).then_inc(sem("h1_transposed"), 1)
            pe.wait_ge(sem("h1_ready"), KD)
            release(token_major(tile("w_in", 0), hT, 4), "w_in", 0)
            release(token_major(tile("w_in", 1), hT, 6), "w_in", 1)
            pe.wait_ge(sem("qk_rotated"), 1)
            release(token_major(tile("w_in", 2), hT, 4), "w_in", 2)
            for h in range(HEADS1):
                for t in range(TT):
                    last = tr(ps[:, h // 2, (h % 2) * 256 + t * P:(h % 2) * 256 + t * P + P],
                              qk_rot[:, 0, t, h * P:(h + 1) * P], ident)
            last.then_inc(sem("qk_transposed"), 1)
            pe.wait_ge(sem("qk_rotated"), 2)
            for h in range(HEADS1):
                for t in range(TT):
                    last = tr(ps[:, 2 + h // 2, (h % 2) * 256 + t * P:(h % 2) * 256 + t * P + P],
                              qk_rot[:, 1, t, h * P:(h + 1) * P], ident)
            last.then_inc(sem("qk_transposed"), 1)
            release(token_major(tile("w_in", 3), hT, 6), "w_in", 3)
            pe.wait_ge(sem("qkT_ready"), 2)
            for h in range(HEADS1):
                mm(ps[:, h, 0:256], qkT[:, 1, h, 0:P], qkT[:, 0, h, :], start=True, stop=True)
                mm(ps[:, h, 256:384], qkT[:, 1, h, P:256], qkT[:, 0, h, P:256], start=True,
                   stop=True).then_inc(sem("scores_done"), 1)
            pe.wait_ge(sem("v_ready"), 1)
            release(feature_major(tile("w_in", 4), hT, 4), "w_in", 4)
            pe.wait_ge(sem("decayed"), HEADS1)
            for t in range(TT):
                for h in range(HEADS1):
                    o = ps[:, t, h * P:(h + 1) * P]
                    mm(o, probs[:, h, t * P:(t + 1) * P], v_tok[:, 0, h * P:(h + 1) * P], start=True, stop=t == 0)
                    if t == 1:
                        mm(o, probs[:, h, 256:384], v_tok[:, 1, h * P:(h + 1) * P], start=False, stop=True)
            pe.wait_ge(sem("g_ready"), 1)
            release(feature_major(tile("w_in", 5), hT, 6), "w_in", 5)
            pe.wait_ge(sem("gb_ready"), 1)
            release(feature_major(tile("w_in", 6), hT, 4), "w_in", 6)
            pe.wait_ge(sem("csil_ready"), 1)
            pe.wait_ge(sem("gc_ready"), 1)
            ada(0)
            pe.wait_ge(sem("ret_ready"), TT)
            for f in range(4):
                for t in range(TT):
                    last = tr(ps[:, 2 + f // 2, (f % 2) * 256 + t * P:(f % 2) * 256 + t * P + P],
                              ret[:, t, f * P:(f + 1) * P], ident)
            last.then_inc(sem("ret_transposed"), 1)
            ada(1)
            ada(2)
            pe.wait_ge(sem("ada_copied"), 3)
            pe.wait_ge(sem("mod_copied"), 2)
            pe.wait_ge(sem("mix_ret_ready"), 4)
            pe.wait_ge(sem("mix_conv_ready"), 4)
            for i in range(2):
                w = tile("w_o", i)
                for t in range(TT):
                    for half in range(2):
                        for k in range(4):
                            last = mm(ps[:, 4 + 2 * t + half, :], mixT[:, 4 * i + k, t * P:(t + 1) * P],
                                      w[:, k, half * 512:half * 512 + 512], start=i + k == 0, stop=i == 1 and k == 3)
                release(last, "w_o", i)

            pe.wait_ge(sem("x1_ready"), TT)
            ada(3)
            pe.wait_ge(sem("token_scaled"), 2 * TT)
            transposed(xn, 0, strided=True).then_inc(sem("h2_transposed"), 1)
            ada(4)
            pe.wait_ge(sem("h2_ready"), KD)
            pe.wait_ge(sem("router_loaded"), 48)
            for t in range(TT):
                for k in range(KD):
                    last = mm(ps[:, 4, t * 72:t * 72 + 72], h2T[:, k, t * P:(t + 1) * P], router_w[:, k, :],
                              start=k == 0, stop=k == KD - 1)
            last.then_inc(sem("router_done"), 1)
            for i in (5, 6, 7):
                ada(i)
            pe.wait_ge(sem("assigned_ready"), 1)
            mm(ps[:, 5, 0:64], before, assigned[:, 0, :], start=True, stop=True)
            mm(ps[:, 5, 64:128], ones, assigned[:, 0, :], start=True, stop=False)
            mm(ps[:, 5, 64:128], before, assigned[:, 1, :], start=False, stop=True)
            mm(ps[:, 5, 128:192], ones, assigned[:, 0, :], start=True, stop=False)
            mm(ps[:, 5, 128:192], ones, assigned[:, 1, :], start=False, stop=True).then_inc(sem("counted"), 1)
            for i in (8, 9, 10):
                ada(i)
            pe.wait_ge(sem("sel_ready"), 1)
            for k in range(KD):
                if k >= 4:
                    pe.wait_ge(sem("gathered"), k - 3)
                for t in range(TT):
                    last = mm(ps[:, k % 4, :], xn[:, t, k::KD], sel[:, t, :], start=t == 0, stop=t == TT - 1)
                last.then_inc(sem("gather_done"), 1)
            for i in (11, 12):
                ada(i)
            pe.wait_ge(sem("gated_ready"), 1)
            for s in range(SLOTS // P):
                for t in range(TT):
                    last = tr(ps[:, 4 + s // 2, (s % 2) * 256 + t * P:(s % 2) * 256 + t * P + P],
                              gated[:, t, s * P:(s + 1) * P], ident)
            last.then_inc(sem("gated_transposed"), 1)
            pe.wait_ge(sem("gathered"), KD)

            def ring_tile(n, width):
                return ring[:, n % RING, :].rearrange("p (k n) -> p k n", n=width)

            def gate_up(u, n):
                gate, up = ring_tile(n, FF), ring_tile(n + 1, FF)
                for k in range(KD // 2):
                    for q, (w, kk) in enumerate(((gate, k), (gate, KD // 2 + k), (up, k), (up, KD // 2 + k))):
                        last = mm(ps[32 * q:32 * q + 32, 0, :], win[:, u, kk, :], w[:, kk, :],
                                  start=k == 0, stop=k == KD // 2 - 1)
                        if k == KD // 2 - 1 and q == 1:
                            last_gate = last
                return last_gate, last

            def down(u, n):
                w = ring_tile(n + 2, D)
                for k in range(KF // 2):
                    for q in range(4):
                        kk = KF // 2 * (q % 2) + k
                        last = mm(ps[32 * q:32 * q + 32, 2, :], hidden[:, u, kk, :],
                                  w[:, kk, (q // 2) * 512:(q // 2) * 512 + 512], start=k == 0, stop=k == KF // 2 - 1)
                return last

            def fold(src, bank, matrix=None):
                for f in range(4):
                    last = mm(ps[:, bank, f * P:(f + 1) * P], src[:, f * P:(f + 1) * P],
                              fold_pairs if matrix is None else matrix, start=True, stop=True)
                return last

            def loaded(n0, u, j, it):
                n = n0 + 3 * u + j
                return sem(f"tile_loaded_{n % RING}"), (it + n // RING + 1) * 16

            def pe_fast(e0, e1):
                n0 = number["gate", e0]

                def gate_up_of(u, it):
                    e = it * 2 + (e0 + u)
                    pe.wait_ge(*loaded(n0, u, 0, it))
                    pe.wait_ge(*loaded(n0, u, 1, it))
                    wait(pe, "win_ready", e + 1)
                    wait(pe, "gu_copied", e)
                    last_gate, last_up = gate_up(u, n0 + 3 * u)
                    last_gate.then_inc(sem("gate_used"), 1)
                    last_up.then_inc(sem("up_used"), 1)

                def fold_gate_up(u, it):
                    e = it * 2 + (e0 + u)
                    wait(pe, "gu_copied", e + 1)
                    wait(pe, "hidden_ready", e)
                    fold(gu_s, 1).then_inc(sem("gu_folded"), 1)

                def down_of(u, it):
                    e = it * 2 + (e0 + u)
                    pe.wait_ge(*loaded(n0, u, 2, it))
                    wait(pe, "hidden_ready", e + 1)
                    wait(pe, "y_copied", e)
                    down(u, n0 + 3 * u).then_inc(sem("down_used"), 1)

                def fold_down(u, it):
                    e = it * 2 + (e0 + u)
                    wait(pe, "y_copied", e + 1)
                    wait(pe, "y_written", e)
                    fold(y_s, 3).then_inc(sem("y_folded"), 1)

                def step(u, it, more=True):
                    after = (1, it) if u == 0 else (0, it + 1)
                    if more:
                        gate_up_of(*after)
                    down_of(u, it)
                    if more:
                        fold_gate_up(*after)
                    fold_down(u, it)

                gate_up_of(0, 0)
                fold_gate_up(0, 0)
                step(0, 0)
                step(1, 0)
                if e1 - e0 > 4:
                    with pe.Fori(1, (e1 - e0) // 2 - 1) as it:
                        step(0, it)
                        step(1, it)
                step(0, (e1 - e0) // 2 - 1)
                step(1, (e1 - e0) // 2 - 1, more=False)

            def pe_slow(e0, e1):
                n0 = number["gate", e0]

                def expert(u, it):
                    for j in range(3):
                        pe.wait_ge(*loaded(n0, u, j, it))
                    for r in range(ROUNDS):
                        q = (it * 2 + (e0 + u)) * ROUNDS + r
                        wait(pe, "win_ready", q + 1)
                        wait(pe, "gu_copied", q)
                        last_gate, last_up = gate_up(u, n0 + 3 * u)
                        if r == ROUNDS - 1:
                            last_gate.then_inc(sem("gate_used"), 1)
                        last_up.then_inc(sem("up_used" if r == ROUNDS - 1 else "round_up"), 1)
                        wait(pe, "gu_copied", q + 1)
                        wait(pe, "hidden_ready", q)
                        fold(gu_s, 1).then_inc(sem("gu_folded"), 1)
                        wait(pe, "hidden_ready", q + 1)
                        wait(pe, "y_copied", q)
                        down(u, n0 + 3 * u).then_inc(sem("down_used" if r == ROUNDS - 1 else "round_down"), 1)
                        wait(pe, "y_copied", q + 1)
                        wait(pe, "y_written", q)
                        fold(y_s, 3).then_inc(sem("y_folded"), 1)

                for u in range(2):
                    expert(u, 0)
                with pe.Fori(1, (e1 - e0) // 2) as it:
                    for u in range(2):
                        expert(u, it)

            def moe(e0, e1):
                flag = pe.value_load(many[0:1, 0:1], min_val=0, max_val=1)
                with pe.If(flag < 1):
                    pe_fast(e0, e1)
                with pe.Else():
                    pe_slow(e0, e1)

            pe.wait_ge(sem("starts_ready"), 1)
            def context(g, stage):
                if stage == "f0" and g == 0:
                    pe.wait_ge(sem("token_scaled"), 3 * TT)
                    pe.wait_ge(sem("mod_copied"), 12)
                    pe.wait_ge(sem("sgT_ready"), 1)
                    transposed(c_raw, 4).then_inc(sem("hc_transposed"), 1)
                    pe.wait_ge(sem("hc_ready"), KD)
                if stage == "f0":
                    wait(pe, "ctx_state_ready", GH * g)
                    release(feature_major(tile("ctx", 3 * g), hcT, 4), "ctx", 3 * g)
                elif stage == "f1":
                    release(feature_major(tile("ctx", 3 * g + 1), hcT, 6), "ctx", 3 * g + 1)
                elif stage == "v":
                    pe.wait_ge(sem("ctx_f_read"), 2 * g + 1)
                    release(token_major(tile("ctx", 3 * g + 2), hcT, 4), "ctx", 3 * g + 2)
                else:
                    pe.wait_ge(sem("ctx_kd_ready"), 2 * (g + 1))
                    pe.wait_ge(sem("ctx_v_ready"), g + 1)
                    for h in range(GH):
                        wait(pe, "ctx_state_ready", GH * g + h)
                        for d in range(2):
                            for t in range(TT):
                                last = tr(ps[:, 4, (2 * d + t) * P:(2 * d + t + 1) * P],
                                          c_p[:, d, h, t * P:(t + 1) * P], ident)
                        last.then_inc(sem("ctx_kd_transposed"), 1)
                        pe.wait_ge(sem("ctx_kdT_ready"), GH * g + h + 1)
                        for d in range(2):
                            for t in range(TT):
                                last = mm(ps[:, 5, d * P:(d + 1) * P], c_kT[:, d, t, :], c_v[:, t, h * P:(h + 1) * P],
                                          start=t == 0, stop=t == 1)
                        last.then_inc(sem("ctx_state_done"), 1)

            for r, (e0, e1) in enumerate(MOE_RANGES):
                moe(e0, e1)
                if r < len(CTX_STAGES):
                    context(r // 4, CTX_STAGES[r])

            pe.wait_ge(sem("y_complete"), 1)
            for s in range(SLOTS // P):
                if s >= 2:
                    pe.wait_ge(sem("y_tok_ready"), s - 1)
                for k in range(KD):
                    last = tr(ps[:, 2 * (s % 2) + k // 4, (k % 4) * P:(k % 4 + 1) * P],
                              YT[:, 2 * (k % 4) + k // 4, s * P:(s + 1) * P], ident)
                last.then_inc(sem("y_transposed"), 1)
            pe.wait_ge(sem("y_tok_ready"), SLOTS // P)
            pe.wait_ge(sem("ctx_state_ready"), HEADS2)

            def combine(b):
                for k in (2 * b, 2 * b + 1):
                    o = ps[:, 4 + b, (k % 2) * 256:(k % 2) * 256 + 256]
                    for s in range(SLOTS // P):
                        mm(o, y_tok[:, s, k * P:(k + 1) * P], sgT[:, s, :], start=s == 0, stop=False)
                    for t in range(TT):
                        last = mm(o[:, t * P:(t + 1) * P], x1[:, t, k * P:(k + 1) * P], ident, start=False, stop=t == 1)
                last.then_inc(sem("combined"), 1)

            def sum_squares(n, where):
                pe.wait_ge(sem("norm_squared"), n + 1)
                for k in (2 * (n % 4), 2 * (n % 4) + 1):
                    for src, bank in where:
                        last = mm(ps[:, bank, 0:TOKENS], ones, src[:, k, :], start=k == 0, stop=k == KD - 1)
                if n % 4 == 3:
                    last.then_inc(sem("norm_summed"), 1)

            combine(0)
            for b in range(4):
                if b < 3:
                    combine(b + 1)
                sum_squares(b, ((sq, 0), (sq_gained, 1)))

            def project(j):
                g, i, half = j // 10, (j % 10) // 2, j % 2
                w = tile("lat", 5 * g + i)
                if j >= 3:
                    pe.wait_ge(sem("lat_read"), j - 2)
                if PARTS[g][i] == "value":
                    for k in range(KD):
                        last = mm(ps[:, j % 3, :], hl[:, k, half * P:(half + 1) * P], w[:, k, :],
                                  start=k == 0, stop=k == KD - 1)
                else:
                    for f in (2 * half, 2 * half + 1):
                        for k in range(KD):
                            if j == 0 and f == 0:
                                pe.wait_ge(sem("hl_ready"), k + 1)
                            last = mm(ps[:, j % 3, (f % 2) * 256:(f % 2) * 256 + 256], w[:, k, f * P:(f + 1) * P],
                                      hl[:, k, :], start=k == 0, stop=k == KD - 1)
                last.then_inc(sem("lat_half_done"), 1)

            def scores(n):
                g, h = n // GH, n % GH
                pe.wait_ge(sem("prod_ready"), 2 * (g + 1))
                wait(pe, "masked_ready", n)
                for d in range(2):
                    for c in range(NCH):
                        lo = (c % 2) * CHUNK2
                        k0, HC = h * TOKENS + c * CHUNK2, CHUNK2 // 2
                        for half in range(2):
                            o = ((c // 2) * 2 + d) * CHUNK2 + half * HC
                            m0, mn = (half * HC, HC) if half == d else (0, CHUNK2)
                            last = mm(ps[lo + m0:lo + m0 + mn, 4, o:o + HC],
                                      prod[g][:, d, 1, k0 + m0:k0 + m0 + mn],
                                      prod[g][:, d, 0, k0 + half * HC:k0 + (half + 1) * HC], start=True, stop=True)
                last.then_inc(sem("s_done"), 1)
                wait(pe, "kdT_ready", n)
                for d in range(2):
                    for t in range(TT):
                        last = tr(ps[:, 5, (2 * d + t) * P:(2 * d + t + 1) * P],
                                  prod[g][:, d, 3, h * TOKENS + t * P:h * TOKENS + (t + 1) * P], ident)
                last.then_inc(sem("kd_transposed"), 1)

            def updates(n):
                g, h = n // GH, n % GH
                pe.wait_ge(sem("kdT_ready"), n + 1)
                pe.wait_ge(sem("lat_read"), halves_to(g, "value"))
                wait(pe, "states_ready", 2 * n)
                for d in range(2):
                    for j in range(NCH - 1):
                        c = j if d == 0 else NCH - 1 - j
                        lo = (c % 2) * CHUNK2
                        last = mm(kv_bank(d, c), kdT[lo:lo + CHUNK2, d, c // 2, :],
                                  v_s[g][lo:lo + CHUNK2, c // 2, h * P:(h + 1) * P], start=True, stop=True)
                last.then_inc(sem("kv_done"), 1)

            def outputs(n):
                g, h = n // GH, n % GH
                pe.wait_ge(sem("masked_ready"), n + 1)
                wait(pe, "readout_done", n)
                o = ps[:, 3, 0:TOKENS]
                for t in range(TT):
                    for d in range(2):
                        mm(o[:, t * P:(t + 1) * P], v_s[g][:, t, h * P:(h + 1) * P], masked[:, d, t, :],
                           start=d == 0 and t == 0, stop=False, skip_group_check=True)
                pe.wait_ge(sem("states_ready"), 2 * (n + 1))
                for d in range(2):
                    for j in range(NCH):
                        c = j if d == 0 else NCH - 1 - j
                        s = state[:, n, d, :] if j == 0 else chunk_state[:, d, j, :]
                        last = mm(o[:, c * CHUNK2:(c + 1) * CHUNK2], s,
                                  prod[g][:, d, 2, h * TOKENS + c * CHUNK2:h * TOKENS + (c + 1) * CHUNK2],
                                  start=False, stop=d == 1 and j == NCH - 1, skip_group_check=True)
                last.then_inc(sem("o_done"), 1)

            def sums(n):
                pe.wait_ge(sem("o_squared"), n + 1)
                mm(ps[:, 3, 256:512], ones, o_sq[:, :], start=True, stop=True).then_inc(sem("o_summed"), 1)

            for j in range(14):
                project(j)
            scores(0)
            project(14)
            updates(0)
            project(15)
            for n in range(GH):
                outputs(n)
                if n < GH - 1:
                    scores(n + 1)
                if n < 2:
                    project(16 + 2 * n)
                if n < GH - 1:
                    updates(n + 1)
                sums(n)
                if n < 2:
                    project(17 + 2 * n)
            scores(GH)
            updates(GH)

            def hg_out(i, b):
                w = tile("hg_out", i)
                for f in (2 * b, 2 * b + 1):
                    for h in range(GH):
                        last = mm(ps[:, b if i else b % 3, (f % 2) * 256:(f % 2) * 256 + 256], w[:, h, f * P:(f + 1) * P],
                                  attn[:, GH * i + h, :], start=h == 0, stop=h == GH - 1)
                last.then_inc(sem("hg_done"), 1)

            for n in range(GH, HEADS2):
                if n < HEADS2 - 1:
                    scores(n + 1)
                outputs(n)
                if n < HEADS2 - 1:
                    updates(n + 1)
                sums(n)
                if n == GH:
                    pe.wait_ge(sem("lat_read"), 20)
                wait(pe, "hg_added", n - GH - 2)
                hg_out(0, n - GH)
            pe.wait_ge(sem("readout_done"), HEADS2)
            pe.wait_ge(sem("hg_added"), 4)
            hg_out(1, 0)
            for b in range(4):
                if b < 3:
                    hg_out(1, b + 1)
                sum_squares(4 + b, ((sq_gained, 4),))

            for b in range(NB):
                i, f = b // 4, b % 4
                for part in range(2):
                    w = tile("ffn_up", 2 * i + part) if f == 0 else slot("ffn_up", 2 * i + part)
                    m = 2 * b + part
                    if m >= 4:
                        pe.wait_ge(sem("conv_read"), m - 3)
                    for k in range(KD):
                        if m == 0:
                            pe.wait_ge(sem("hl_ready"), KD + k + 1)
                        last = mm(ps[:, m % 4, 0:256], w[:, k, f * P:(f + 1) * P], hl[:, k, :],
                                  start=k == 0, stop=k == KD - 1)
                    last.then_inc(sem("up_done"), 1) if not (f == 3 or b == NB - 1) else release(last, "ffn_up", 2 * i + part)

            def back(half):
                pe.wait_ge(sem("last_residual"), half + 1)
                for t in range(TT):
                    for k in range(4):
                        last = tr(ps[:, 4 + 2 * t + half, k * P:(k + 1) * P], lat[:, 4 * half + k, t * P:(t + 1) * P],
                                  ident)
                    last.then_inc(sem("out_transposed"), 1)

            for half in range(2):
                for part in range(3):
                    w = tile("ffn_down", 3 * half + part)
                    k0, kn = (0, 8, 16)[part], (8, 8, 6)[part]
                    pe.wait_ge(sem("act_ready"), k0 + kn)
                    if half == 0 and part == 0:
                        pe.wait_ge(sem("hl_ready"), 2 * KD)
                    if half == 1 and part == 0:
                        pe.wait_ge(sem("act_ready"), NB)
                    for f in range(4):
                        for k in range(kn):
                            last = mm(ps[:, 4 - 4 * half + f, 0:TOKENS], w[:, k, f * P:(f + 1) * P], act[:, k0 + k, :],
                                      start=k0 + k == 0, stop=k0 + k == NB - 1)
                    release(last, "ffn_down", 3 * half + part)
                    if half == 1 and part == 1:
                        back(0)
            back(1)

        @block.scalar
        def _(act_e):
            af = nc.scalar.activation
            steps = [0]

            def link(ins):
                steps[0] += 1
                ins.then_inc(sem("scalar_step"), 1)
                act_e.wait_ge(sem("scalar_step"), steps[0])

            act_e.dma_start(consts[:, :, :], a["consts"]).then_inc(sem("consts_loaded"), 16)
            act_e.dma_start(vecs[:, :], a["vecs"]).then_inc(sem("vecs_loaded"), 16)
            act_e.dma_start(rope, a["rope"]).then_inc(sem("rope_loaded"), 16)
            act_e.dma_start(decay, a["decay"]).then_inc(sem("decay_loaded"), 16)
            act_e.dma_start(hmask[:, :, :], a["hmask"]).then_inc(sem("hmask_loaded"), 16)

            def rsqrt(dst, src):
                link(af(dst, src, ACT.Ln))
                return af(dst, dst, ACT.Exp, scale=-0.5)

            act_e.wait_ge(sem("x_loaded"), 16)
            for t in range(TT):
                last = af(xn[:, t, :], x1[:, t, :], ACT.Square, accum_out=col(t))
            last.then_inc(sem("token_sums"), 1)
            act_e.wait_ge(sem("token_mean"), 1)
            rsqrt(col(2, 2), col(2, 2)).then_inc(sem("token_rstd"), 1)
            act_e.wait_ge(sem("h1_transposed"), 1)
            act_e.wait_ge(sem("vecs_loaded"), 16)
            for k in range(KD):
                af(hT[:, k, :], ps[:, k // 2, (k % 2) * 256:(k % 2) * 256 + 256], ACT.Copy,
                   scale=vec("norm1", k)).then_inc(sem("h1_ready"), 1)
            def ada(i):
                if i < 12:
                    dense_wait(act_e, "ada", i)
                    if i:
                        act_e.wait_ge(sem("ada_folded"), i)
                    af(ada_s, ps[:, 6, :], ACT.Copy).then_inc(sem("ada_copied"), 1)
                if i:
                    act_e.wait_ge(sem("ada_folded"), i)
                    af(mod[:, 4 * i - 4:4 * i, :], ps[:, 7, :].rearrange("p (f n) -> p f n", f=4)[:, :, 0:2],
                       ACT.Copy).then_inc(sem("mod_copied"), 1)

            act_e.wait_ge(sem("csil_zeroed"), 1)
            for j, name in enumerate(("c", "c_ctx")):
                last = af(csil[:, :, j], vec(name, 0, KD), ACT.Silu)
            last.then_inc(sem("csil_ready"), 1)
            dense_wait(act_e, "w_in", 2)
            af(v_tok, ps[:, 4:6, :], ACT.Copy).then_inc(sem("v_ready"), 1)
            for j in range(2):
                act_e.wait_ge(sem("qk_transposed"), j + 1)
                af(qkT[:, j].rearrange("p (b h) n -> p b (h n)", b=2), ps[:, 2 * j:2 * j + 2, :],
                   ACT.Copy).then_inc(sem("qkT_ready"), 1)
            dense_wait(act_e, "w_in", 3)
            af(g_tok, ps[:, 6:8, :], ACT.Silu).then_inc(sem("g_ready"), 1)
            dense_wait(act_e, "w_in", 4)
            af(gb_s.rearrange("p (b f) n -> p b (f n)", b=2), ps[:, 4:6, :], ACT.Copy).then_inc(sem("gb_ready"), 1)
            dense_wait(act_e, "w_in", 5)
            af(gc_s.rearrange("p (b f) n -> p b (f n)", b=2), ps[:, 6:8, :], ACT.Copy).then_inc(sem("gc_ready"), 1)
            act_e.wait_ge(sem("gn_var"), 1)
            rsqrt(col(8, 8), col(8, 8)).then_inc(sem("gn_rstd"), 1)
            ada(0)
            act_e.wait_ge(sem("ret_transposed"), 1)
            for f in range(4):
                af(mixT[:, f, :], ps[:, 2 + f // 2, (f % 2) * 256:(f % 2) * 256 + 256], ACT.Copy,
                   scale=vec("ret_gn", f)).then_inc(sem("mix_ret_ready"), 1)

            ada(1)
            ada(2)

            act_e.wait_ge(sem("x1_ready"), TT)
            for t in range(TT):
                last = af(xn[:, t, :], x1[:, t, :], ACT.Square, accum_out=col(t))
            last.then_inc(sem("token_sums"), 1)
            act_e.dma_start(router_w, a["router_w"]).then_inc(sem("router_loaded"), 16)
            act_e.dma_start(router_b, a["router_b"]).then_inc(sem("router_loaded"), 16)
            act_e.dma_start(iota, a["iota"]).then_inc(sem("router_loaded"), 16)
            act_e.wait_ge(sem("token_mean"), 2)
            rsqrt(col(2, 2), col(2, 2)).then_inc(sem("token_rstd"), 1)
            ada(3)
            act_e.wait_ge(sem("h2_transposed"), 1)
            for k in range(KD):
                af(h2T[:, k, :], ps[:, k // 2, (k % 2) * 256:(k % 2) * 256 + 256], ACT.Copy,
                   scale=vec("norm2", k)).then_inc(sem("h2_ready"), 1)
            ada(4)
            for j in range(2):
                act_e.wait_ge(sem("softmax_in"), j + 1)
                for t in range(TT):
                    last = af(rt[:, t, 8 + 40 * j:16 + 40 * j], rt[:, t, 8 + 40 * j:16 + 40 * j], ACT.Exp,
                              accum_out=rt[:, t, 36 + 40 * j:37 + 40 * j])
                last.then_inc(sem("softmax_exp"), 1)
                for i in ((5, 6), (7, 8, 9, 10))[j]:
                    ada(i)
            for k in range(KD):
                act_e.wait_ge(sem("gather_done"), k + 1)
                af(XgT[:, k, 0:SLOTS], ps[:, k % 4, :], ACT.Copy, scale=vec("norm2", k)).then_inc(sem("gathered"), 1)
            for i in (11, 12):
                ada(i)
            act_e.wait_ge(sem("gated_transposed"), 1)
            af(sgT[:, :, :].rearrange("p (b s) n -> p b (s n)", b=2), ps[:, 4:6, :], ACT.Copy).then_inc(
                sem("sgT_ready"), 1)

            def copy_gu(q):
                wait(act_e, "gu_folded", q)
                af(gu_s, ps[:, 0, :], ACT.Copy).then_inc(sem("gu_copied"), 1)

            def silu(q):
                wait(act_e, "gu_folded", q + 1)
                wait(act_e, "hidden_ready", q)
                af(silu_g, ps[:, 1, :].rearrange("p (f n) -> p f n", f=KF)[:, :, 0:WIN], ACT.Silu).then_inc(
                    sem("silu_ready"), 1)

            def store(e, r, q):
                begin = act_e.value_load(starts[0:1, r, bass.ds(e, 1)], min_val=0, max_val=SLOTS)
                wait(act_e, "y_folded", q + 1)
                wait(act_e, "y_written", q)
                for f in range(4):
                    last = af(YT[:, 2 * f:2 * f + 2, bass.ds(begin, WIN)],
                              ps[:, 3, f * P:f * P + 2 * WIN].rearrange("p (a b) -> p a b", b=WIN), ACT.Copy)
                last.then_inc(sem("y_written"), 1)

            def act_fast(e0, e1):
                def step(u, it, more=True):
                    e = it * 2 + (e0 + u)
                    if more:
                        wait(act_e, "up_used", e + 2)
                        copy_gu(e + 1)
                        silu(e + 1)
                    store(e, 0, e)

                wait(act_e, "up_used", e0 + 1)
                copy_gu(e0)
                silu(e0)
                step(0, 0)
                step(1, 0)
                if e1 - e0 > 4:
                    with act_e.Fori(1, (e1 - e0) // 2 - 1) as it:
                        step(0, it)
                        step(1, it)
                step(0, (e1 - e0) // 2 - 1)
                step(1, (e1 - e0) // 2 - 1, more=False)

            def act_slow(e0, e1):
                def expert(u, it):
                    e = it * 2 + (e0 + u)
                    for r in range(ROUNDS):
                        q = e * ROUNDS + r
                        if r == ROUNDS - 1:
                            wait(act_e, "up_used", e + 1)
                        else:
                            wait(act_e, "round_up", e * (ROUNDS - 1) + (r + 1))
                        copy_gu(q)
                        silu(q)
                        store(e, r, q)

                for u in range(2):
                    expert(u, 0)
                with act_e.Fori(1, (e1 - e0) // 2) as it:
                    for u in range(2):
                        expert(u, it)

            def moe(e0, e1):
                flag = act_e.value_load(many[0:1, 0:1], min_val=0, max_val=1)
                with act_e.If(flag < 1):
                    act_fast(e0, e1)
                with act_e.Else():
                    act_slow(e0, e1)

            act_e.wait_ge(sem("starts_ready"), 1)
            moe(*MOE_RANGES[0])

            act_e.wait_ge(sem("lb_in"), 1)
            af(vec("lb", 0, 32), vec("lb", 0, 32), ACT.Exp).then_inc(sem("lb_exp"), 1)
            act_e.wait_ge(sem("ctx_loaded"), 16)
            for t in range(TT):
                last = af(hcT.rearrange("p a b -> p (a b)")[:, t * D:(t + 1) * D], c_raw[:, t, :], ACT.Square,
                          accum_out=col(t))
            last.then_inc(sem("token_sums"), 1)
            act_e.wait_ge(sem("token_mean"), 3)
            rsqrt(col(2, 2), col(2, 2)).then_inc(sem("token_rstd"), 1)
            act_e.wait_ge(sem("hc_transposed"), 1)
            act_e.wait_ge(sem("mod_ready"), 1)
            for k in range(KD):
                af(hcT[:, k, :], ps[:, 4 + k // 2, (k % 2) * 256:(k % 2) * 256 + 256], ACT.Identity,
                   scale=scales[:, 0, k:k + 1], bias=mod[:, k, 1:2]).then_inc(sem("hc_ready"), 1)

            def context(g, stage):
                if stage in ("f0", "f1"):
                    d = int(stage[1])
                    dense_wait(act_e, "ctx", 3 * g + d)
                    wait(act_e, "ctx_kd_ready", 2 * g + d)
                    af(c_f.rearrange("p (b f) n -> p b (f n)", b=2), ps[:, 4 + 2 * d:6 + 2 * d, :],
                       ACT.Sigmoid).then_inc(sem("ctx_f_read"), 1)
                elif stage == "v":
                    dense_wait(act_e, "ctx", 3 * g + 2)
                    wait(act_e, "ctx_state_done", GH * g)
                    af(c_v, ps[:, 4:6, :], ACT.Copy).then_inc(sem("ctx_v_ready"), 1)
                else:
                    for n in range(GH * g, GH * g + GH):
                        act_e.wait_ge(sem("ctx_kd_transposed"), n + 1)
                        wait(act_e, "ctx_state_done", n)
                        af(c_kT.rearrange("p a b c -> p (a b c)"), ps[:, 4, :], ACT.Copy).then_inc(
                            sem("ctx_kdT_ready"), 1)
                        act_e.wait_ge(sem("ctx_state_done"), n + 1)
                        af(state[:, n].rearrange("p a b -> p (a b)"), ps[:, 5, 0:256], ACT.Copy).then_inc(
                            sem("ctx_state_ready"), 1)

            for r, stage in enumerate(CTX_STAGES):
                context(r // 4, stage)
                moe(*MOE_RANGES[r + 1])
            flag = act_e.value_load(many[0:1, 0:1], min_val=0, max_val=1)
            with act_e.If(flag < 1):
                act_e.wait_ge(sem("y_written"), EXPERTS)
            with act_e.Else():
                act_e.wait_ge(sem("y_written"), EXPERTS * ROUNDS)
            act_e.nop().then_inc(sem("y_complete"), 1)

            for s in range(SLOTS // P):
                act_e.wait_ge(sem("y_transposed"), s + 1)
                if s == 0:
                    act_e.wait_ge(sem("up_used"), EXPERTS)
                af(y_tok[:, s, :].rearrange("p (a b) -> p a b", b=512), ps[:, 2 * (s % 2):2 * (s % 2) + 2, :],
                   ACT.Copy).then_inc(sem("y_tok_ready"), 1)

            def root(name, bank, n):
                act_e.wait_ge(sem(name + "_mean"), n)
                link(af(o_n[:, :], o_n[:, :], ACT.Ln))
                af(ps[:, bank, 256:512], o_n[:, :], ACT.Exp, scale=-0.5).then_inc(sem(name + "_rstd"), 1)

            for b in range(4):
                act_e.wait_ge(sem("norm_in"), b + 1)
                af(sq[:, 2 * b:2 * b + 2, :], hl[:, 2 * b:2 * b + 2, :], ACT.Square)
                for k in (2 * b, 2 * b + 1):
                    last = af(sq_gained[:, k, :], hl[:, k, :], ACT.Square, scale=vec("final1", k))
                last.then_inc(sem("norm_squared"), 1)
            root("norm", 0, 1)
            root("norm", 1, 2)

            def add_shift(n, chunk):
                for k in range(KD):
                    act_e.wait_ge(sem("hl_scaled"), n * KD + k + 1)
                    af(hl[:, k, :], hl[:, k, :], ACT.Identity, bias=mod[:, chunk + k, 0:1]).then_inc(sem("hl_ready"), 1)

            add_shift(0, 0)

            def evacuate(j):
                g, i, half = j // 10, (j % 10) // 2, j % 2
                act_e.wait_ge(sem("lat_half_done"), j + 1)
                part = PARTS[g][i]
                if g and part not in ("value", "gate"):
                    act_e.wait_ge(sem("prod_ready"), 2 * g)
                cols = slice(half * 512, half * 512 + 512)
                flat = lambda v: v.rearrange("p a b -> p (a b)")[:, cols]
                dst, how = {"forward": (lf[:, cols], ACT.Sigmoid), "backward": (dd[:, cols], ACT.Sigmoid),
                            "query": (flat(q_s), ACT.Silu), "value": (v_s[g][:, half, :], ACT.Copy),
                            "gate": (flat(g_s[g]), ACT.Silu)}[part]
                af(dst, ps[:, j % 3, :], how).then_inc(sem("lat_read"), 1)

            def logarithm(m):
                buf = (lf, dd)[m % 2]
                act_e.wait_ge(sem("f_ready"), m + 1)
                af(buf, buf, ACT.Ln).then_inc(sem("logf_ready"), 1)

            def exponentials(m):
                g, d = m // 2, m % 2
                pr = prod[g]
                act_e.wait_ge(sem("b_ready"), m + 1)
                af(pr[:, d, 2, :], b_s, ACT.Exp).then_inc(sem("eb_ready"), 1)
                act_e.wait_ge(sem("bref_ready"), m + 1)
                af(pr[:, d, 0, :], pr[:, d, 1, :], ACT.Exp).then_inc(sem("eq_ready"), 1)
                act_e.wait_ge(sem("eq_ready"), m + 1)
                af(pr[:, d, 1, :], pr[:, d, 1, :], ACT.Exp, scale=-1.0).then_inc(sem("ek_ready"), 1)
                act_e.wait_ge(sem("blast_ready"), m + 1)
                af(pr[:, d, 3, :], pr[:, d, 3, :], ACT.Exp).then_inc(sem("el_ready"), 1)
                last_of = (CHUNK2 - 1, 0)[d]
                af(dec[:, g, d, :], b_s.rearrange("p (c n) -> p c n", n=CHUNK2)[:, :, last_of], ACT.Exp).then_inc(
                    sem("dec_ready"), 1)

            def copy_kd(n):
                act_e.wait_ge(sem("kd_transposed"), n + 1)
                wait(act_e, "kv_done", n)
                af(kdT[:, :, :, :].rearrange("p a b c -> p (a b c)"), ps[:, 5, :], ACT.Copy).then_inc(
                    sem("kdT_ready"), 1)

            def square(n):
                act_e.wait_ge(sem("o_done"), n + 1)
                wait(act_e, "o_summed", n)
                af(o_sq[:, :], ps[:, 3, 0:256], ACT.Square).then_inc(sem("o_squared"), 1)

            for j in range(10):
                evacuate(j)
            for m in range(2):
                logarithm(m)
                exponentials(m)
                evacuate(10 + 2 * m)
                evacuate(11 + 2 * m)
            copy_kd(0)
            evacuate(14)
            evacuate(15)
            logarithm(2)
            for n in range(GH):
                square(n)
                if n < GH - 1:
                    copy_kd(n + 1)
                if n < 2:
                    evacuate(16 + 2 * n)
                root("o", 3, n + 1)
                if n < 2:
                    evacuate(17 + 2 * n)
                if n == 0:
                    exponentials(2)
                if n == 1:
                    logarithm(3)
                if n == 2:
                    exponentials(3)
            copy_kd(GH)
            for n in range(GH, HEADS2):
                if n < HEADS2 - 1:
                    copy_kd(n + 1)
                square(n)
                root("o", 3, n + 1)

            for b in range(4):
                act_e.wait_ge(sem("norm_in"), 4 + b + 1)
                af(sq_gained[:, 2 * b:2 * b + 2, :], lat[:, 2 * b:2 * b + 2, :], ACT.Square).then_inc(
                    sem("norm_squared"), 1)
            act_e.dma_start(final_gain, a["final_gain"]).then_inc(sem("final_gain_loaded"), 16)
            root("norm", 5, 3)
            add_shift(1, 24)
            for b in range(NB):
                for part in range(2):
                    m = 2 * b + part
                    i = part * NB + b
                    if b % 4 == 3 or b == NB - 1:
                        dense_wait(act_e, "ffn_up", 2 * (b // 4) + part)
                    else:
                        act_e.wait_ge(sem("up_done"), 2 * (3 * (b // 4) + b % 4) + part + 1)
                    if b >= 2:
                        act_e.wait_ge(sem("act_ready"), b - 1)
                    af(up_s[:, b % 2, part, :], ps[:, m % 4, 0:256], ACT.Identity,
                       scale=vec("ffn_w", 2 * NB + i), bias=vec("ffn_b", i)).then_inc(sem("conv_begun"), 1)
                act_e.wait_ge(sem("conv_read"), 2 * b + 2)
                af(sg_s[:, b % 2, :], up_s[:, b % 2, 0, :], ACT.Silu).then_inc(sem("ffn_silu"), 1)
            for half in range(2):
                for t in range(TT):
                    act_e.wait_ge(sem("out_transposed"), 2 * half + t + 1)
                    last = af(sq[:, 2 * t:2 * t + 2, :].rearrange("p a b -> p (a b)"), ps[:, 4 + 2 * t + half, :],
                              ACT.Square, accum_out=col(60 + 2 * half + t))
                if half == 0:
                    link(last)
            last.then_inc(sem("token_sums"), 1)
            act_e.wait_ge(sem("token_mean"), 4)
            rsqrt(col(2, 2), col(2, 2)).then_inc(sem("token_rstd"), 1)

        @block.gpsimd
        def _(pool):
            pool.memset(csil, 0.0).then_inc(sem("csil_zeroed"), 1)
            pool.memset(gcu[:, :, 0:2], 0.0).then_inc(sem("pads_ready"), 1)
            pool.wait_ge(sem("mix_conv_ready"), 4)
            pool.wait_ge(sem("x1_ready"), TT)
            pool.memset(XgT[:, :, SLOTS:COLS], 0.0).then_inc(sem("tail_ready"), 1)
            pool.memset(masked[:, :, :, :], 0.0).then_inc(sem("masked_zeroed"), 1)

            def pool_fast(e0, e1):
                def one(u, it):
                    e = it * 2 + (e0 + u)
                    begin = pool.value_load(starts[0:1, 0, bass.ds(e, 1)], min_val=0, max_val=SLOTS)
                    wait(pool, "up_used", e - 1)
                    pool.tensor_copy(win[:, u], XgT[:, :, bass.ds(begin, WIN)]).then_inc(sem("win_ready"), 1)

                for u in range(2):
                    one(u, 0)
                with pool.Fori(1, (e1 - e0) // 2) as it:
                    for u in range(2):
                        one(u, it)

            def pool_slow(e0, e1):
                def expert(u, it):
                    e = it * 2 + (e0 + u)
                    for r in range(ROUNDS):
                        begin = pool.value_load(starts[0:1, r, bass.ds(e, 1)], min_val=0, max_val=SLOTS)
                        wait(pool, "gu_copied", e * ROUNDS + r)
                        pool.tensor_copy(win[:, u], XgT[:, :, bass.ds(begin, WIN)]).then_inc(sem("win_ready"), 1)

                for u in range(2):
                    expert(u, 0)
                with pool.Fori(1, (e1 - e0) // 2) as it:
                    for u in range(2):
                        expert(u, it)

            def moe(e0, e1):
                flag = pool.value_load(many[0:1, 0:1], min_val=0, max_val=1)
                with pool.If(flag < 1):
                    pool_fast(e0, e1)
                with pool.Else():
                    pool_slow(e0, e1)

            pool.wait_ge(sem("starts_ready"), 1)
            pool.wait_ge(sem("gathered"), KD)
            pool.wait_ge(sem("gated_transposed"), 1)
            pool.dma_start(c_raw, a["ctx"]).then_inc(sem("ctx_loaded"), 16)
            pool.memset(zeros, 0.0).then_inc(sem("zeros_ready"), 1)
            for e0, e1 in MOE_RANGES:
                moe(e0, e1)
            pool.wait_ge(sem("combined"), 4)
            pool.memset(smask, 1.0).then_inc(sem("smask_step"), 1)
            pool.wait_ge(sem("smask_step"), 1)
            pool.memset(smask.rearrange("p (c n) -> p c n", n=CHUNK2)[:, :, 0:1], 0.0).then_inc(sem("smask_ready"), 1)

        @block.vector
        def _(dve):
            tt, ts, stt_ = nc.vector.tensor_tensor, nc.vector.tensor_scalar, nc.vector.scalar_tensor_tensor
            steps = [0]

            def link(ins):
                steps[0] += 1
                ins.then_inc(sem("vector_step"), 1)
                dve.wait_ge(sem("vector_step"), steps[0])

            def token_norm(n, src, dst):
                dve.wait_ge(sem("token_sums"), n)
                ts(col(2, 2), col(0, 2), 1.0 / D, EPS, ALU.mult, ALU.add).then_inc(sem("token_mean"), 1)
                dve.wait_ge(sem("token_rstd"), n)
                for t in range(TT):
                    ts(dst[:, t, :], src[:, t, :], col(2 + t), None, ALU.mult).then_inc(sem("token_scaled"), 1)

            token_norm(1, x1, xn)
            dve.wait_ge(sem("rope_loaded"), 16)
            for j in range(2):
                dense_wait(dve, "w_in", j)
                for t in range(TT):
                    src = ps[:, 4 + 2 * j + t, :].rearrange("p (h s d) -> p h s d", h=HEADS1, s=2)
                    ra = rot_a.rearrange("p (h d) -> p h d", h=HEADS1)
                    rb = rot_b.rearrange("p (h s d) -> p h s d", h=HEADS1, s=2)
                    cos = rope[:, 0, t, :].unsqueeze(1).to_broadcast([P, HEADS1, P])
                    tt(ra, ps[:, 4 + 2 * j + t, :].rearrange("p (h d) -> p h d", h=HEADS1), cos, ALU.mult)
                    for s in range(2):
                        sin = rope[:, 1, t, s * 64:(s + 1) * 64].unsqueeze(1).to_broadcast([P, HEADS1, 64])
                        last = tt(rb[:, :, s, :], src[:, :, 1 - s, :], sin, ALU.mult)
                    link(last)
                    last = tt(qk_rot[:, j, t, :], rot_a, rot_b, ALU.add)
                    if t == 0:
                        link(last)
                last.then_inc(sem("qk_rotated"), 1)
                dve.wait_ge(sem("qk_rotated"), j + 1)
            dve.wait_ge(sem("decay_loaded"), 16)
            for h in range(HEADS1):
                dve.wait_ge(sem("scores_done"), h + 1)
                tt(probs[:, h, 0:256], ps[:, h, 0:256], decay[:, h, :], ALU.mult)
                tt(probs[:, h, 256:384], ps[:, h, 256:384], decay[:, h, 0:P], ALU.mult).then_inc(sem("decayed"), 1)
            dense_wait(dve, "w_in", 5)
            for t in range(TT):
                for h in range(HEADS1):
                    last = nc.vector.bn_stats(stats[:, 4 * t + h, :], ps[:, t, h * P:(h + 1) * P])
            link(last)
            for m in range(8):
                last = nc.vector.bn_aggr(mv[:, m, :], stats[:, m, :])
            link(last)
            ts(col(8, 8), mv[:, :, 1], EPS, None, ALU.add).then_inc(sem("gn_var"), 1)
            dve.wait_ge(sem("gn_rstd"), 1)
            for t in range(TT):
                for h in range(HEADS1):
                    m = 4 * t + h
                    last = ts(ret[:, t, h * P:(h + 1) * P], ps[:, t, h * P:(h + 1) * P], mv[:, m, 0:1], col(8 + m),
                              ALU.subtract, ALU.mult)
            link(last)
            dve.wait_ge(sem("g_ready"), 1)
            for t in range(TT):
                tt(ret[:, t, :], ret[:, t, :], g_tok[:, t, :], ALU.mult).then_inc(sem("ret_ready"), 1)
            dense_wait(dve, "w_in", 6)
            dve.wait_ge(sem("gc_ready"), 1)
            dve.wait_ge(sem("pads_ready"), 1)
            for f in range(4):
                last = tt(gcu[:, f, 2:], gc_s[:, f, :], ps[:, 4 + f // 2, (f % 2) * 256:(f % 2) * 256 + 256], ALU.mult)
            link(last)
            for f in range(4):
                last = ts(conv_a[:, f, :], gcu[:, f, 0:256], vec("conv", f), None, ALU.mult)
            link(last)
            for tap in (1, 2):
                for f in range(4):
                    last = stt_(conv_a[:, f, :], gcu[:, f, tap:tap + 256], vec("conv", 4 * tap + f), conv_a[:, f, :],
                                ALU.mult, ALU.add)
                link(last)
            dve.wait_ge(sem("gb_ready"), 1)
            dve.wait_ge(sem("qkT_ready"), 2)
            for f in range(4):
                tt(mixT[:, 4 + f, :], conv_a[:, f, :], gb_s[:, f, :], ALU.mult).then_inc(sem("mix_conv_ready"), 1)
            dense_wait(dve, "w_o", 1)
            for t in range(TT):
                xv = x1[:, t, :].rearrange("p (a b) -> p a b", b=512)
                tt(xv, xv, ps[:, 4 + 2 * t:6 + 2 * t, :], ALU.add).then_inc(sem("x1_ready"), 1)

            token_norm(2, x1, xn)
            dve.wait_ge(sem("router_done"), 1)
            dve.wait_ge(sem("router_loaded"), 48)
            L = logits
            for t in range(TT):
                last = tt(L[:, t, :], ps[:, 4, t * 72:t * 72 + 72], router_b, ALU.add)
            link(last)

            def softmax_in(j, src, both):
                o = 40 * j
                for t in range(TT):
                    last = nc.vector.max(rt[:, t, o:o + 8], src(t))
                link(last)
                tt(rt[:, :, o + 8:o + 16], both, rt[:, :, o:o + 1].to_broadcast([P, TT, 8]), ALU.subtract).then_inc(
                    sem("softmax_in"), 1)

            def softmax_top(j):
                o = 40 * j
                dve.wait_ge(sem("softmax_exp"), j + 1)
                link(nc.vector.reciprocal(rt[:, :, o + 37:o + 38], rt[:, :, o + 36:o + 37]))
                link(tt(rt[:, :, o + 8:o + 16], rt[:, :, o + 8:o + 16], rt[:, :, o + 37:o + 38].to_broadcast([P, TT, 8]),
                        ALU.mult))
                for t in range(TT):
                    last = nc.vector.max(rt[:, t, o + 16:o + 24], rt[:, t, o + 8:o + 16])
                link(last)
                for t in range(TT):
                    last = nc.vector.max_index(rt[:, t, o + 24:o + 32].bitcast(u32), rt[:, t, o + 16:o + 24],
                                               rt[:, t, o + 8:o + 16])
                link(last)
                link(nc.vector.tensor_copy(rt[:, :, o + 32:o + 34], rt[:, :, o + 24:o + 26].bitcast(u32)))

            softmax_in(0, lambda t: L[:, t, 0:8], L[:, :, 0:8])
            softmax_top(0)
            for t in range(TT):
                last = ts(rt[:, t, 80:88], iota[:, 0:8], rt[:, t, 32:33], None, ALU.is_equal)
            link(last)
            for t in range(TT):
                last = tt(rt[:, t, 96:160].rearrange("p (e g) -> p e g", g=8),
                          L[:, t, 8:72].rearrange("p (g e) -> p e g", g=8),
                          rt[:, t, 80:88].unsqueeze(1).to_broadcast([P, 8, 8]), ALU.mult)
            link(last)
            for t in range(TT):
                last = nc.vector.reduce_sum(rt[:, t, 88:96], rt[:, t, 96:160].rearrange("p (e g) -> p e g", g=8), axis=X)
            link(last)
            softmax_in(1, lambda t: rt[:, t, 88:96], rt[:, :, 88:96])
            softmax_top(1)
            for t in range(TT):
                last = stt_(rt[:, t, 80:82], rt[:, t, 32:33].to_broadcast([P, 2]), 8.0, rt[:, t, 72:74], ALU.mult, ALU.add)
            link(last)
            for t in range(TT):
                last = tt(rt[:, t, 84:85], rt[:, t, 56:57], rt[:, t, 57:58], ALU.add)
            link(last)
            for t in range(TT):
                last = nc.vector.reciprocal(rt[:, t, 84:85], rt[:, t, 84:85])
            link(last)
            for t in range(TT):
                last = ts(rt[:, t, 82:84], rt[:, t, 56:58], rt[:, t, 84:85], rt[:, t, 16:17], ALU.mult, ALU.mult)
            link(last)
            for j in range(2):
                for t in range(TT):
                    last = ts(onehot[:, j, t, :], iota[:, 0:EXPERTS], rt[:, t, 80 + j:81 + j], None, ALU.is_equal)
            link(last)
            tt(assigned, onehot[:, 0], onehot[:, 1], ALU.add).then_inc(sem("assigned_ready"), 1)
            dve.wait_ge(sem("counted"), 1)
            link(nc.vector.tensor_copy(count, ps[:, 5, 0:192].rearrange("p (a b) -> p a b", b=EXPERTS)))
            link(ts(place[:, 0, :], count[:, 2, :], 0.0, 1.0, ALU.mult, ALU.add))
            link(nc.vector.tensor_tensor_scan(place[:, 1, :], place[:, 0, :], count[:, 2, :], 0.0, ALU.mult, ALU.add))
            link(tt(place[:, 1, :], place[:, 1, :], count[:, 2, :], ALU.subtract))
            for r in range(ROUNDS):
                ts(starts[0:1, r, :], place[0:1, 1, :], float(WIN * r), float(SLOTS), ALU.add, ALU.min)
            link(nc.vector.reduce_max(col(20), count[:, 2, :], axis=X))
            ts(many[0:1, 0:1], col(20)[0:1, :], float(WIN), None, ALU.is_gt).then_inc(sem("starts_ready"), 1)
            for t in range(TT):
                last = tt(count[:, t, :], count[:, t, :], place[:, 1, :], ALU.add)
            link(last)
            for j in range(2):
                for t in range(TT):
                    last = tt(onehot[:, j, t, :], onehot[:, j, t, :], count[:, t, :], ALU.mult)
            link(last)
            link(nc.vector.reduce_sum(col(24, 4), onehot.rearrange("p j t e -> p (j t) e"), axis=X))
            for t in range(TT):
                last = ts(sel[:, t, :], iota, col(24 + t), None, ALU.is_equal)
            link(last)
            for t in range(TT):
                last = stt_(sel[:, t, :], iota, col(26 + t), sel[:, t, :], ALU.is_equal, ALU.add)
            last.then_inc(sem("sel_ready"), 1)
            for t in range(TT):
                last = ts(gated[:, t, :], iota, col(24 + t), rt[:, t, 82:83], ALU.is_equal, ALU.mult)
            link(last)
            for t in range(TT):
                last = ts(h2T.rearrange("p a b -> p (a b)")[:, t * 512:(t + 1) * 512], iota, col(26 + t),
                          rt[:, t, 83:84], ALU.is_equal, ALU.mult)
            link(last)
            for t in range(TT):
                last = tt(gated[:, t, :], gated[:, t, :], h2T.rearrange("p a b -> p (a b)")[:, t * 512:(t + 1) * 512],
                          ALU.add)
            last.then_inc(sem("gated_ready"), 1)

            def copy_y(q):
                wait(dve, "y_folded", q)
                nc.vector.tensor_copy(y_s, ps[:, 2, :]).then_inc(sem("y_copied"), 1)

            def multiply(u, q):
                wait(dve, "silu_ready", q + 1)
                tt(hidden[:, u], silu_g, ps[:, 1, :].rearrange("p (f n) -> p f n", f=KF)[:, :, WIN:2 * WIN],
                   ALU.mult).then_inc(sem("hidden_ready"), 1)

            def dve_fast(e0, e1):
                def step(u, it, more=True):
                    e = it * 2 + (e0 + u)
                    wait(dve, "down_used", e + 1)
                    copy_y(e)
                    if more:
                        multiply(1 - u, e + 1)

                multiply(0, e0)
                step(0, 0)
                step(1, 0)
                if e1 - e0 > 4:
                    with dve.Fori(1, (e1 - e0) // 2 - 1) as it:
                        step(0, it)
                        step(1, it)
                step(0, (e1 - e0) // 2 - 1)
                step(1, (e1 - e0) // 2 - 1, more=False)

            def dve_slow(e0, e1):
                def expert(u, it):
                    e = it * 2 + (e0 + u)
                    for r in range(ROUNDS):
                        q = e * ROUNDS + r
                        multiply(u, q)
                        if r == ROUNDS - 1:
                            wait(dve, "down_used", e + 1)
                        else:
                            wait(dve, "round_down", e * (ROUNDS - 1) + (r + 1))
                        copy_y(q)

                for u in range(2):
                    expert(u, 0)
                with dve.Fori(1, (e1 - e0) // 2) as it:
                    for u in range(2):
                        expert(u, it)

            def moe(e0, e1):
                flag = dve.value_load(many[0:1, 0:1], min_val=0, max_val=1)
                with dve.If(flag < 1):
                    dve_fast(e0, e1)
                with dve.Else():
                    dve_slow(e0, e1)

            lbv = vecs[:, VEC["lb"]:VEC["lb"] + 32].rearrange("p (l n) -> p l n", l=2)
            link(tt(small[:, 32:48], lbv[:, 0, :], lbv[:, 1, :], ALU.max))
            for l in range(2):
                last = tt(lbv[:, l, :], lbv[:, l, :], small[:, 32:48], ALU.subtract)
            last.then_inc(sem("lb_in"), 1)
            dve.wait_ge(sem("starts_ready"), 1)
            moe(*MOE_RANGES[0])

            dve.wait_ge(sem("mod_copied"), 12)
            link(tt(mod[:, :, :], mod[:, :, :], vec("b_ada", 0, 48).unsqueeze(2).to_broadcast([P, 48, 2]), ALU.add))
            for row, (chunk, who, gain) in enumerate(((8, 1, 0), (8, 0, 0), (32, 0, 8))):
                last = stt_(scales[:, row, :], mod[:, chunk:chunk + 8, who], 1.0, vec("norm_g", gain, 8), ALU.add,
                            ALU.mult)
            last.then_inc(sem("mod_ready"), 1)
            dve.wait_ge(sem("lb_exp"), 1)
            link(tt(small[:, 32:48], lbv[:, 0, :], lbv[:, 1, :], ALU.add))
            link(nc.vector.reciprocal(small[:, 32:48], small[:, 32:48]))
            lbf = lbs[:, 0].rearrange("p a b -> p (a b)")
            link(tt(lbf, lbv[:, 0, :], small[:, 32:48], ALU.mult))
            link(ts(lbs[:, 1].rearrange("p a b -> p (a b)"), lbf, -1.0, 1.0, ALU.mult, ALU.add))
            token_norm(3, c_raw, c_raw)
            dve.wait_ge(sem("zeros_ready"), 1)

            def context(g, d):
                m = 2 * g + d
                dve.wait_ge(sem("ctx_f_read"), m + 1)
                for h in range(GH):
                    last = ts(c_f[:, h, :], c_f[:, h, :], lbs[:, 1, d, GH * g + h:GH * g + h + 1],
                              lbs[:, 0, d, GH * g + h:GH * g + h + 1], ALU.mult, ALU.add)
                link(last)
                wait(dve, "ctx_kd_transposed", GH * g)
                for h in range(GH):
                    if d == 0:
                        nc.vector.memset(c_p[:, d, h, TOKENS - 1:TOKENS], 1.0)
                        last = nc.vector.tensor_tensor_scan(c_p[:, d, h, TOKENS - 2::-1], c_f[:, h, TOKENS - 1:0:-1],
                                                            zeros[:, 0:TOKENS - 1], 1.0, ALU.mult, ALU.add)
                    else:
                        nc.vector.memset(c_p[:, d, h, 0:1], 1.0)
                        last = nc.vector.tensor_tensor_scan(c_p[:, d, h, 1:TOKENS], c_f[:, h, 0:TOKENS - 1],
                                                            zeros[:, 0:TOKENS - 1], 1.0, ALU.mult, ALU.add)
                link(last)
                cf = c_f.rearrange("p a b -> p (a b)")
                cp = c_p[:, d].rearrange("p a b -> p (a b)")
                link(ts(cf, cf, -1.0, 1.0, ALU.mult, ALU.add))
                tt(cp, cp, cf, ALU.mult).then_inc(sem("ctx_kd_ready"), 1)

            for r, stage in enumerate(CTX_STAGES):
                if stage in ("f0", "f1"):
                    context(r // 4, int(stage[1]))
                moe(*MOE_RANGES[r + 1])

            def mean(name, where, width, n):
                dve.wait_ge(sem(name + "_summed"), n)
                ts(o_n[:, :], where, 1.0 / width, EPS, ALU.mult, ALU.add).then_inc(sem(name + "_mean"), 1)

            for b in range(4):
                dve.wait_ge(sem("combined"), b + 1)
                nc.vector.tensor_copy(hl[:, 2 * b:2 * b + 2, :].rearrange("p a b -> p (a b)"), ps[:, 4 + b, :]).then_inc(
                    sem("norm_in"), 1)
            mean("norm", ps[:, 0, 0:256], D, 1)
            link(ts(o_sq[:, :], ps[:, 1, 0:256], 1.0 / D, None, ALU.mult))
            dve.wait_ge(sem("norm_rstd"), 1)
            link(tt(o_sq[:, :], o_sq[:, :], ps[:, 0, 256:512], ALU.mult))
            link(tt(o_sq[:, :], o_sq[:, :], ps[:, 0, 256:512], ALU.mult))
            ts(o_n[:, :], o_sq[:, :], EPS, None, ALU.add).then_inc(sem("norm_mean"), 1)
            for k in range(KD):
                last = stt_(lat[:, k, :], hl[:, k, :], vec("final1", k), ps[:, 0, 256:512], ALU.mult, ALU.mult)
            link(last)
            dve.wait_ge(sem("norm_rstd"), 2)
            for k in range(KD):
                stt_(hl[:, k, :], lat[:, k, :], scales[:, 1, k:k + 1], ps[:, 1, 256:512], ALU.mult, ALU.mult).then_inc(
                    sem("hl_scaled"), 1)

            dve.wait_ge(sem("smask_ready"), 1)
            dve.wait_ge(sem("hmask_loaded"), 16)
            dve.wait_ge(sem("masked_zeroed"), 1)
            chunks = lambda v: v.rearrange("p (c n) -> p c n", n=CHUNK2)
            wide = lambda v: v.unsqueeze(2).to_broadcast([P, GH * NCH, CHUNK2])
            qf = q_s.rearrange("p a b -> p (a b)")

            def forget(m):
                g, d = m // 2, m % 2
                buf = (lf, dd)[d]
                dve.wait_ge(sem("lat_read"), halves_to(g, ("forward", "backward")[d]))
                for h in range(GH):
                    last = ts(buf[:, h * TOKENS:(h + 1) * TOKENS], buf[:, h * TOKENS:(h + 1) * TOKENS],
                              lbs[:, 1, d, GH * g + h:GH * g + h + 1], lbs[:, 0, d, GH * g + h:GH * g + h + 1],
                              ALU.mult, ALU.add)
                link(last)
                ts(kk, buf, -1.0, 1.0, ALU.mult, ALU.add).then_inc(sem("f_ready"), 1)

            def cumulate(m):
                g, d = m // 2, m % 2
                buf, pr = (lf, dd)[d], prod[g]
                dve.wait_ge(sem("logf_ready"), m + 1)
                wait(dve, "dec_ready", m)
                if d == 0:
                    nc.vector.tensor_tensor_scan(b_s, smask, buf, 0.0, ALU.mult, ALU.add).then_inc(sem("b_ready"), 1)
                else:
                    link(nc.vector.tensor_tensor_scan(lf, smask, buf, 0.0, ALU.mult, ALU.add))
                    link(tt(buf, buf, lf, ALU.subtract))
                    tt(chunks(b_s), chunks(buf), wide(chunks(lf)[:, :, CHUNK2 - 1]), ALU.add).then_inc(
                        sem("b_ready"), 1)
                dve.wait_ge(sem("b_ready"), m + 1)
                ref, end = (CHUNK2 // 2, CHUNK2 - 1) if d == 0 else (CHUNK2 - 1 - CHUNK2 // 2, 0)
                tt(chunks(pr[:, d, 1, :]), chunks(b_s), wide(chunks(b_s)[:, :, ref]), ALU.subtract).then_inc(
                    sem("bref_ready"), 1)
                tt(chunks(pr[:, d, 3, :]), wide(chunks(b_s)[:, :, end]), chunks(b_s), ALU.subtract).then_inc(
                    sem("blast_ready"), 1)

            def products(m):
                g, d = m // 2, m % 2
                pr = prod[g]
                dve.wait_ge(sem("lat_read"), halves_to(g, "query"))
                dve.wait_ge(sem("eb_ready"), m + 1)
                tt(pr[:, d, 2, :], pr[:, d, 2, :], qf, ALU.mult)
                dve.wait_ge(sem("eq_ready"), m + 1)
                dve.wait_ge(sem("ek_ready"), m + 1)
                tt(pr[:, d, 0, :], pr[:, d, 0, :], qf, ALU.mult)
                tt(pr[:, d, 1, :], pr[:, d, 1, :], kk, ALU.mult)
                dve.wait_ge(sem("el_ready"), m + 1)
                tt(pr[:, d, 3, :], pr[:, d, 3, :], kk, ALU.mult).then_inc(sem("prod_ready"), 1)
                dve.wait_ge(sem("prod_ready"), m + 1)

            def mask(n):
                dve.wait_ge(sem("s_done"), n + 1)
                wait(dve, "o_done", n)
                HC = CHUNK2 // 2
                for d in range(2):
                    for quarter in range(4):
                        lo, late_keys = quarter * HC, quarter % 2 != d
                        q0, qn = ((quarter % 2) * HC, HC) if late_keys else (0, CHUNK2)
                        to = (quarter // 2) * CHUNK2 + q0
                        last = nc.vector.copy_predicated(
                            masked[lo:lo + HC, d, :, to:to + qn],
                            hmask[lo:lo + HC, d, q0:q0 + qn].unsqueeze(1).to_broadcast([HC, TT, qn]),
                            ps[lo:lo + HC, 4, 0:256].rearrange("p (t d n) -> p t d n", t=TT, d=2)[:, :, d, q0:q0 + qn])
                last.then_inc(sem("masked_ready"), 1)

            def states(n):
                g, h = n // GH, n % GH
                dve.wait_ge(sem("kv_done"), n + 1)
                dve.wait_ge(sem("dec_ready"), 2 * (g + 1))
                for j in range(1, NCH):
                    for d in range(2):
                        c = j - 1 if d == 0 else NCH - j
                        prev = state[:, n, d, :] if j == 1 else chunk_state[:, d, j - 1, :]
                        last = stt_(chunk_state[:, d, j, :], prev, dec[:, g, d, h * NCH + c:h * NCH + c + 1],
                                    kv_bank(d, c), ALU.mult, ALU.add)
                        if j == NCH - 1:
                            last.then_inc(sem("states_ready"), 1)
                    if j < NCH - 1:
                        link(last)

            def readout(n):
                g, h = n // GH, n % GH
                mean("o", ps[:, 3, 256:512], P, n + 1)
                dve.wait_ge(sem("o_rstd"), n + 1)
                link(tt(gated_rstd, g_s[g][:, h, :], ps[:, 3, 256:512], ALU.mult))
                stt_(attn[:, n, :], ps[:, 3, 0:256], vec("gnorm"), gated_rstd, ALU.mult, ALU.mult).then_inc(
                    sem("readout_done"), 1)

            for m in range(2):
                forget(m)
                cumulate(m)
                products(m)
            mask(0)
            states(0)
            forget(2)
            for n in range(GH - 1):
                readout(n)
                mask(n + 1)
                states(n + 1)
                if n == 0:
                    cumulate(2)
                if n == 1:
                    products(2)
                    forget(3)
                    cumulate(3)
                if n == 2:
                    products(3)
            readout(GH - 1)
            mask(GH)
            states(GH)

            def add_mixed(b, group):
                for k in (2 * b, 2 * b + 1):
                    last = stt_(lat[:, k, :], ps[:, b if group else b % 3, (k % 2) * 256:(k % 2) * 256 + 256],
                                mod[:, 16 + k, 0:1], lat[:, k, :], ALU.mult, ALU.add)
                return last

            for n in range(GH, HEADS2):
                if n < HEADS2 - 1:
                    mask(n + 1)
                    states(n + 1)
                readout(n)
                dve.wait_ge(sem("hg_done"), n - GH + 1)
                add_mixed(n - GH, 0).then_inc(sem("hg_added"), 1)
            dve.wait_ge(sem("hg_added"), 4)
            for b in range(4):
                dve.wait_ge(sem("hg_done"), 4 + b + 1)
                add_mixed(b, 1).then_inc(sem("norm_in"), 1)
            dve.wait_ge(sem("norm_in"), 8)
            mean("norm", ps[:, 4, 0:256], D, 2)
            dve.wait_ge(sem("norm_rstd"), 3)
            for k in range(KD):
                stt_(hl[:, k, :], lat[:, k, :], scales[:, 2, k:k + 1], ps[:, 5, 256:512], ALU.mult, ALU.mult).then_inc(
                    sem("hl_scaled"), 1)

            for b in range(NB):
                for part in range(2):
                    i = part * NB + b
                    dve.wait_ge(sem("conv_begun"), 2 * b + part + 1)
                    p_in, acc = ps[:, (2 * b + part) % 4, 0:256], up_s[:, b % 2, part, :]
                    link(stt_(acc[:, 1:], p_in[:, 0:255], vec("ffn_w", i), acc[:, 1:], ALU.mult, ALU.add))
                    stt_(acc[:, 0:255], p_in[:, 1:], vec("ffn_w", 4 * NB + i), acc[:, 0:255], ALU.mult,
                         ALU.add).then_inc(sem("conv_read"), 1)
                dve.wait_ge(sem("conv_read"), 2 * b + 2)
                dve.wait_ge(sem("ffn_silu"), b + 1)
                tt(act[:, b, :], sg_s[:, b % 2, :], up_s[:, b % 2, 1, :], ALU.mult).then_inc(sem("act_ready"), 1)
            for half in range(2):
                dense_wait(dve, "ffn_down", 3 * half + 2)
                for f in range(4):
                    k = 4 * half + f
                    last = stt_(lat[:, k, :], ps[:, 4 - 4 * half + f, 0:256], mod[:, 40 + k, 0:1], lat[:, k, :], ALU.mult,
                                ALU.add)
                last.then_inc(sem("last_residual"), 1)
            dve.wait_ge(sem("token_sums"), 4)
            link(tt(col(2, 2), col(60, 2), col(62, 2), ALU.add))
            ts(col(2, 2), col(2, 2), 1.0 / D, EPS, ALU.mult, ALU.add).then_inc(sem("token_mean"), 1)
            dve.wait_ge(sem("token_rstd"), 4)
            dve.wait_ge(sem("final_gain_loaded"), 16)
            for t in range(TT):
                stt_(o_tok[:, t, :].rearrange("p (a b) -> p a b", b=512), ps[:, 4 + 2 * t:6 + 2 * t, :], col(2 + t),
                     final_gain.rearrange("p (a b) -> p a b", b=512), ALU.mult, ALU.mult).then_inc(
                    sem("out_ready"), 1)


def constants():
    t = np.arange(TOKENS, dtype=np.float32)
    half = 64
    inv = (10000.0 ** (-np.arange(half, dtype=np.float32) / half)).astype(np.float32)
    ang = t[:, None] * inv[None, :]
    cos, sin = np.cos(ang).astype(np.float32), np.sin(ang).astype(np.float32)
    rope = np.stack([np.concatenate([cos, cos], 1), np.concatenate([-sin, sin], 1)])
    rope = rope.reshape(2, TT, P, P).transpose(2, 0, 1, 3)
    log_g = np.log1p(-(2.0 ** (-5.0 - np.arange(HEADS1))))
    rel = np.arange(TOKENS)[None, :] - np.arange(P)[:, None]
    decay = np.where(rel[:, None] >= 0, np.exp(log_g[None, :, None] * np.maximum(rel, 0)[:, None]), 0.0) * 128 ** -0.5
    p = np.arange(P)
    quarter, row, n = p[:, None] // 32, p[:, None] % 32, p[None, :]
    pairs, every = (quarter // 2 == n // 32) & (row == n % 32), (row == n)
    consts = np.stack([np.eye(P), np.ones((P, P)), p[:, None] < p[None, :], pairs, every], 1)
    j, i = p[:, None] % CHUNK2, np.arange(CHUNK2)[None, :]
    hmask = np.stack([j <= i, j >= i], 1)
    iota = np.broadcast_to(np.arange(SLOTS), (P, SLOTS))
    f = lambda v, dt=np.float32: np.ascontiguousarray(v).astype(dt)
    return {"rope": f(rope), "decay": f(decay), "consts": f(consts), "hmask": f(hmask, np.int32), "iota": f(iota)}


def kernel(**inputs):
    import concourse.bacc as bacc
    from concourse.bass_utils import run_bass_kernel_spmd as run

    g = {k: np.asarray(v) for k, v in inputs.items()}
    tok = lambda v: np.ascontiguousarray(v.reshape(TT, P, D).transpose(1, 0, 2))
    blk = lambda v: v.reshape(-1, P).T
    packed = {"norm1": blk(g["norm1_w"]), "ret_gn": blk(g["ret_gn_w"]), "conv": blk(g["conv_w"]),
              "norm2": g["norm2_w"].reshape(P, KD), "final1": blk(g["final_norm_w"]), "norm_g": blk(g["norm_g_2"]),
              "lb": blk(g["hg_lb_logits_2"]), "gnorm": blk(g["hg_gnorm_2"]),
              "b_ada": blk(g["b_ada_2"]), "ffn_w": blk(g["ffn_conv_w_2"]), "ffn_b": blk(g["ffn_conv_b_2"]),
              "c": blk(g["c_2"]), "c_ctx": blk(g["c_ctx_2"])}
    router = np.concatenate([g["router_g_w"][0], g["router_e_w"][0].transpose(1, 0, 2).reshape(D, 64)], 1)
    bias = np.concatenate([g["router_g_b"].reshape(1, 8), g["router_e_b"].reshape(1, 64)], 1)
    arrays = {
        "x": tok(g["x"]), "ctx": tok(g["ctx_2"]),
        "vecs": np.ascontiguousarray(np.concatenate([packed[n] for n in VEC], 1)),
        "router_w": np.ascontiguousarray(router.reshape(P, KD, 72)),
        "router_b": np.ascontiguousarray(np.repeat(bias, P, 0)),
        "w_in": g["w_in"][0], "w_o": g["w_o"][0], "w_gate": g["w_gate"][0], "w_up": g["w_up"][0],
        "w_down": g["w_down"][0], "w_ada": g["w_ada_2"][0], "hg_in": g["hg_w_in_2"][0], "hg_out": g["hg_w_out_2"][0],
        "final_gain": np.ascontiguousarray(np.repeat(g["final_g_2"].reshape(1, D), P, 0)),
        "ffn_up": g["ffn_w_up_2"][0], "ffn_down": g["ffn_w_down_2"][0],
        **constants(),
    }
    nc = bacc.Bacc("TRN2", target_bir_lowering=False, num_devices=1)
    sent, a = {}, {}
    for name, v in arrays.items():
        v = np.ascontiguousarray(v)
        sent["in_" + name] = v
        a[name] = nc.dram_tensor("in_" + name, v.shape, mybir.dt.from_np(v.dtype), kind="ExternalInput").ap()
    out = nc.dram_tensor("out_0", (1, TOKENS, D), mybir.dt.float32, kind="ExternalOutput").ap()
    program(nc, a, out)
    return run(nc, [sent], core_ids=[0]).results[0]["out_0"]
```
